# Optimizing a Trainium2 kernel written in Bass

```python
import jax, jax.numpy as jnp
from jax import lax
import numpy as np
import math

D_MODEL = 1024
BATCH = 1
SEQ = 512
DEPTH = 2

N_META = 16
BLK = 128
PAD = BLK - N_META
ROPE_THETA = 10000.0
EPS = 1e-6
NEG = -1e30

FOX_HEADS = 8
FOX_DH = 64

MLA_HEADS = 8
MLA_NOPE = 64
MLA_ROPE = 32
MLA_V = 64
MLA_QLORA = 384
MLA_KVLORA = 256

SWA_HEADS = 8
SWA_KV_HEADS = 2
SWA_DH = 64
WINDOW = 128

BRANCH_W = 512
N_BRANCH = 3

SPLIT_SIZES = (
    FOX_HEADS * FOX_DH, FOX_HEADS * FOX_DH, FOX_HEADS * FOX_DH, FOX_HEADS, BRANCH_W,
    MLA_QLORA, MLA_KVLORA, MLA_ROPE, BRANCH_W,
    SWA_HEADS * SWA_DH, SWA_KV_HEADS * SWA_DH, SWA_KV_HEADS * SWA_DH, BRANCH_W,
    N_BRANCH * D_MODEL,
)
N_IN = sum(SPLIT_SIZES)


def rmsnorm(x, g):
    xf = x.astype(jnp.float32)
    y = xf * lax.rsqrt(jnp.mean(xf * xf, axis=-1, keepdims=True) + EPS)
    return (y * g.astype(jnp.float32)).astype(x.dtype)

def rope(x, pos):
    half = x.shape[-1] // 2
    inv = ROPE_THETA ** (-jnp.arange(half, dtype=jnp.float32) / half)
    ang = pos.astype(jnp.float32)[:, None] * inv[None, :]
    cos = jnp.cos(ang)[None, :, None, :]
    sin = jnp.sin(ang)[None, :, None, :]
    xf = x.astype(jnp.float32)
    x1, x2 = xf[..., :half], xf[..., half:]
    return jnp.concatenate([x1 * cos - x2 * sin, x2 * cos + x1 * sin], axis=-1).astype(x.dtype)

def causal_block_attention(q, k, v, scale, log_cum=None):
    B, L, H, _ = q.shape
    nb = L // BLK
    kpos = jnp.arange(L)
    key_ok = kpos >= PAD
    qb = jnp.moveaxis(q.reshape(B, nb, BLK, H, q.shape[-1]), 1, 0)
    if log_cum is None:
        xs = (jnp.arange(nb), qb)
        ck = None
    else:
        cb = jnp.moveaxis(log_cum.reshape(B, nb, BLK, H), 1, 0)
        xs = (jnp.arange(nb), qb, cb)
        ck = jnp.swapaxes(log_cum, 1, 2)

    def block(args):
        i, qi = args[0], args[1]
        s = jnp.einsum('bqhd,bkhd->bhqk', qi, k).astype(jnp.float32) * scale
        if log_cum is not None:
            ci = jnp.swapaxes(args[2], 1, 2)
            s = s + (ci[..., :, None] - ck[..., None, :])
        qpos = i * BLK + jnp.arange(BLK)
        mask = (kpos[None, :] <= qpos[:, None]) & key_ok[None, :]
        s = jnp.where(mask, s, NEG)
        p = jax.nn.softmax(s, axis=-1)
        return jnp.einsum('bhqk,bkhd->bqhd', p.astype(v.dtype), v)

    o = lax.map(block, xs)
    return jnp.moveaxis(o, 0, 1).reshape(B, L, H, v.shape[-1])

def sliding_window_sink_attention(q, k, v, sinks):
    B, L, H, D = q.shape
    Hkv = k.shape[2]
    G = H // Hkv
    nb = L // BLK
    qb = q.reshape(B, nb, BLK, Hkv, G, D)

    def with_prev(t):
        prev = jnp.concatenate([jnp.zeros_like(t[:, :1]), t[:, :-1]], axis=1)
        return jnp.concatenate([prev, t], axis=2)

    kx = with_prev(k.reshape(B, nb, BLK, Hkv, D))
    vx = with_prev(v.reshape(B, nb, BLK, Hkv, D))
    s = jnp.einsum('bnqhgd,bnkhd->bnhgqk', qb, kx).astype(jnp.float32) * (D ** -0.5)
    blocks = jnp.arange(nb)[:, None]
    qpos = blocks * BLK + jnp.arange(BLK)[None, :]
    kpos = (blocks - 1) * BLK + jnp.arange(2 * BLK)[None, :]
    rel = qpos[:, :, None] - kpos[:, None, :]
    mask = (rel >= 0) & (rel < WINDOW) & (kpos >= PAD)[:, None, :]
    s = jnp.where(mask[None, :, None, None], s, NEG)
    sink = jnp.broadcast_to(sinks.astype(jnp.float32).reshape(1, 1, Hkv, G, 1, 1), s.shape[:-1] + (1,))
    p = jax.nn.softmax(jnp.concatenate([s, sink], axis=-1), axis=-1)[..., :-1]
    o = jnp.einsum('bnhgqk,bnkhd->bnqhgd', p.astype(v.dtype), vx)
    return o.reshape(B, L, H, D)

def hybrid_layer(x, pos, norm_g, w_in, b_f, g_cq, g_ckv, w_uq, w_ukv, sinks, w_branch, w_out):
    B, L, _ = x.shape
    h = rmsnorm(x, norm_g)
    proj = h @ w_in
    (a_q, a_k, a_v, a_f, a_z,
     b_cq, b_ckv, b_kr, b_z,
     c_q, c_k, c_v, c_z, gates) = jnp.split(proj, np.cumsum(SPLIT_SIZES)[:-1], axis=-1)

    log_f = jax.nn.log_sigmoid((a_f + b_f).astype(jnp.float32))
    log_cum = jnp.cumsum(log_f, axis=1)
    y_a = causal_block_attention(a_q.reshape(B, L, FOX_HEADS, FOX_DH),
                                 a_k.reshape(B, L, FOX_HEADS, FOX_DH),
                                 a_v.reshape(B, L, FOX_HEADS, FOX_DH),
                                 FOX_DH ** -0.5, log_cum)

    cq = rmsnorm(b_cq, g_cq)
    ckv = rmsnorm(b_ckv, g_ckv)
    qB = (cq @ w_uq).reshape(B, L, MLA_HEADS, MLA_NOPE + MLA_ROPE)
    q_b = jnp.concatenate([qB[..., :MLA_NOPE], rope(qB[..., MLA_NOPE:], pos)], axis=-1)
    kvB = (ckv @ w_ukv).reshape(B, L, MLA_HEADS, MLA_NOPE + MLA_V)
    k_rope = rope(b_kr.reshape(B, L, 1, MLA_ROPE), pos)
    k_b = jnp.concatenate([kvB[..., :MLA_NOPE],
                           jnp.broadcast_to(k_rope, (B, L, MLA_HEADS, MLA_ROPE))], axis=-1)
    v_b = kvB[..., MLA_NOPE:]
    y_b = causal_block_attention(q_b, k_b, v_b, (MLA_NOPE + MLA_ROPE) ** -0.5)

    qc = rope(c_q.reshape(B, L, SWA_HEADS, SWA_DH), pos)
    kc = rope(c_k.reshape(B, L, SWA_KV_HEADS, SWA_DH), pos)
    vc = c_v.reshape(B, L, SWA_KV_HEADS, SWA_DH)
    y_c = sliding_window_sink_attention(qc, kc, vc, sinks)

    branches = jnp.stack([y_a.reshape(B, L, BRANCH_W) * jax.nn.silu(a_z),
                          y_b.reshape(B, L, BRANCH_W) * jax.nn.silu(b_z),
                          y_c.reshape(B, L, BRANCH_W) * jax.nn.silu(c_z)], axis=2)
    proj_br = jnp.einsum('blnw,nwd->blnd', branches, w_branch)
    g = jax.nn.sigmoid(gates.reshape(B, L, N_BRANCH, D_MODEL))
    merged = jnp.sum(g * proj_br, axis=2)
    return x + merged @ w_out

def first_inputs(seed: int = 0) -> dict:
    key = jax.random.key(seed)
    ks = jax.random.split(key, 14)
    f32 = jnp.float32
    nrm = lambda k, shape, scale: jax.random.normal(k, shape, f32) * scale
    return {
        "x": nrm(ks[0], (BATCH, SEQ, D_MODEL), 1.0),
        "meta_tokens": nrm(ks[1], (N_META, D_MODEL), 1.0),
        "norm_g": 1.0 + nrm(ks[2], (DEPTH, D_MODEL), 0.02),
        "w_in": nrm(ks[3], (DEPTH, D_MODEL, N_IN), D_MODEL ** -0.5),
        "b_f": jax.random.uniform(ks[4], (DEPTH, FOX_HEADS), f32, 1.0, 4.0),
        "g_cq": 1.0 + nrm(ks[5], (DEPTH, MLA_QLORA), 0.02),
        "g_ckv": 1.0 + nrm(ks[6], (DEPTH, MLA_KVLORA), 0.02),
        "w_uq": nrm(ks[7], (DEPTH, MLA_QLORA, MLA_HEADS * (MLA_NOPE + MLA_ROPE)), MLA_QLORA ** -0.5),
        "w_ukv": nrm(ks[8], (DEPTH, MLA_KVLORA, MLA_HEADS * (MLA_NOPE + MLA_V)), MLA_KVLORA ** -0.5),
        "sinks": nrm(ks[9], (DEPTH, SWA_HEADS), 0.5),
        "w_branch": nrm(ks[10], (DEPTH, N_BRANCH, BRANCH_W, D_MODEL), BRANCH_W ** -0.5),
        "w_out": nrm(ks[11], (DEPTH, D_MODEL, D_MODEL), D_MODEL ** -0.5),
        "final_g": 1.0 + nrm(ks[12], (D_MODEL,), 0.02),
    }

def first_block(x, meta_tokens, norm_g, w_in, b_f, g_cq, g_ckv, w_uq, w_ukv, sinks, w_branch, w_out, final_g):
    B = x.shape[0]
    pad = jnp.zeros((B, PAD, D_MODEL), x.dtype)
    meta = jnp.broadcast_to(meta_tokens.astype(x.dtype)[None], (B, N_META, D_MODEL))
    h = jnp.concatenate([pad, meta, x], axis=1)
    pos = jnp.arange(h.shape[1]) - PAD
    for l in range(DEPTH):
        h = hybrid_layer(h, pos, norm_g[l], w_in[l], b_f[l], g_cq[l], g_ckv[l],
                         w_uq[l], w_ukv[l], sinks[l], w_branch[l], w_out[l])
    h = rmsnorm(h, final_g)
    return h[:, BLK:]


HEAD_DIM = 64
A_HEADS = 4
A_VDIM = 2 * HEAD_DIM
B_HEADS = 8
B_BRANCHES = ((128, 1), (512, 4), (2048, 16))
B_BLOCK = 128
C_HEADS = 16
C_Q_RANK = 384
C_KV_RANK = 256
C_NOPE = 64
C_ROPE = 32
C_VDIM = 64
C_SCALE = (C_NOPE + C_ROPE) ** -0.5
IDX_HEADS = 8
IDX_DIM = 64
IDX_ROPE = 32
TOPK_MAX = 256
Q_BLOCK = 128
D_FF = 4 * D_MODEL
PLE_DIM = 256
N_EVEN = (DEPTH + 1) // 2
N_ODD = DEPTH // 2
AB_SPLITS = (A_HEADS * 2 * HEAD_DIM, A_HEADS * 2 * HEAD_DIM, A_HEADS * A_VDIM,
             B_HEADS * HEAD_DIM, B_HEADS * HEAD_DIM, B_HEADS * HEAD_DIM)
AB_IN = sum(AB_SPLITS)
AB_OUT = A_HEADS * A_VDIM + B_HEADS * HEAD_DIM
C_SPLITS = (C_Q_RANK, C_KV_RANK, C_ROPE, IDX_DIM, IDX_HEADS)
C_IN = sum(C_SPLITS)
C_OUT = C_HEADS * C_VDIM


F32 = jnp.float32

def rms(x, g):
    xf = x.astype(F32)
    y = xf * lax.rsqrt(jnp.mean(xf * xf, axis=-1, keepdims=True) + EPS) * g.astype(F32)
    return y.astype(x.dtype)

def rope_2(x, pos):
    half = x.shape[-1] // 2
    inv = ROPE_THETA ** (-jnp.arange(half, dtype=F32) / half)
    ang = pos.astype(F32)[:, None] * inv[None, :]
    cos = jnp.cos(ang)[:, None, :]
    sin = jnp.sin(ang)[:, None, :]
    x1 = x[..., :half].astype(F32)
    x2 = x[..., half:].astype(F32)
    return jnp.concatenate([x1 * cos - x2 * sin, x1 * sin + x2 * cos], axis=-1).astype(x.dtype)

def split_cols(t, sizes):
    offs = np.cumsum(sizes)[:-1].tolist()
    return jnp.split(t, offs, axis=-1)

def diff_attention(q, k, v, lam):
    S = q.shape[3]
    scale = HEAD_DIM ** -0.5
    outs = []
    for start in range(0, S, Q_BLOCK):
        end = start + Q_BLOCK
        s = jnp.einsum('bhmqd,bhmkd->bhmqk', q[:, :, :, start:end], k[:, :, :, :end]).astype(F32) * scale
        causal = jnp.arange(start, end)[:, None] >= jnp.arange(end)[None, :]
        pr = jax.nn.softmax(jnp.where(causal, s, -jnp.inf), axis=-1)
        a = pr[:, :, 0] - lam * pr[:, :, 1]
        outs.append(jnp.einsum('bhqk,bhkd->bhqd', a.astype(v.dtype), v[:, :, :end]))
    return jnp.concatenate(outs, axis=2)

def dilated_branch(q, k, v, window, dilation):
    Bn, H, S, dh = q.shape
    steps = window // dilation
    L = S // dilation
    nb = -(-L // B_BLOCK)
    Lp = nb * B_BLOCK

    def strided(t):
        t = t.reshape(Bn, H, L, dilation, dh).transpose(0, 1, 3, 2, 4)
        t = jnp.pad(t, ((0, 0), (0, 0), (0, 0), (0, Lp - L), (0, 0)))
        return t.reshape(Bn, H, dilation, nb, B_BLOCK, dh)

    def with_prev(t):
        prev = jnp.pad(t, ((0, 0), (0, 0), (0, 0), (1, 0), (0, 0), (0, 0)))[:, :, :, :-1]
        return jnp.concatenate([prev, t], axis=-2)

    qb = strided(q)
    kk = with_prev(strided(k))
    vv = with_prev(strided(v))
    s = jnp.einsum('bhcnqd,bhcnkd->bhcnqk', qb, kk).astype(F32) * dh ** -0.5
    ki = jnp.arange(2 * B_BLOCK)[None, :]
    dist = (jnp.arange(B_BLOCK)[:, None] + B_BLOCK) - ki
    blk = jnp.arange(nb)[:, None, None]
    ok = (dist >= 0) & (dist <= steps) & ((blk > 0) | (ki >= B_BLOCK))
    s = jnp.where(ok, s, -jnp.inf)
    lse = jax.nn.logsumexp(s, axis=-1)
    pr = jnp.exp(s - lse[..., None])
    o = jnp.einsum('bhcnqk,bhcnkd->bhcnqd', pr.astype(v.dtype), vv)
    o = o.reshape(Bn, H, dilation, Lp, dh)[:, :, :, :L].transpose(0, 1, 3, 2, 4).reshape(Bn, H, S, dh)
    lse = lse.reshape(Bn, H, dilation, Lp)[..., :L].transpose(0, 1, 3, 2).reshape(Bn, H, S)
    return o, lse

def dilated_attention(q, k, v):
    res = [dilated_branch(q, k, v, w, d) for (w, d) in B_BRANCHES]
    outs = jnp.stack([r[0] for r in res]).astype(F32)
    lses = jnp.stack([r[1] for r in res])
    wts = jax.nn.softmax(lses, axis=0)
    return jnp.einsum('gbhs,gbhsd->bhsd', wts, outs)

def mixer_ab(h, pos, w_in, w_out, lq1, lk1, lq2, lk2, g_sub, lam_init):
    Bn, S, _ = h.shape
    aq, ak, av, bq, bk, bv = split_cols(h @ w_in, AB_SPLITS)
    def a_qk(t):
        t = rope_2(t.reshape(Bn, S, A_HEADS * 2, HEAD_DIM), pos)
        return t.reshape(Bn, S, A_HEADS, 2, HEAD_DIM).transpose(0, 2, 3, 1, 4)
    av = av.reshape(Bn, S, A_HEADS, A_VDIM).transpose(0, 2, 1, 3)
    lam = (jnp.exp(jnp.sum(lq1.astype(F32) * lk1.astype(F32)))
           - jnp.exp(jnp.sum(lq2.astype(F32) * lk2.astype(F32))) + lam_init)
    ao = diff_attention(a_qk(aq), a_qk(ak), av, lam)
    ao = rms(ao, g_sub) * (1.0 - lam_init)
    ao = ao.transpose(0, 2, 1, 3).reshape(Bn, S, A_HEADS * A_VDIM)
    def b_heads(t, rot):
        t = t.reshape(Bn, S, B_HEADS, HEAD_DIM)
        t = rope_2(t, pos) if rot else t
        return t.transpose(0, 2, 1, 3)
    bo = dilated_attention(b_heads(bq, True), b_heads(bk, True), b_heads(bv, False))
    bo = bo.transpose(0, 2, 1, 3).reshape(Bn, S, B_HEADS * HEAD_DIM).astype(h.dtype)
    return jnp.concatenate([ao.astype(h.dtype), bo], axis=-1) @ w_out

def partial_rope(t, pos):
    return jnp.concatenate([rope_2(t[..., :IDX_ROPE], pos), t[..., IDX_ROPE:]], axis=-1)

def mixer_c(h, pos, w_in, g_cq, g_ckv, w_uq, w_qi, w_uk, w_uv, w_out):
    Bn, S, _ = h.shape
    cq, ckv, krope, kidx, widx = split_cols(h @ w_in, C_SPLITS)
    cq = rms(cq, g_cq)
    ckv = rms(ckv, g_ckv)
    q = (cq @ w_uq).reshape(Bn, S, C_HEADS, C_NOPE + C_ROPE)
    q_lat = jnp.einsum('bshd,chd->bshc', q[..., :C_NOPE], w_uk)
    q_full = jnp.concatenate([q_lat, rope_2(q[..., C_NOPE:], pos)], axis=-1)
    k_rope = rope_2(krope[:, :, None, :], pos)[:, :, 0]
    kv = jnp.concatenate([ckv, k_rope], axis=-1)
    qi = partial_rope((cq @ w_qi).reshape(Bn, S, IDX_HEADS, IDX_DIM), pos)
    ki = partial_rope(kidx[:, :, None, :], pos)[:, :, 0]
    wi = widx.astype(F32) * IDX_HEADS ** -0.5
    k_sel = min(TOPK_MAX, S // 4)
    nb = S // Q_BLOCK

    def blocks(t):
        return t.reshape((Bn, nb, Q_BLOCK) + t.shape[2:]).swapaxes(0, 1)

    def one_block(args):
        qf, qib, wib, start = args
        tq = start + jnp.arange(Q_BLOCK)
        dots = jnp.einsum('bqhd,bsd->bqhs', qib, ki).astype(F32)
        score = jnp.einsum('bqh,bqhs->bqs', wib, jax.nn.relu(dots)) * IDX_DIM ** -0.5
        causal = jnp.arange(S)[None, :] <= tq[:, None]
        score = jnp.where(causal, score, -jnp.inf)
        _, idx = lax.top_k(score, k_sel)
        valid = idx <= tq[None, :, None]
        sel = jax.vmap(lambda kvb, ib: kvb[ib])(kv, idx)
        s = jnp.einsum('bqhc,bqkc->bqhk', qf, sel).astype(F32) * C_SCALE
        pr = jax.nn.softmax(jnp.where(valid[:, :, None, :], s, -jnp.inf), axis=-1)
        o_lat = jnp.einsum('bqhk,bqkc->bqhc', pr.astype(sel.dtype), sel[..., :C_KV_RANK])
        return jnp.einsum('bqhc,chd->bqhd', o_lat, w_uv)

    o = lax.map(one_block, (blocks(q_full), blocks(qi), blocks(wi), jnp.arange(nb) * Q_BLOCK))
    o = o.swapaxes(0, 1).reshape(Bn, S, C_OUT)
    return o @ w_out

def second_inputs(seed: int = 0) -> dict:
    key = jax.random.key(seed)
    ks = iter(jax.random.split(key, 32))

    def nrm(shape, fan_in):
        return jax.random.normal(next(ks), shape, F32) * fan_in ** -0.5

    def gain(shape):
        return 1.0 + 0.02 * jax.random.normal(next(ks), shape, F32)

    def small(shape):
        return 0.1 * jax.random.normal(next(ks), shape, F32)

    return {
        "x": jax.random.normal(next(ks), (BATCH, SEQ, D_MODEL), F32),
        "p": jax.random.normal(next(ks), (DEPTH, BATCH, SEQ, PLE_DIM), F32),
        "g_mix_pre": gain((DEPTH, D_MODEL)),
        "g_mix_post": gain((DEPTH, D_MODEL)),
        "g_mlp_pre": gain((DEPTH, D_MODEL)),
        "g_mlp_post": gain((DEPTH, D_MODEL)),
        "w_mlp_in": nrm((DEPTH, D_MODEL, D_FF), D_MODEL),
        "w_mlp_out": nrm((DEPTH, D_FF, D_MODEL), D_FF),
        "w_ple_proj": nrm((DEPTH, PLE_DIM, D_MODEL), PLE_DIM),
        "w_ple_gate": nrm((DEPTH, D_MODEL, D_MODEL), D_MODEL),
        "w_in_ab": nrm((N_EVEN, D_MODEL, AB_IN), D_MODEL),
        "w_out_ab": nrm((N_EVEN, AB_OUT, D_MODEL), AB_OUT),
        "diff_lq1": small((N_EVEN, HEAD_DIM)),
        "diff_lk1": small((N_EVEN, HEAD_DIM)),
        "diff_lq2": small((N_EVEN, HEAD_DIM)),
        "diff_lk2": small((N_EVEN, HEAD_DIM)),
        "g_diff_sub": gain((N_EVEN, A_VDIM)),
        "w_in_c": nrm((N_ODD, D_MODEL, C_IN), D_MODEL),
        "g_cq": gain((N_ODD, C_Q_RANK)),
        "g_ckv": gain((N_ODD, C_KV_RANK)),
        "w_uq": nrm((N_ODD, C_Q_RANK, C_HEADS * (C_NOPE + C_ROPE)), C_Q_RANK),
        "w_qi": nrm((N_ODD, C_Q_RANK, IDX_HEADS * IDX_DIM), C_Q_RANK),
        "w_uk": nrm((N_ODD, C_KV_RANK, C_HEADS, C_NOPE), C_KV_RANK),
        "w_uv": nrm((N_ODD, C_KV_RANK, C_HEADS, C_VDIM), C_KV_RANK),
        "w_out_c": nrm((N_ODD, C_OUT, D_MODEL), C_OUT),
    }

def second_block(x, p, g_mix_pre, g_mix_post, g_mlp_pre, g_mlp_post, w_mlp_in, w_mlp_out,
              w_ple_proj, w_ple_gate, w_in_ab, w_out_ab, diff_lq1, diff_lk1, diff_lq2,
              diff_lk2, g_diff_sub, w_in_c, g_cq, g_ckv, w_uq, w_qi, w_uk, w_uv, w_out_c):
    S = x.shape[1]
    pos = jnp.arange(S)
    h = x
    for i in range(DEPTH):
        hn = rms(h, g_mix_pre[i])
        j = i // 2
        if i % 2 == 0:
            lam_init = 0.8 - 0.6 * math.exp(-0.3 * i)
            y = mixer_ab(hn, pos, w_in_ab[j], w_out_ab[j], diff_lq1[j], diff_lk1[j],
                         diff_lq2[j], diff_lk2[j], g_diff_sub[j], lam_init)
        else:
            y = mixer_c(hn, pos, w_in_c[j], g_cq[j], g_ckv[j], w_uq[j], w_qi[j],
                        w_uk[j], w_uv[j], w_out_c[j])
        h = h + rms(y, g_mix_post[i])
        hn = rms(h, g_mlp_pre[i])
        y = jnp.square(jax.nn.relu(hn @ w_mlp_in[i])) @ w_mlp_out[i]
        h = h + rms(y, g_mlp_post[i])
        gate = jax.nn.sigmoid(h @ w_ple_gate[i])
        h = h + gate * (p[i] @ w_ple_proj[i])
    return h


def setup_inputs(seed=0):
    out = dict(first_inputs(seed))
    for name, value in second_inputs(seed + 1).items():
        if name != "x":
            out[name + "_2"] = value
    return out


def reference(
    x, meta_tokens, norm_g, w_in, b_f, g_cq, g_ckv, w_uq, w_ukv, sinks, w_branch, w_out,
    final_g, p_2, g_mix_pre_2, g_mix_post_2, g_mlp_pre_2, g_mlp_post_2, w_mlp_in_2, w_mlp_out_2,
    w_ple_proj_2, w_ple_gate_2, w_in_ab_2, w_out_ab_2, diff_lq1_2, diff_lk1_2, diff_lq2_2,
    diff_lk2_2, g_diff_sub_2, w_in_c_2, g_cq_2, g_ckv_2, w_uq_2, w_qi_2, w_uk_2, w_uv_2,
    w_out_c_2,
):
    x = first_block(
        x, meta_tokens, norm_g, w_in, b_f, g_cq, g_ckv, w_uq, w_ukv, sinks, w_branch, w_out,
        final_g,
    )
    return second_block(
        x, p_2, g_mix_pre_2, g_mix_post_2, g_mlp_pre_2, g_mlp_post_2, w_mlp_in_2, w_mlp_out_2,
        w_ple_proj_2, w_ple_gate_2, w_in_ab_2, w_out_ab_2, diff_lq1_2, diff_lk1_2, diff_lq2_2,
        diff_lk2_2, g_diff_sub_2, w_in_c_2, g_cq_2, g_ckv_2, w_uq_2, w_qi_2, w_uk_2, w_uv_2,
        w_out_c_2,
    )


_drawn_inputs = setup_inputs


def setup_inputs(seed=0):
    import zlib

    import numpy as np

    out = dict(_drawn_inputs(seed))
    spreads = {}
    factors = {'norm_g': 2.671,
     'g_cq': 7.683,
     'g_ckv': 5.5,
     'sinks': 8.0,
     'g_cq_2': 3.29,
     'g_ckv_2': 5.284}
    for name, (base, spread) in spreads.items():
        noise = np.random.default_rng([zlib.crc32(name.encode()), seed]).standard_normal(out[name].shape)
        drawn = base * np.exp(spread * noise) if base else spread * noise
        out[name] = __import__('jax').numpy.asarray(drawn.astype(out[name].dtype))
    for name, factor in factors.items():
        out[name] = (out[name] * factor).astype(out[name].dtype)
    return out
```

```python
import numpy as np
from contextlib import ExitStack

import concourse.bass as bass
from concourse import mybir

F = mybir.dt.float32
FR = mybir.dt.float32r
ALU = mybir.AluOpType
ACT = mybir.ActivationFunctionType
AX = mybir.AxisListType

D = 1024
NM = 16
S = 512
T = NM + S
EPS = 1e-6
NEG = -1e30
BIG = 3e38
TAKEN = -3e38
HALF = 264
PAN = 1024
RAW = 2
WS = 2
WTOTAL = 128 * 389184
LAM_INIT = 0.8 - 0.6

NORM_G, G_CQ, G_CKV, FINAL_G = 0, 16, 22, 26
MIX_PRE, MIX_POST, MLP_PRE, MLP_POST = 34, 50, 66, 82
DIFF_SUB, G_CQ2, G_CKV2, B_F, SINKS, LAMS = 98, 99, 102, 104, 106, 122
NSM = 122 + 256

IDENT, ONES, MASKF, MASKS, COS, SIN, T2, NCON = 0, 128, 256, 784, 1040, 1568, 2096, 2624


class Queue:

    def __init__(self, sem):
        self.sem, self.n, self.list, self.waited = sem, 0, [], {}

    def wait(self, *tokens):
        for t in tokens:
            if t is None:
                continue
            if isinstance(t, list):
                self.wait(*t)
                continue
            sem, v = t
            if self.waited.get(id(sem), 0) < v:
                self.waited[id(sem)] = v
                self.list.append(("wait", sem, v))

    def op(self, make, *after, count=True):
        self.wait(*after)
        self.list.append(("op", make, count))
        self.n += count
        return self.last()

    def chain(self, make, *after):
        return self.op(make, self.last(), *after)

    def last(self):
        return (self.sem, self.n) if self.n else None

    def dma(self, make, sem, *after):
        self.wait(*after)
        self.list.append(("dma", make, sem))

    def play(self, eng):
        for kind, a, b in self.list:
            if kind == "wait":
                eng.wait_ge(a, b)
            elif kind == "dma":
                a(eng).then_inc(b, 16)
            else:
                ins = a(eng)
                if b:
                    ins.then_inc(self.sem, 1)


def program(nc, A, out):
    with ExitStack() as ctx:
        def sb(name, cols, dt=F):
            return ctx.enter_context(nc.sbuf_tensor(name, [128, cols], dt))

        def sem(name):
            return ctx.enter_context(nc.semaphore(name))

        m = {
            "X": sb("X", 8 * T), "Hh": sb("Hh", 8 * T, FR), "Hl": sb("Hl", 8 * T, FR),
            "M": sb("M", 8 * T), "Q": sb("Q", 8 * T), "K": sb("K", 8 * T), "V": sb("V", 5 * 512),
            "Yh": sb("Yh", 8 * 512, FR), "Yl": sb("Yl", 8 * 512, FR), "Z": sb("Z", 4 * T),
            "raw": sb("raw", RAW * PAN), "wh": sb("wh", WS * PAN, FR), "wl": sb("wl", WS * PAN, FR),
            "P": sb("P", 3 * T), "PT": sb("PT", 2 * 640), "O": sb("O", 2 * 512),
            "tmp": sb("tmp", 2 * T), "rs": sb("rs", T), "st": sb("st", 64),
            "con": sb("con", NCON), "sm": sb("sm", NSM), "k1": sb("k1", 4),
        }
        PP = [ctx.enter_context(nc.psum_tensor(f"pp{i}", [128, 1024], F)) for i in range(4)]
        sems = {n: sem(n) for n in ("pe", "act", "dve", "pool", "sp", "in0", "in1", "in2", "in3", "md", "aug0", "aug1", "aug2", "aug3", "pin0", "pin1", "out")}
        sems["w"] = [sem(f"w{i}") for i in range(RAW)]
        spec = emit(m, PP, sems, A, out, None)[1]
        queues, _ = emit(m, PP, sems, A, out, spec)
        block = ctx.enter_context(nc.Block())

        @block.sync
        def _(eng):
            queues["sp"].play(eng)

        @block.scalar
        def _(eng):
            queues["act"].play(eng)

        @block.vector
        def _(eng):
            queues["dve"].play(eng)

        @block.gpsimd
        def _(eng):
            queues["pool"].play(eng)

        @block.tensor
        def _(eng):
            queues["pe"].play(eng)
    return spec


def emit(m, PP, sems, A, out, spec):
    SP, AC, DV, GP, PE = (Queue(sems[n]) for n in ("sp", "act", "dve", "pool", "pe"))
    panels = []
    con, sm, k1, st = m["con"], m["sm"], m["k1"], m["st"]

    def bank(b):
        return PP[b // 2][:, 512 * (b % 2):512 * (b % 2) + 512]

    free = [None] * 8

    def v3(name, n, c, off=0):
        return m[name][:, off:off + n * c].rearrange("p (c n) -> p c n", c=c)

    done = []
    where = []
    off = 0
    for _, _, kcs, cols in spec or []:
        where.append((off, len(kcs) * len(cols)))
        off += 128 * len(kcs) * len(cols)
    assert not spec or off == WTOTAL, off // 128
    landed, split_at = {}, {}

    def fetch(j):
        if j >= len(where):
            return
        o, n = where[j]
        dst = m["raw"][:, (j % RAW) * PAN:(j % RAW) * PAN + n]
        src = A["w"][o:o + 128 * n].rearrange("(p n) -> p n", p=128)
        SP.dma(lambda e: e.dma_start(dst, src), sems["w"][j % RAW], split_at.get(j - RAW))
        landed[j] = (sems["w"][j % RAW], 16 * (j // RAW + 1))

    def split(j):
        if j >= len(where):
            return
        n = where[j][1]
        raw = m["raw"][:, (j % RAW) * PAN:(j % RAW) * PAN + n]
        hi = m["wh"][:, (j % WS) * PAN:(j % WS) * PAN + n]
        lo = m["wl"][:, (j % WS) * PAN:(j % WS) * PAN + n]
        used = done[j - WS] if j >= WS else None
        a = AC.op(lambda e: e.activation(hi, raw, ACT.Copy), landed[j], used)
        b = DV.op(lambda e: e.tensor_tensor(lo, raw, hi.bitcast(F), ALU.subtract), a, used)
        split_at[j] = [a, b]
        fetch(j + RAW)

    def panel(name, idx, kcs, cols):
        kcs, cols = list(kcs), list(cols)
        j = len(panels)
        panels.append((name, idx, kcs, cols))
        assert len(kcs) * len(cols) <= PAN
        while len(done) < j:
            done.append(PE.last())
        if spec:
            if j == 0:
                for i in range(RAW):
                    fetch(i)
                split(0)
            split(j + 1)
        o, n = (j % WS) * PAN, len(kcs) * len(cols)
        hi, lo = (m[x][:, o:o + n].rearrange("p (k n) -> p k n", k=len(kcs)) for x in ("wh", "wl"))
        return hi, lo, split_at.get(j)

    def mm3(ps, wh, wl, xh, xl, first, last, *after):
        PE.op(lambda e: e.matmul(ps, wh, xh, start=first, stop=False), *after, count=False)
        PE.op(lambda e: e.matmul(ps, wh, xl, start=False, stop=False), count=False)
        return PE.op(lambda e: e.matmul(ps, wl, xh, start=False, stop=last), count=last)

    rot = {"banks": list(range(8)), "n": 0}

    def next_bank():
        b = rot["banks"][rot["n"] % len(rot["banks"])]
        rot["n"] += 1
        return b

    def gemm(pan, c0, c1, xh, xl, kc, ranges, ready, evac):
        hi, lo, there = pan
        for a, b in ranges:
            bk = next_bank()
            ps = bank(bk)[0:c1 - c0, 0:b - a]
            for k in range(kc):
                t = mm3(ps, hi[:, k, c0:c1], lo[:, k, c0:c1], xh[:, k, a:b], xl[:, k, a:b],
                        k == 0, k == kc - 1, there, ready, free[bk])
            free[bk] = evac(ps, a, b, t)

    def gemm_tok(name, idx, kc, cols, xh, xl, tiles, ready, evac):
        per = max(1, PAN // len(cols))
        bks = [next_bank() for _ in tiles]
        for k0 in range(0, kc, per):
            kcs = range(k0, min(kc, k0 + per))
            hi, lo, there = panel(name, idx, kcs, cols)
            for (a, b), bk in zip(tiles, bks):
                ps = bank(bk)[:, 0:len(cols)]
                for k in kcs:
                    t = mm3(ps, xh[:, k, a:a + 128], xl[:, k, a:a + 128], hi[:, k - k0, :], lo[:, k - k0, :],
                            k == 0, k == kc - 1, there, ready, free[bk] if k == 0 else None)
            if k0 + per < kc:
                PE.list[-1] = (*PE.list[-1][:2], True)
                PE.n += 1
        for n, ((a, b), bk) in enumerate(zip(tiles, bks)):
            free[bk] = evac(bank(bk)[0:b - a, 0:len(cols)], n, a, b, t)

    def parts(src, hi, lo, *after):
        a = AC.chain(lambda e: e.activation(hi, src, ACT.Copy), *after)
        return DV.chain(lambda e: e.tensor_tensor(lo, src, hi.bitcast(F), ALU.subtract), a, *after)

    tmp = v3("tmp", T, 2)
    ones = con[:, ONES:ONES + 128]

    def rstd(x, nch, width, n, *after):
        ranges = [(0, n)] if n <= 512 else [(0, HALF), (HALF, n)]
        bks = [next_bank() for _ in ranges]
        for c in range(nch):
            sq = tmp[:, c % 2, 0:n]
            a = AC.chain(lambda e, c=c, sq=sq: e.activation(sq, x[:, c, :], ACT.Square), PE.last(), DV.last(), *after)
            for (p, q), bk in zip(ranges, bks):
                t = PE.op(lambda e, sq=sq, bk=bk, c=c, p=p, q=q: e.matmul(
                    bank(bk)[:, 0:q - p], ones, sq[:, p:q], start=c == 0, stop=c == nch - 1), a, free[bk] if c == 0 else None)
        rs = m["rs"]
        for (p, q), bk in zip(ranges, bks):
            a = AC.chain(lambda e, bk=bk, p=p, q=q: e.activation(
                rs[:, p:q], bank(bk)[:, 0:q - p], ACT.Sqrt, bias=k1[:, 0:1], scale=1.0 / width), t, DV.last())
            free[bk] = a
        return DV.chain(lambda e: e.reciprocal(rs[:, 0:n], rs[:, 0:n]), a)

    def norm_parts(x, nch, width, n, g, hi, lo, *after):
        r = rstd(x, nch, width, n, *after)
        for c in range(nch):
            t = tmp[:, c % 2, 0:n]
            a = DV.chain(lambda e, c=c, t=t: e.scalar_tensor_tensor(
                out=t, in0=x[:, c, :], scalar=sm[:, g + c:g + c + 1], in1=m["rs"][:, 0:n], op0=ALU.mult, op1=ALU.mult),
                r, AC.last(), PE.last())
            r = parts(t, hi[:, c, :], lo[:, c, :], a)
        return r

    def add_norm(x, y, n, g):
        rstd(y, 8, D, n, DV.last())
        for c in range(8):
            t = tmp[:, c % 2, 0:n]
            DV.chain(lambda e, c=c, t=t: e.scalar_tensor_tensor(
                out=t, in0=y[:, c, :], scalar=sm[:, g + c:g + c + 1], in1=m["rs"][:, 0:n], op0=ALU.mult, op1=ALU.mult), AC.last(), PE.last())
            DV.chain(lambda e, c=c, t=t: e.tensor_tensor(x[:, c, :], x[:, c, :], t, ALU.add))

    ident = con[:, IDENT:IDENT + 128]
    units = {"n": 0}

    def attend(heads, finish, fill):
        pend1, pend2 = [], []

        def scores(u):
            n = units["n"]
            units["n"] += 1
            u["n"] = n
            qr, ext = u["qr"], u["ext"]
            u["p"] = []
            for x, (q, k) in enumerate(u["qk"]):
                pair = u["pair"] = (n * len(u["qk"]) + x) % 2
                slot = (n * len(u["qk"]) + x) % 3 if len(u["qk"]) == 1 else 0
                c0 = 0 if ext <= 512 else 1024 - ext
                sc = PP[pair][0:qr, c0:c0 + ext]
                fr = [free[2 * pair], free[2 * pair + 1]]
                if ext <= 512:
                    t = PE.op(lambda e, sc=sc, q=q, k=k: e.matmul(sc, q, k, start=True, stop=True), fr, u["ready"])
                else:
                    cut = ext - 512
                    PE.op(lambda e, pair=pair, q=q, k=k: e.matmul(PP[pair][0:qr, c0:512], q, k[:, 0:cut], start=True, stop=True), fr, u["ready"])
                    t = PE.op(lambda e, pair=pair, q=q, k=k: e.matmul(PP[pair][0:qr, 512:1024], q, k[:, cut:ext], start=True, stop=True))
                slot = u["slot"] = (n * len(u["qk"]) + x) % 3 if len(u["qk"]) == 1 else 2 * (n % 2) + x
                p = pbuf(slot)[0:qr, 0:ext]
                s = (n % 16) * 2 + 32 * x if len(u["qk"]) == 1 else (n % 8) * 4 + 2 * x
                neg, tot = st[0:qr, s:s + 1], u["sums"][x]
                a = DV.chain(lambda e, sc=sc, p=p, neg=neg: e.tensor_tensor_reduce(
                    p, sc, u["mask"], -u["scale"], u["init"], ALU.add, ALU.min, neg), t, pfree[slot], AC.last())
                free[2 * pair] = free[2 * pair + 1] = a
                b = AC.chain(lambda e, p=p, neg=neg, tot=tot: e.activation(
                    p, p, ACT.Exp, bias=neg, scale=-1.0, accum_out=tot), a)
                u["p"].append(p)
                u["neg"] = neg
                u["exp"] = b
            if "sink" in u:
                snk, e1 = u["sink"]
                AC.chain(lambda e: e.activation(e1, snk, ACT.Exp, bias=u["neg"], scale=1.0))
                DV.chain(lambda e: e.tensor_tensor(tot, tot, e1, ALU.add), AC.last())
            if "mix" in u:
                u["exp"] = u["mix"](u)

        def turn(u):
            qr = u["qr"]
            p = u["p"][0]
            big = [c for c in u["chunks"] if c[1] == 128]
            small = [c for c in u["chunks"] if c[1] != 128]
            slot = u["n"] % 2
            pt = m["PT"][:, slot * 640:slot * 640 + 640]
            u["pt"] = []
            for x, (o, rows, v) in enumerate(small):
                if qr == 128:
                    t = PE.op(lambda e, o=o: e.transpose(bank(5)[:, 0:128], p[:, o:o + 128], ident), free[5], u["exp"])
                else:
                    t = PE.op(lambda e, o=o, rows=rows: e.matmul(bank(5)[0:rows, 0:qr], p[:, o:o + rows], ident[0:qr, 0:qr], start=True, stop=True), free[5], u["exp"])
                free[5] = DV.chain(lambda e, rows=rows: e.tensor_copy(pt[0:rows, 512:512 + qr], bank(5)[0:rows, 0:qr]), t, ptfree[slot])
                u["pt"].append((pt[0:rows, 512:512 + qr], v))
                u["cp"] = [free[5]]
            if big:
                for x, (o, rows, v) in enumerate(big):
                    t = PE.op(lambda e, o=o, x=x: e.transpose(bank(4)[:, 128 * x:128 * x + 128], p[:, o:o + 128], ident), free[4] if x == 0 else None, u["exp"])
                    u["pt"].append((pt[:, 128 * x:128 * x + 128], v))
                w = 128 * len(big)
                if u["n"] % 2:
                    free[4] = AC.chain(lambda e: e.activation(pt[:, 0:w], bank(4)[:, 0:w], ACT.Copy), t, ptfree[slot])
                else:
                    free[4] = DV.chain(lambda e: e.tensor_copy(pt[:, 0:w], bank(4)[:, 0:w]), t, ptfree[slot])
                u["cp"] = [free[4], free[5] if small else None]
            pfree[u["slot"]] = t
            if "mix" in u:
                pfree[u["slot"] - 1] = t

        def product(u):
            qr = u["qr"]
            o = bank(6)[0:qr, u["o"]:u["o"] + u["dv"]]
            n = len(u["pt"])
            for x, (p, v) in enumerate(u["pt"]):
                t = PE.op(lambda e, x=x, p=p, v=v: e.matmul(o, p, v, start=x == 0, stop=x == n - 1),
                          u["cp"], free[6] if u["o"] == 0 else None, count=x == n - 1)
            ptfree[u["n"] % 2] = t
            if "end" in u:
                free[6], free[5] = finish(u, t)

        for u in heads + [None, None]:
            if u:
                scores(u)
                pend1.append(u)
            fill()
            if len(pend1) > 1 or not u and pend1:
                turn(pend1[0])
                pend2.append(pend1.pop(0))
                fill()
            if len(pend2) > 1 or not u and pend2 and not pend1:
                while len(pend2) > (1 if u else 0):
                    product(pend2.pop(0))

    pfree, ptfree = [None] * 4, [None, None]

    def pbuf(slot):
        return m["P"][:, slot * T:(slot + 1) * T] if slot < 3 else m["Z"][:, 0:T]

    def no_fill():
        pass

    def turn_out(o, qr, *after):
        for c in range(4):
            t = PE.op(lambda e, c=c: e.transpose(bank(5)[:, 128 * c:128 * c + qr], o[0:qr, 128 * c:128 * c + 128], ident[0:qr, 0:qr]),
                      free[5] if c == 0 else None, *after)
        return t

    def osb(u):
        return m["O"][0:u["qr"], 512 * (u["end"] % 2):512 * (u["end"] % 2) + 512]

    def divided(u, t, sums):
        qr = u["qr"]
        o = osb(u)
        DV.chain(lambda e: e.reciprocal(sums, sums), t, AC.last())
        return o, DV.chain(lambda e: e.tensor_tensor(
            o.rearrange("p (h d) -> p h d", h=8), bank(6)[0:qr, :].rearrange("p (h d) -> p h d", h=8),
            sums.unsqueeze(2).to_broadcast([qr, 8, 64]), ALU.mult), PE.last())

    X = v3("X", T, 8)
    SP.dma(lambda e: e.dma_start(m["X"][:, :], A["x"]), sems["in0"])
    AC.dma(lambda e: e.dma_start(con[:, :], A["con"]), sems["in1"])
    AC.dma(lambda e: e.dma_start(sm[:, :], A["sm"]), sems["in2"])
    loaded = [(sems["in0"], 16), (sems["in1"], 16), (sems["in2"], 16)]
    DV.chain(lambda e: e.memset(k1[:, 0:1], EPS))
    DV.chain(lambda e: e.memset(k1[:, 1:2], 1.0))
    DV.chain(lambda e: e.memset(k1[:, 2:3], BIG))
    for q in (AC, DV, PE):
        q.wait(loaded, DV.last())

    maskF = con[:, MASKF:MASKF + T]
    maskS = con[:, MASKS:MASKS + 256]
    cos, sin, t2 = (con[:, o:o + T] for o in (COS, SIN, T2))
    big = k1[:, 2:3]

    def rope64(ps, dst, a, b, t):
        p, q = (tmp[:, i, 0:b - a] for i in range(2))
        for r in range(4):
            s = r ^ 1
            DV.op(lambda e, r=r, s=s: e.tensor_tensor(
                p[32 * r:32 * r + 32], ps[32 * s:32 * s + 32, :], sin[32 * s:32 * s + 32, a:b], ALU.mult), t, AC.last(), PE.last(), DV.last() if r == 0 else None)
        DV.op(lambda e: e.tensor_tensor(q, ps, cos[:, a:b], ALU.mult))
        f = DV.last()
        DV.chain(lambda e: e.tensor_tensor(dst, p, q, ALU.add))
        return f

    def rope32(ps, row, dst, a, b, t):
        p, q = (tmp[row:row + 32, i, 0:b - a] for i in range(2))
        DV.chain(lambda e: e.tensor_tensor(p, ps[96:128, :], t2[96:128, a:b], ALU.mult), t, AC.last(), PE.last())
        f = DV.op(lambda e: e.tensor_tensor(q, ps[row:row + 32, :], t2[row:row + 32, a:b], ALU.mult))
        DV.chain(lambda e: e.tensor_tensor(dst, p, q, ALU.add))
        return f

    K8, K4, K3, K2 = range(8), range(4), range(3), range(2)

    def cols(a, n):
        return range(a, a + n)

    def swapped(a):
        return [*range(a + 16, a + 32), *range(a, a + 16)]

    def mla_q(name, l, heads, base, xh, xl, ranges, ready, Q):
        for h in range(0, len(heads), 2):
            cs = []
            for x in heads[h:h + 2]:
                cs += [*cols(96 * x, 64), *cols(96 * x + 64, 32), *swapped(96 * x + 64)]
            pan = panel(name, l, K3, cs)
            for x in range(2):
                def evac(ps, a, b, t, x=x, h=h):
                    AC.chain(lambda e: e.activation(Q[0:64, h + x, a:b], ps[0:64, :], ACT.Copy), t)
                    return rope32_free(ps, Q[64:96, h + x, a:b], a, b, t)
                gemm(pan, 128 * x, 128 * x + 128, xh, xl, 3, ranges, ready, evac)

    def rope32_free(ps, dst, a, b, t):
        f = AC.last()
        return [f, rope32(ps, 64, dst, a, b, t)]

    def two_heads(dst, h, a, b):
        def copy(ps, t):
            x = AC.chain(lambda e: e.activation(dst[0:64, h, a:b], ps[0:64, :], ACT.Copy), t)
            y = DV.chain(lambda e: e.tensor_copy(dst[0:64, h + 1, a:b], ps[64:128, :]), t)
            return [x, y]
        return copy

    TOKR = [(0, HALF), (HALF, T)]
    TILES = [(0, NM)] + [(NM + 128 * i, NM + 128 * i + 128) for i in range(4)]

    def first_layer(l):
        Hh, Hl = v3("Hh", T, 8), v3("Hl", T, 8)
        Q, K, M, Z = v3("Q", T, 8), v3("K", T, 8), v3("M", T, 8), v3("Z", T, 4)
        V = v3("V", 512, 5)
        Yh, Yl = v3("Yh", T, 4), v3("Yl", T, 4)
        rot["banks"] = list(range(8))
        hr = norm_parts(X, 8, D, T, NORM_G + 8 * l, Hh, Hl)

        def win(c0, n, evac):
            gemm(panel("w_in", l, K8, cols(c0, n)), 0, n, Hh, Hl, 8, TOKR, hr, evac)

        def zgate(c0):
            for c in range(4):
                def evac(ps, a, b, t, c=c):
                    g = tmp[:, 0, 0:b - a]
                    x = AC.chain(lambda e: e.activation(g, ps, ACT.Tanh, scale=0.5), t, DV.last(), PE.last())
                    return DV.chain(lambda e: e.scalar_tensor_tensor(
                        out=Z[:, c, a:b], in0=g, scalar=1.0, in1=ps, op0=ALU.add, op1=ALU.mult), x, PE.last())
                win(c0 + 128 * c, 128, evac)

        def merge(n):
            for c in range(8):
                tg = m["P"][:, T * (c % 2):T * (c % 2) + T]

                def gate(ps, a, b, t, tg=tg):
                    return AC.chain(lambda e: e.activation(tg[:, a:b], ps, ACT.Tanh, scale=0.5), t, DV.last(), PE.last())
                win(4520 + 1024 * n + 128 * c, 128, gate)
                g = AC.last()

                def proj(ps, a, b, t, tg=tg, c=c, g=g):
                    if n == 0:
                        return DV.chain(lambda e: e.scalar_tensor_tensor(
                            out=M[:, c, a:b], in0=tg[:, a:b], scalar=1.0, in1=ps, op0=ALU.add, op1=ALU.mult), t, g)
                    q = tmp[:, 0, 0:b - a]
                    f = DV.chain(lambda e: e.scalar_tensor_tensor(
                        out=q, in0=tg[:, a:b], scalar=1.0, in1=ps, op0=ALU.add, op1=ALU.mult), t, g, AC.last())
                    DV.chain(lambda e: e.tensor_tensor(M[:, c, a:b], M[:, c, a:b], q, ALU.add))
                    return f
                gemm(panel("w_branch", (l, n), K4, cols(128 * c, 128)), 0, 128, Yh, Yl, 4, TOKR, DV.last(), proj)

        def finish(u, t):
            qr, a = u["qr"], u["tok"]
            o, r = divided(u, t, u["all"])
            x = turn_out(o, qr, r)
            q = tmp[:, 0, 0:4 * qr].rearrange("p (c n) -> p c n", c=4)
            f = DV.chain(lambda e: e.tensor_tensor(q, bank(5)[:, :].rearrange("p (c n) -> p c n", c=4)[:, :, 0:qr],
                                                   Z[:, :, a:a + qr], ALU.mult), x, AC.last(), PE.last())
            parts(q, Yh[:, :, a:a + qr], Yl[:, :, a:a + qr], f)
            return r, f

        def units_of(qk, vof, scale, sinks=None, window=False):
            us = []
            for i in range(-1 if l == 0 else 0, 4):
                qr, a = (NM, 0) if i < 0 else (128, NM + 128 * i)
                if i < 0:
                    k0, ext = 0, NM
                    mk = maskF[0:NM, 400:400 + NM] if not window else maskS[0:NM, 128:128 + NM]
                elif window:
                    k0 = 0 if i == 0 else NM + 128 * (i - 1)
                    ext = a + 128 - k0
                    mk = maskS[:, 256 - ext:256]
                else:
                    k0, ext = 0, a + 128
                    mk = maskF[:, T - ext:T]
                chunks = [(x - k0, y - x, v) for v, (x, y) in enumerate(TILES) if x >= k0 and y <= k0 + ext]
                sums = st[0:qr, 32 + 16 * (i % 2):32 + 16 * (i % 2) + 8]
                e1 = st[0:qr, 32 + 16 * (i % 2) + 8:32 + 16 * (i % 2) + 16]
                for h in range(8):
                    q, k = qk(h)
                    u = dict(qr=qr, ext=ext, tok=a, mask=mk, scale=scale, qk=[(q[:, a:a + qr], k[:, k0:k0 + ext])],
                             chunks=[(o, r, vof(v, h)[0:r]) for o, r, v in chunks], dv=64, o=64 * h,
                             sums=[sums[:, h:h + 1]], all=sums, init=big[0:qr], ready=[DV.last(), AC.last()])
                    if sinks is not None:
                        u["init"] = negs[0:qr, h:h + 1]
                        u["sink"] = (sm[0:qr, sinks + h:sinks + h + 1], e1[:, h:h + 1])
                    if h == 7:
                        u["end"] = i + 1
                    us.append(u)
            return us

        cum = m["Z"][0:8, 0:T]
        w1 = m["Z"][0:8, T:2 * T]
        w2 = m["Z"][0:8, 2 * T:3 * T]

        def fgate(ps, a, b, t):
            return DV.chain(lambda e: e.tensor_scalar(cum[:, a:b], ps[0:8], sm[0:8, B_F + l:B_F + l + 1], None, ALU.add), t, PE.last(), AC.last())
        gemm(panel("w_in", l, K8, [*cols(1536, 8)] * 16), 0, 128, Hh, Hl, 8, TOKR, hr, fgate)
        AC.chain(lambda e: e.activation(w1, cum, ACT.Abs), DV.last())
        AC.chain(lambda e: e.activation(w1, w1, ACT.Exp, scale=-1.0))
        AC.chain(lambda e: e.activation(w1, w1, ACT.Ln, bias=k1[0:8, 1:2], scale=1.0))
        DV.chain(lambda e: e.scalar_tensor_tensor(out=w2, in0=cum, scalar=0.0, in1=w1, op0=ALU.min, op1=ALU.subtract), AC.last())
        DV.chain(lambda e: e.memset(w1, 1.0))
        DV.chain(lambda e: e.tensor_tensor_scan(cum, w1, w2, 0.0, ALU.mult, ALU.add))
        DV.chain(lambda e: e.tensor_scalar(w1, cum, 8.0, None, ALU.mult))
        DV.chain(lambda e: e.tensor_scalar(w2, cum, -8.0, None, ALU.mult))
        f = DV.last()
        DV.chain(lambda e: e.memset(Q[64:66, :, :], 1.0), PE.last())
        r = DV.chain(lambda e: e.memset(K[64:66, :, :], 1.0))
        for h in range(8):
            SP.dma(lambda e, h=h: e.dma_start(Q[64:65, h, :], w1[h:h + 1, :]), sems[f"aug{2 * l}"], f, r)
            SP.dma(lambda e, h=h: e.dma_start(K[65:66, h, :], w2[h:h + 1, :]), sems[f"aug{2 * l + 1}"])
        for dst, c0 in ((Q, 0), (K, 512)):
            for c in range(4):
                win(c0 + 128 * c, 128, lambda ps, a, b, t, c=c, dst=dst: two_heads(dst, 2 * c, a, b)(ps, t))

        def vcopy(ps, n, a, b, t):
            return (AC.chain(lambda e: e.activation(V[0:b - a, n, :], ps, ACT.Copy), t, PE.last()))
        gemm_tok("w_in", l, 8, cols(1024, 512), Hh, Hl, TILES, hr, vcopy)
        for q in (AC, DV, PE):
            q.wait((sems[f"aug{2 * l}"], 8 * 16), (sems[f"aug{2 * l + 1}"], 8 * 16))
        zgate(1544)
        rot["banks"] = [7]
        attend(units_of(lambda h: (Q[0:66, h, :], K[0:66, h, :]), lambda v, h: V[:, v, 64 * h:64 * h + 64], 0.125), finish, no_fill)
        rot["banks"] = list(range(8))
        merge(0)

        B0 = 2056
        cq = m["Z"][:, 0:3 * T].rearrange("p (c n) -> p c n", c=3)
        ckv = m["V"][:, 0:2 * T].rearrange("p (c n) -> p c n", c=2)
        for dst, n, c0 in ((cq, 3, B0), (ckv, 2, B0 + 384)):
            for c in range(n):
                win(c0 + 128 * c, 128, lambda ps, a, b, t, c=c, dst=dst: AC.chain(
                    lambda e: e.activation(dst[:, c, a:b], ps, ACT.Copy), t, DV.last(), PE.last()))
        kr = K[64:96, 0, :]

        def krope(ps, a, b, t):
            return rope32(ps, 64, kr[:, a:b], a, b, t)
        c0 = B0 + 640
        gemm(panel("w_in", l, K8, [*cols(c0, 32), *swapped(c0)] * 2), 0, 128, Hh, Hl, 8, TOKR, hr, krope)
        for h in range(1, 8):
            GP.op(lambda e, h=h: e.tensor_copy(K[64:96, h, :], kr), DV.last(), PE.last())
        cqh, cql = v3("Yh", T, 3), v3("Yl", T, 3)
        ckh, ckl = v3("Yh", T, 2, 3 * T), v3("Yl", T, 2, 3 * T)
        norm_parts(cq, 3, 384, T, G_CQ + 3 * l, cqh, cql, AC.last())
        r = norm_parts(ckv, 2, 256, T, G_CKV + 2 * l, ckh, ckl, AC.last())
        mla_q("w_uq", l, list(range(8)), 0, cqh, cql, TOKR, r, Q)
        pan = panel("w_ukv", l, K2, [128 * h + d for h in range(8) for d in range(64)])
        for c in range(4):
            gemm(pan, 128 * c, 128 * c + 128, ckh, ckl, 2, TOKR, r, lambda ps, a, b, t, c=c: two_heads(K, 2 * c, a, b)(ps, t))
        gemm_tok("w_ukv", l, 2, [128 * h + 64 + d for h in range(8) for d in range(64)], ckh, ckl, TILES, r, vcopy)
        zgate(B0 + 672)
        PE.wait(GP.last())
        rot["banks"] = [7]
        attend(units_of(lambda h: (Q[0:96, h, :], K[0:96, h, :]), lambda v, h: V[:, v, 64 * h:64 * h + 64], 96 ** -0.5), finish, no_fill)
        rot["banks"] = list(range(8))
        merge(1)

        C0 = 3240
        for c in range(4):
            cs = [*cols(C0 + 64 * c, 64), *cols(C0 + 64 * (c + 4), 64)]
            gemm(panel("w_in", l, K8, cs), 0, 128, Hh, Hl, 8, TOKR, hr,
                 lambda ps, a, b, t, c=c: rope64(ps, Q[:, c, a:b], a, b, t))
        win(C0 + 512, 128, lambda ps, a, b, t: rope64(ps, K[:, 0, a:b], a, b, t))
        gemm_tok("w_in", l, 8, cols(C0 + 640, 128), Hh, Hl, TILES, hr, lambda ps, n, a, b, t: AC.chain(
            lambda e: e.activation(V[0:b - a, n, 0:128], ps, ACT.Copy), t))
        zgate(C0 + 768)
        negs = m["rs"][:, 0:8]
        DV.chain(lambda e: e.tensor_scalar(negs, sm[:, SINKS + 8 * l:SINKS + 8 * l + 8], -1.0, None, ALU.mult))
        rot["banks"] = [7]
        attend(units_of(lambda h: (Q[64 * (h // 4):64 * (h // 4) + 64, h % 4, :], K[64 * (h // 4):64 * (h // 4) + 64, 0, :]),
                        lambda v, h: V[:, v, 64 * (h // 4):64 * (h // 4) + 64], 0.125, SINKS + 8 * l, True), finish, no_fill)
        rot["banks"] = list(range(8))
        merge(2)

        for c in range(8):
            r = parts(M[:, c, :], Hh[:, c, :], Hl[:, c, :], DV.last(), PE.last())
        for c in range(8):
            gemm(panel("w_out", l, K8, cols(128 * c, 128)), 0, 128, Hh, Hl, 8, TOKR, r,
                 lambda ps, a, b, t, c=c: DV.chain(lambda e: e.scalar_tensor_tensor(
                     out=X[:, c, a:b], in0=ps, scalar=0.25, in1=X[:, c, a:b], op0=ALU.mult, op1=ALU.add), t))

    for l in range(2):
        first_layer(l)

    X2 = X[:, :, NM:T]
    rstd(X2, 8, D, S, DV.last())
    for c in range(8):
        DV.chain(lambda e, c=c: e.scalar_tensor_tensor(
            out=X2[:, c, :], in0=X2[:, c, :], scalar=sm[:, FINAL_G + c:FINAL_G + c + 1], in1=m["rs"][:, 0:S], op0=ALU.mult, op1=ALU.mult))
    maskD = con[:, MASKF:MASKF + S]
    ALLR = [(0, S)]
    ST = [(128 * i, 128 * i + 128) for i in range(4)]
    Hh, Hl = v3("Hh", S, 8), v3("Hl", S, 8)
    Yh, Yl = v3("Yh", S, 8), v3("Yl", S, 8)
    M = v3("M", S, 8)
    V = v3("V", 512, 4)

    def out_proj(name, l):
        r = DV.last()
        for c in range(8):
            gemm(panel(name, l, K8, cols(128 * c, 128)), 0, 128, Yh, Yl, 8, ALLR, r, lambda ps, a, b, t, c=c: AC.chain(
                lambda e: e.activation(M[:, c, :], ps, ACT.Copy), t, DV.last(), PE.last()))

    def mlp(i):
        r = norm_parts(X2, 8, D, S, MLP_PRE + 8 * i, Hh, Hl, DV.last())
        for f in range(4):
            for c in range(8):
                def evac(ps, a, b, t, c=c):
                    q = tmp[:, 0, 0:S]
                    x = AC.chain(lambda e: e.activation(q, ps, ACT.Relu), t, DV.last(), PE.last())
                    AC.chain(lambda e: e.activation(q, q, ACT.Square))
                    parts(q, Yh[:, c, :], Yl[:, c, :], AC.last(), PE.last())
                    return x
                gemm(panel("w_mlp_in_2", i, K8, cols(1024 * f + 128 * c, 128)), 0, 128, Hh, Hl, 8, ALLR, r, evac)
            y = DV.last()
            for c in range(8):
                def add(ps, a, b, t, c=c):
                    if f == 0:
                        return DV.chain(lambda e: e.tensor_copy(M[:, c, :], ps), t, AC.last())
                    return DV.chain(lambda e: e.tensor_tensor(M[:, c, :], ps, M[:, c, :], ALU.add), t)
                gemm(panel("w_mlp_out_2", i, range(8 * f, 8 * f + 8), cols(128 * c, 128)), 0, 128, Yh, Yl, 8, ALLR, y, add)
        add_norm(X2, M, S, MLP_POST + 8 * i)

    def ple(i):
        for c in range(8):
            r = parts(X2[:, c, :], Hh[:, c, :], Hl[:, c, :], DV.last(), PE.last())
        p = v3("Z", S, 2)
        SP.dma(lambda e: e.dma_start(m["Z"][:, 0:2 * S], A["p"][i]), sems[f"pin{i}"], PE.last(), AC.last(), DV.last())
        for c in range(2):
            y = parts(p[:, c, :], Yh[:, c, :], Yl[:, c, :], (sems[f"pin{i}"], 16), PE.last())
        for c in range(8):
            tg = m["P"][:, T * (c % 2):T * (c % 2) + S]
            gemm(panel("w_ple_gate_2", i, K8, cols(128 * c, 128)), 0, 128, Hh, Hl, 8, ALLR, r, lambda ps, a, b, t, tg=tg: AC.chain(
                lambda e: e.activation(tg, ps, ACT.Tanh, scale=0.5), t, DV.last(), PE.last()))
            g = AC.last()

            def add(ps, a, b, t, tg=tg, c=c, g=g):
                f = DV.chain(lambda e: e.scalar_tensor_tensor(out=tg, in0=tg, scalar=1.0, in1=ps, op0=ALU.add, op1=ALU.mult), t, g)
                DV.chain(lambda e: e.scalar_tensor_tensor(
                    out=X2[:, c, :], in0=tg, scalar=0.5, in1=X2[:, c, :], op0=ALU.mult, op1=ALU.add), PE.last())
                return f
            gemm(panel("w_ple_proj_2", i, K2, cols(128 * c, 128)), 0, 128, Yh, Yl, 2, ALLR, y, add)

    def finish2(y0):
        def finish(u, t):
            qr, a = u["qr"], u["tok"]
            o, r = divided(u, t, u["all"])
            x = turn_out(o, qr, r)
            src = bank(5)[:, :].rearrange("p (c n) -> p c n", c=4)
            f = parts(src, Yh[:, y0:y0 + 4, a:a + 128], Yl[:, y0:y0 + 4, a:a + 128], x)
            return r, f
        return finish

    def plain_units(qk, vof, scale, mask):
        us = []
        for i in range(4):
            ext = 128 * i + 128
            sums = st[:, 32 + 16 * (i % 2):32 + 16 * (i % 2) + 8]
            for h in range(8):
                q, k = qk(h)
                u = dict(qr=128, ext=ext, tok=128 * i, mask=mask(i, ext), scale=scale, qk=[(q[:, 128 * i:ext], k[:, 0:ext])],
                         chunks=[(128 * v, 128, vof(v, h)) for v in range(i + 1)], dv=64, o=64 * h,
                         sums=[sums[:, h:h + 1]], all=sums, init=big, ready=[DV.last(), AC.last(), GP.last()])
                if h == 7:
                    u["end"] = i
                us.append(u)
        return us

    def vcopy2(ps, n, a, b, t):
        return AC.chain(lambda e: e.activation(V[:, n, :], ps, ACT.Copy), t, PE.last())

    def mixer_ab():
        r = norm_parts(X2, 8, D, S, MIX_PRE, Hh, Hl, DV.last())
        Q, K = v3("Q", S, 8), v3("K", S, 8)
        for dst, o, c0 in ((Q, 0, 0), (K, 0, 512), (Q, 4, 1536), (K, 4, 2048)):
            for c in range(4):
                gemm(panel("w_in_ab_2", 0, K8, cols(c0 + 128 * c, 128)), 0, 128, Hh, Hl, 8, ALLR, r,
                     lambda ps, a, b, t, c=c, dst=dst, o=o: rope64(ps, dst[:, o + c, :], a, b, t))
        gemm_tok("w_in_ab_2", 0, 8, cols(1024, 512), Hh, Hl, ST, r, vcopy2)
        la = [sm[:, LAMS + 64 * i:LAMS + 64 * i + 64] for i in range(4)]
        e2 = k1[:, 3:4]
        pr = m["rs"][:, 0:64]
        lam = m["rs"][:, 64:68]
        for x in range(2):
            DV.chain(lambda e, x=x: e.tensor_tensor_reduce(pr, la[2 * x], la[2 * x + 1], 1.0, 0.0, ALU.mult, ALU.add, lam[:, x:x + 1]))
        AC.chain(lambda e: e.activation(lam[:, 0:2], lam[:, 0:2], ACT.Exp), DV.last())
        DV.chain(lambda e: e.scalar_tensor_tensor(out=e2, in0=lam[:, 1:2], scalar=-LAM_INIT, in1=lam[:, 0:1], op0=ALU.add, op1=ALU.subtract), AC.last())

        def mix(u):
            s = u["pairsum"]
            p1, p2 = u["p"]
            DV.chain(lambda e: e.reciprocal(s, s), AC.last())
            DV.chain(lambda e: e.tensor_scalar(p2, p2, s[:, 1:2], e2, ALU.mult, ALU.mult))
            return DV.chain(lambda e: e.scalar_tensor_tensor(out=p1, in0=p1, scalar=s[:, 0:1], in1=p2, op0=ALU.mult, op1=ALU.add))

        def finish(u, t):
            a = u["tok"]
            o = osb(u)
            f = AC.chain(lambda e: e.activation(o, bank(6), ACT.Copy), t, PE.last())
            sq = tmp[:, 1, 0:512]
            ss = m["rs"][:, 128:132]
            DV.chain(lambda e: e.tensor_tensor(sq, o, o, ALU.mult), f, PE.last())
            DV.chain(lambda e: e.tensor_reduce(ss, sq.rearrange("p (h d) -> p h d", h=4), AX.X, ALU.add))
            AC.chain(lambda e: e.activation(ss, ss, ACT.Sqrt, bias=k1[:, 0:1], scale=1.0 / 128), DV.last())
            DV.chain(lambda e: e.reciprocal(ss, ss), AC.last())
            o3 = o.rearrange("p (h d) -> p h d", h=4)
            r = DV.chain(lambda e: e.tensor_tensor(o3, o3, ss.unsqueeze(2).to_broadcast([128, 4, 128]), ALU.mult))
            x = turn_out(o, 128, r)
            q = tmp[:, 0, 0:512]
            y = DV.chain(lambda e: e.tensor_scalar(q, bank(5), sm[:, DIFF_SUB:DIFF_SUB + 1], 1.0 - LAM_INIT, ALU.mult, ALU.mult), x, AC.last(), PE.last())
            q3 = q.rearrange("p (c n) -> p c n", c=4)
            parts(q3, Yh[:, 0:4, a:a + 128], Yl[:, 0:4, a:a + 128], y)
            return f, y

        us = []
        for i in range(4):
            ext = 128 * i + 128
            for h in range(4):
                s = m["rs"][:, 136 + 8 * (h % 2):138 + 8 * (h % 2)]
                u = dict(qr=128, ext=ext, tok=128 * i, mask=con[:, MASKF + T - ext:MASKF + T], scale=0.125,
                         qk=[(Q[64 * x:64 * x + 64, h, 128 * i:ext], K[64 * x:64 * x + 64, h, 0:ext]) for x in range(2)],
                         chunks=[(128 * v, 128, V[:, v, 128 * h:128 * h + 128]) for v in range(i + 1)], dv=128, o=128 * h,
                         sums=[s[:, 0:1], s[:, 1:2]], pairsum=s, init=big, mix=mix, ready=[DV.last(), AC.last()])
                if h == 3:
                    u["end"] = i
                us.append(u)
        rot["banks"] = [7]
        attend(us, finish, no_fill)
        rot["banks"] = list(range(8))
        SP.dma(lambda e: e.dma_start(maskD, A["maskd"]), sems["md"], DV.last())
        gemm_tok("w_in_ab_2", 0, 8, cols(2560, 512), Hh, Hl, ST, r, vcopy2)
        DV.wait((sems["md"], 16))
        rot["banks"] = [7]
        attend(plain_units(lambda h: (Q[64 * (h % 2):64 * (h % 2) + 64, 4 + h // 2, :], K[64 * (h % 2):64 * (h % 2) + 64, 4 + h // 2, :]),
                           lambda v, h: V[:, v, 64 * h:64 * h + 64], 0.125, lambda i, ext: maskD[:, S - ext:S]), finish2(4), no_fill)
        rot["banks"] = list(range(8))
        out_proj("w_out_ab_2", 0)
        add_norm(X2, M, S, MIX_POST)

    def mixer_c():
        r = norm_parts(X2, 8, D, S, MIX_PRE + 8, Hh, Hl, DV.last())
        cq, ckv = v3("P", S, 3), v3("V", S, 2)
        ki = m["M"][0:64, 0:S]
        kr = m["M"][64:96, S:2 * S]
        Q, K = v3("Q", S, 8), v3("K", S, 8)
        for dst, n, c0 in ((cq, 3, 0), (ckv, 2, 384)):
            for c in range(n):
                gemm(panel("w_in_c_2", 0, K8, cols(c0 + 128 * c, 128)), 0, 128, Hh, Hl, 8, ALLR, r, lambda ps, a, b, t, c=c, dst=dst: AC.chain(
                    lambda e: e.activation(dst[:, c, :], ps, ACT.Copy), t, DV.last(), PE.last()))
        gemm(panel("w_in_c_2", 0, K8, [*cols(640, 32), *swapped(640)] * 2), 0, 128, Hh, Hl, 8, ALLR, r,
             lambda ps, a, b, t: rope32(ps, 64, kr, a, b, t))

        def index_rope(dst):
            def evac(ps, a, b, t):
                x = AC.chain(lambda e: e.activation(dst[32:64], ps[32:64, :], ACT.Copy), t, PE.last())
                return [x, rope32(ps, 0, dst[0:32], a, b, t)]
            return evac
        gemm(panel("w_in_c_2", 0, K8, [*cols(672, 64), *cols(704, 32), *swapped(672)]), 0, 128, Hh, Hl, 8, ALLR, r, index_rope(ki))
        k2 = st[:, 0:32].rearrange("p (i h) -> p i h", i=4)
        gemm_tok("w_in_c_2", 0, 8, cols(736, 8), Hh, Hl, ST, r, lambda ps, n, a, b, t: AC.chain(
            lambda e: e.activation(k2[:, n, :], ps, ACT.Copy, scale=8.0 ** -0.5 / 8.0), t, DV.last()))
        cqh, cql = v3("Hh", S, 3), v3("Hl", S, 3)
        ckh, ckl = v3("Hh", S, 2, 3 * S), v3("Hl", S, 2, 3 * S)
        norm_parts(cq, 3, 384, S, G_CQ2, cqh, cql, AC.last())
        r = norm_parts(ckv, 2, 256, S, G_CKV2, ckh, ckl, AC.last())
        for h in range(0, 8, 2):
            cs = []
            for x in (h, h + 1):
                cs += [*cols(64 * x, 64), *cols(64 * x + 32, 32), *swapped(64 * x)]
            pan = panel("w_qi_2", 0, K3, cs)
            for x in range(2):
                gemm(pan, 128 * x, 128 * x + 128, cqh, cql, 3, ALLR, r, index_rope(Q[0:64, h + x, :]))
        sel = v3("Z", S, 4)
        best = m["O"][:, 0:8]
        ready = [DV.last(), AC.last()]
        score = tmp[:, 0, 0:S]
        def pick(i):
            ext = 128 * i + 128
            for h in range(8):
                bk = next_bank()
                ps = bank(bk)[:, 0:ext]
                t = PE.op(lambda e, ps=ps, h=h, i=i, ext=ext: e.matmul(ps, Q[0:64, h, 128 * i:ext], ki[:, 0:ext], start=True, stop=True), free[bk], ready)
                rl = m["P"][:, T * (h % 3):T * (h % 3) + ext]
                free[bk] = AC.chain(lambda e, ps=ps, rl=rl: e.activation(rl, ps, ACT.Relu), t, DV.last() if h < 3 else rel[h % 3])
                if h == 0:
                    rel = [None] * 3
                    DV.chain(lambda e, rl=rl, i=i: e.tensor_scalar(score[:, 0:ext], rl, k2[:, i, 0:1], 0.0, ALU.mult, ALU.add), AC.last())
                else:
                    DV.chain(lambda e, rl=rl, i=i, h=h: e.scalar_tensor_tensor(
                        out=score[:, 0:ext], in0=rl, scalar=k2[:, i, h:h + 1], in1=score[:, 0:ext], op0=ALU.mult, op1=ALU.add), AC.last())
                rel[h % 3] = DV.last()
            DV.chain(lambda e, ext=ext: e.tensor_tensor(score[:, 0:ext], score[:, 0:ext], causal(ext), ALU.add))
            for _ in range(16):
                DV.chain(lambda e, ext=ext: e.max(best, score[:, 0:ext]))
                DV.chain(lambda e, ext=ext: e.match_replace(score[:, 0:ext], best, score[:, 0:ext], TAKEN))
            DV.chain(lambda e, i=i, ext=ext: e.tensor_scalar(sel[:, i, 0:ext], score[:, 0:ext], -2e38, NEG, ALU.is_gt, ALU.mult))
        for i in range(1, 4):
            pick(i)
        for g in range(2):
            heads = list(range(8 * g, 8 * g + 8))
            mla_q("w_uq_2", 0, heads, 0, cqh, cql, ALLR, r, Q)
            pan = panel("w_uk_2", 0, K2, [64 * h + d for h in heads for d in range(64)])
            for c in range(4):
                gemm(pan, 128 * c, 128 * c + 128, ckh, ckl, 2, ALLR, r, lambda ps, a, b, t, c=c: two_heads(K, 2 * c, a, b)(ps, t))
            if g == 0:
                for h in range(8):
                    GP.op(lambda e, h=h: e.tensor_copy(K[64:96, h, :], kr), DV.last(), PE.last())
            gemm_tok("w_uv_2", 0, 2, [64 * h + d for h in heads for d in range(64)], ckh, ckl, ST, r, vcopy2)
            rot["banks"] = [7]
            attend(plain_units(lambda h: (Q[0:96, h, :], K[0:96, h, :]), lambda v, h: V[:, v, 64 * h:64 * h + 64], 96 ** -0.5,
                               lambda i, ext: causal(128) if i == 0 else sel[:, i, 0:ext]), finish2(4 * g), no_fill)
            rot["banks"] = list(range(8))
        out_proj("w_out_c_2", 0)
        add_norm(X2, M, S, MIX_POST + 8)

    def causal(ext):
        return con[:, MASKF + T - ext:MASKF + T]

    mixer_ab()
    mlp(0)
    ple(0)
    SP.dma(lambda e: e.dma_start(con[:, MASKF:MASKF + T], A["con"][:, MASKF:MASKF + T]), sems["in3"], DV.last())
    DV.wait((sems["in3"], 16))
    mixer_c()
    mlp(1)
    ple(1)
    SP.dma(lambda e: e.dma_start(out, X2), sems["out"], DV.last())
    SP.wait((sems["out"], 16))
    return dict(sp=SP, act=AC, dve=DV, pool=GP, pe=PE), panels


def tables():
    c = np.zeros((128, NCON), np.float32)
    c[:, IDENT:IDENT + 128] = np.eye(128)
    c[:, ONES:ONES + 128] = 1.0
    q, k = np.arange(128)[:, None], np.arange(128)[None, :]
    c[:, MASKF + 400:MASKF + 528] = np.where(k <= q, 0.0, NEG)
    c[:, MASKS:MASKS + 128] = np.where(k > q, 0.0, NEG)
    c[:, MASKS + 128:MASKS + 256] = np.where(k <= q, 0.0, NEG)
    pos = np.arange(T, dtype=np.float32)

    def angles(half):
        inv = (np.float32(10000.0) ** (-np.arange(half, dtype=np.float32) / np.float32(half))).astype(np.float32)
        return inv[:, None] * pos[None, :]
    a = angles(32)
    for h in range(0, 128, 64):
        c[h:h + 32, COS:COS + T] = c[h + 32:h + 64, COS:COS + T] = np.cos(a)
        c[h:h + 32, SIN:SIN + T] = np.sin(a)
        c[h + 32:h + 64, SIN:SIN + T] = -np.sin(a)
    a = angles(16)
    for h in (0, 64):
        c[h:h + 16, T2:T2 + T] = c[h + 16:h + 32, T2:T2 + T] = np.cos(a)
    c[96:112, T2:T2 + T] = -np.sin(a)
    c[112:128, T2:T2 + T] = np.sin(a)
    d = (np.arange(128)[:, None] + 384) - np.arange(512)[None, :]
    n = ((d >= 0) & (d <= 128)).astype(int) + ((d >= 0) & (d % 4 == 0)) + ((d >= 0) & (d % 16 == 0))
    maskd = np.where(n > 0, 8.0 * np.log(np.maximum(n, 1)), NEG).astype(np.float32)
    return c, maskd


_NAMES = ("w_in", "w_branch", "w_out", "w_uq", "w_ukv", "w_mlp_in_2", "w_mlp_out_2", "w_ple_proj_2", "w_ple_gate_2",
          "w_in_ab_2", "w_out_ab_2", "w_in_c_2", "w_uq_2", "w_qi_2", "w_uk_2", "w_uv_2", "w_out_c_2")


def kernel(**inputs):
    import concourse.bacc as _bacc
    from concourse.bass_utils import run_bass_kernel_spmd as _run

    a = {k: np.asarray(v) for k, v in inputs.items()}
    con, maskd = tables()
    x = np.concatenate([a["meta_tokens"], a["x"][0]], axis=0)
    xT = np.ascontiguousarray(x.reshape(T, 8, 128).transpose(2, 1, 0)).reshape(128, 8 * T)
    pT = np.ascontiguousarray(a["p_2"][:, 0].reshape(2, S, 2, 128).transpose(0, 3, 2, 1)).reshape(2, 128, 2 * S)
    sm = np.zeros((128, NSM), np.float32)

    def put(o, v):
        v = v.reshape(-1, 128).T
        sm[:, o:o + v.shape[1]] = v
    for o, n in ((NORM_G, "norm_g"), (G_CQ, "g_cq"), (G_CKV, "g_ckv"), (FINAL_G, "final_g"), (MIX_PRE, "g_mix_pre_2"),
                 (MIX_POST, "g_mix_post_2"), (MLP_PRE, "g_mlp_pre_2"), (MLP_POST, "g_mlp_post_2"),
                 (DIFF_SUB, "g_diff_sub_2"), (G_CQ2, "g_cq_2"), (G_CKV2, "g_ckv_2")):
        put(o, a[n])
    sm[0:8, B_F:B_F + 2] = a["b_f"].T
    sm[:, SINKS:SINKS + 16] = a["sinks"].reshape(1, 16)
    for i, n in enumerate(("diff_lq1_2", "diff_lk1_2", "diff_lq2_2", "diff_lk2_2")):
        sm[:, LAMS + 64 * i:LAMS + 64 * i + 64] = a[n].reshape(1, 64)

    nc = _bacc.Bacc("TRN2", target_bir_lowering=False, num_devices=1)
    A = {
        "x": nc.dram_tensor("in_x", (128, 8 * T), F, kind="ExternalInput").ap(),
        "con": nc.dram_tensor("in_con", (128, NCON), F, kind="ExternalInput").ap(),
        "sm": nc.dram_tensor("in_sm", (128, NSM), F, kind="ExternalInput").ap(),
        "p": nc.dram_tensor("in_p", (2, 128, 2 * S), F, kind="ExternalInput").ap(),
        "maskd": nc.dram_tensor("in_maskd", (128, S), F, kind="ExternalInput").ap(),
        "w": nc.dram_tensor("in_w", (WTOTAL,), F, kind="ExternalInput").ap(),
    }
    out = nc.dram_tensor("out_0", (128, 8, S), F, kind="ExternalOutput").ap()
    spec = program(nc, A, out)

    w = np.empty(WTOTAL, np.float32)
    mats = {n: a[n] for n in _NAMES}
    for n in ("w_uk_2", "w_uv_2"):
        mats[n] = mats[n].reshape(1, 256, 1024)
    o = 0
    for name, idx, kcs, cols in spec:
        mat = mats[name][idx]
        cs = np.asarray(cols)
        rows = mat[128 * kcs[0]:128 * kcs[-1] + 128]
        part = rows[:, cs[0]:cs[0] + len(cs)] if np.all(np.diff(cs) == 1) else rows[:, cs]
        n = 128 * len(kcs) * len(cs)
        w[o:o + n].reshape(128, len(kcs), len(cs))[:] = part.reshape(len(kcs), 128, len(cs)).transpose(1, 0, 2)
        o += n
    r = _run(nc, [{"in_x": xT, "in_con": con, "in_sm": sm, "in_p": pT, "in_maskd": maskd, "in_w": w}], core_ids=[0])
    y = r.results[0]["out_0"]
    return np.ascontiguousarray(y.reshape(128, 8, S).transpose(2, 1, 0)).reshape(1, S, D)
```

```python
import numpy as np
from contextlib import ExitStack

import concourse.bass as bass
from concourse import mybir

F = mybir.dt.float32
FR = mybir.dt.float32r
ALU = mybir.AluOpType
ACT = mybir.ActivationFunctionType
AX = mybir.AxisListType

D = 1024
NM = 16
S = 512
T = NM + S
EPS = 1e-6
NEG = -1e30
BIG = 3e38
TAKEN = -3e38
HALF = 264
PAN = 512
RAW = 5
WS = 4
WTOTAL = 128 * 389184
LAM_INIT = 0.8 - 0.6

NORM_G, G_CQ, G_CKV, FINAL_G = 0, 16, 22, 26
MIX_PRE, MIX_POST, MLP_PRE, MLP_POST = 34, 50, 66, 82
DIFF_SUB, G_CQ2, G_CKV2, B_F, SINKS = 98, 99, 102, 104, 106
NSM = 122

IDENT, ONES, MASKF, MASKS, COS, SIN, T2, NCON = 0, 128, 256, 784, 1040, 1568, 2096, 2624


class Queue:

    def __init__(self, sem):
        self.sem, self.n, self.list, self.waited = sem, 0, [], {}

    def wait(self, *tokens):
        for t in tokens:
            if t is None:
                continue
            if isinstance(t, list):
                self.wait(*t)
                continue
            sem, v = t
            if self.waited.get(id(sem), 0) < v:
                self.waited[id(sem)] = v
                self.list.append(("wait", sem, v))

    def op(self, make, *after, count=True):
        self.wait(*after)
        self.list.append(("op", make, count))
        self.n += count
        return self.last()

    def chain(self, make, *after):
        return self.op(make, self.last(), *after)

    def last(self):
        return (self.sem, self.n) if self.n else None

    def dma(self, make, sem, *after):
        self.wait(*after)
        self.list.append(("dma", make, sem))

    def play(self, eng):
        for kind, a, b in self.list:
            if kind == "wait":
                eng.wait_ge(a, b)
            elif kind == "dma":
                a(eng).then_inc(b, 16)
            else:
                ins = a(eng)
                if b:
                    ins.then_inc(self.sem, 1)


def program(nc, A, out):
    with ExitStack() as ctx:
        def sb(name, cols, dt=F):
            return ctx.enter_context(nc.sbuf_tensor(name, [128, cols], dt))

        def sem(name):
            return ctx.enter_context(nc.semaphore(name))

        m = {
            "X": sb("X", 8 * T), "Hh": sb("Hh", 8 * T, FR), "Hl": sb("Hl", 8 * T, FR),
            "M": sb("M", 8 * T), "Q": sb("Q", 8 * T), "K": sb("K", 8 * T), "V": sb("V", 5 * 512),
            "Yh": sb("Yh", 8 * T, FR), "Yl": sb("Yl", 8 * T, FR), "Z": sb("Z", 4 * T),
            "raw": sb("raw", RAW * PAN), "wh": sb("wh", WS * PAN, FR), "wl": sb("wl", WS * PAN, FR),
            "P": sb("P", 3 * T), "PT": sb("PT", 2 * 640), "O": sb("O", 512),
            "tmp": sb("tmp", 2 * T), "rs": sb("rs", T), "st": sb("st", 160),
            "con": sb("con", NCON), "sm": sb("sm", NSM), "k1": sb("k1", 4),
        }
        PP = [ctx.enter_context(nc.psum_tensor(f"pp{i}", [128, 1024], F)) for i in range(4)]
        sems = {n: sem(n) for n in ("pe", "act", "dve", "pool", "sp", "in0", "in1", "in2", "in3", "md", "aug0", "aug1", "aug2", "aug3", "pin0", "pin1", "lam", "out")}
        sems["w"] = [sem(f"w{i}") for i in range(RAW)]
        spec = emit(m, PP, sems, A, out, None)[1]
        queues, _ = emit(m, PP, sems, A, out, spec)
        block = ctx.enter_context(nc.Block())

        @block.sync
        def _(eng):
            queues["sp"].play(eng)

        @block.scalar
        def _(eng):
            queues["act"].play(eng)

        @block.vector
        def _(eng):
            queues["dve"].play(eng)

        @block.gpsimd
        def _(eng):
            queues["pool"].play(eng)

        @block.tensor
        def _(eng):
            queues["pe"].play(eng)
    return spec


def emit(m, PP, sems, A, out, spec):
    SP, AC, DV, GP, PE = (Queue(sems[n]) for n in ("sp", "act", "dve", "pool", "pe"))
    panels = []
    con, sm, k1, st = m["con"], m["sm"], m["k1"], m["st"]

    def bank(b):
        return PP[b // 2][:, 512 * (b % 2):512 * (b % 2) + 512]

    free = [None] * 8

    def v3(name, n, c, off=0):
        return m[name][:, off:off + n * c].rearrange("p (c n) -> p c n", c=c)

    done = []
    where = []
    off = 0
    for _, _, kcs, cols in spec or []:
        where.append((off, len(kcs) * len(cols)))
        off += 128 * len(kcs) * len(cols)
    assert not spec or off == WTOTAL, off // 128
    landed, split_at = {}, {}

    def fetch(j):
        if j >= len(where):
            return
        o, n = where[j]
        dst = m["raw"][:, (j % RAW) * PAN:(j % RAW) * PAN + n]
        src = A["w"][o:o + 128 * n].rearrange("(p n) -> p n", p=128)
        SP.dma(lambda e: e.dma_start(dst, src), sems["w"][j % RAW], split_at.get(j - RAW))
        landed[j] = (sems["w"][j % RAW], 16 * (j // RAW + 1))

    def split(j):
        if j >= len(where):
            return
        n = where[j][1]
        raw = m["raw"][:, (j % RAW) * PAN:(j % RAW) * PAN + n]
        hi = m["wh"][:, (j % WS) * PAN:(j % WS) * PAN + n]
        lo = m["wl"][:, (j % WS) * PAN:(j % WS) * PAN + n]
        used = done[j - WS] if j >= WS else None
        a = AC.op(lambda e: e.activation(hi, raw, ACT.Copy), landed[j], used)
        b = DV.op(lambda e: e.tensor_tensor(lo, raw, hi.bitcast(F), ALU.subtract), a, used)
        split_at[j] = [a, b]
        fetch(j + RAW)

    def panel(name, idx, kcs, cols):
        kcs, cols = list(kcs), list(cols)
        per = PAN // len(cols)
        assert per
        out = []
        for i in range(0, len(kcs), per):
            ks = kcs[i:i + per]
            panels.append((name, idx, ks, cols))
            out.append((range(i, i + len(ks)), len(panels) - 1))
        return out

    def use(part):
        ks, j = part
        while len(done) < j:
            done.append(PE.last())
        if where:
            if j == 0:
                for i in range(RAW):
                    fetch(i)
                for i in range(WS - 2):
                    split(i)
            split(j + WS - 2)
        n = len(panels[j][2]) * len(panels[j][3])
        o = (j % WS) * PAN
        hi, lo = (m[x][:, o:o + n].rearrange("p (k n) -> p k n", k=len(ks)) for x in ("wh", "wl"))
        return ks, hi, lo, split_at.get(j)

    NB = 5
    FREE, FILL = [0, 1, 2, 3, 4, 6, 7], [2, 3, 7]
    rot = {"banks": FREE, "n": 0}

    def next_bank():
        b = rot["banks"][rot["n"] % len(rot["banks"])]
        rot["n"] += 1
        return b

    def products(w, x, first, last, outs, *after):
        (wh, wl), (xh, xl) = w, x
        for n, (p, q) in enumerate(((wh, xh), (wh, xl), (wl, xh))):
            for ps, wc, xc in outs:
                t = PE.op(lambda e, ps=ps, p=p[:, wc], q=q[:, xc], n=n: e.matmul(
                    ps, p, q, start=first and n == 0, stop=last and n == 2), *after, count=n == 2)
        return t

    def gemm_steps(parts_, c0, c1, x, kc, ranges, ready, evac):
        bks = [next_bank() for _ in ranges]
        outs = [(bank(bk)[0:c1 - c0, 0:b - a], slice(c0, c1), slice(a, b)) for bk, (a, b) in zip(bks, ranges)]
        fr = [free[bk] for bk in bks]
        for part in parts_:
            ks, hi, lo, there = use(part)
            for k in ks:
                t = products((hi[:, k - ks[0], :], lo[:, k - ks[0], :]), x[k], k == 0, k == kc - 1, outs,
                             there, fr, ready[k] if isinstance(ready, dict) else ready)
            yield
        for bk, (a, b), (ps, _, _) in zip(bks, ranges, outs):
            free[bk] = evac(ps, a, b, t)

    def run(steps):
        for _ in steps:
            pass

    def gemm(*args):
        run(gemm_steps(*args))

    def gemm_tok(name, idx, kc, cols, x, tiles, ready, evac):
        bks = [next_bank() for _ in tiles]
        for part in panel(name, idx, range(kc), cols):
            ks, hi, lo, there = use(part)
            for (a, b), bk in zip(tiles, bks):
                for k in ks:
                    t = products(x[k], (hi[:, k - ks[0], :], lo[:, k - ks[0], :]), k == 0, k == kc - 1,
                                 [(bank(bk)[:, 0:len(cols)], slice(a, a + 128), slice(0, len(cols)))],
                                 there, ready[k] if isinstance(ready, dict) else ready, free[bk] if k == 0 else None)
        for n, ((a, b), bk) in enumerate(zip(tiles, bks)):
            free[bk] = evac(bank(bk)[0:b - a, 0:len(cols)], n, a, b, t)

    def parts(src, hi, lo, *after):
        a = AC.op(lambda e: e.activation(hi, src, ACT.Copy), *after)
        return DV.op(lambda e: e.tensor_tensor(lo, src, hi.bitcast(F), ALU.subtract), a, *after)

    def scaled_parts(src, g, hi, lo, *after):
        a = AC.op(lambda e: e.activation(hi, src, ACT.Copy, scale=g), *after)
        return DV.op(lambda e: e.scalar_tensor_tensor(out=lo, in0=src, scalar=g, in1=hi.bitcast(F), op0=ALU.mult, op1=ALU.subtract), a, *after)

    def both(h, l, n, c, off=0):
        return [(m[h][:, off + n * i:off + n * i + n], m[l][:, off + n * i:off + n * i + n]) for i in range(c)]

    tmp = v3("tmp", T, 2)
    ones = con[:, ONES:ONES + 128]
    ident = con[:, IDENT:IDENT + 128]
    sqs = v3("P", T, 3)
    norm = {}
    tu = [None, None]

    def norm_begin(tiles, nch):
        norm.update(tiles=tiles, nch=nch, c=0, free=[free[NB], DV.last(), PE.last()], pend=None)

    def norm_sums():
        if norm["pend"] is None:
            return
        c, sq, a = norm["pend"]
        norm["pend"] = None
        tiles = norm["tiles"]
        base = tiles[0][0]
        for n, (i, (p, q)) in enumerate(reversed(list(enumerate(tiles)))):
            t = PE.op(lambda e, n=n, i=i, p=p, q=q, last=c == norm["nch"] - 1: e.matmul(
                bank(NB)[0:q - p, i:i + 1], sq[:, p - base:q - base], ones[:, 0:1], start=c == 0 and n == 0,
                stop=last, skip_group_check=True), a, norm["free"] if c == 0 else None, count=n == len(tiles) - 1)
        norm["sq", c % 2] = t

    def norm_chunk(src, *after):
        norm_sums()
        c = norm["c"]
        norm["c"] += 1
        n = norm["tiles"][-1][1] - norm["tiles"][0][0]
        sq = sqs[:, c % 2, 0:n]
        a = AC.op(lambda e: e.activation(sq, src, ACT.Square), norm.get(("sq", c % 2)), norm["free"] if c < 2 else None, *after)
        norm["pend"] = (c, sq, a)

    def norm_end(width, rs, col):
        norm_sums()
        tiles = norm["tiles"]
        t = norm["sq", (norm["nch"] - 1) % 2]
        k = len(tiles)
        small = tiles[0][1] - tiles[0][0] < 128
        groups = ([(NM, 0, 1)] if small else []) + [(128, int(small), k)]
        base = tiles[0][0]
        for r, x, y in groups:
            a = AC.op(lambda e, r=r, x=x, y=y: e.activation(
                col[0:r, x:y], bank(NB)[0:r, x:y], ACT.Sqrt, bias=k1[0:r, 0:1], scale=1.0 / width), t, norm["free"])
        free[NB] = a
        for r, x, y in groups:
            d = DV.op(lambda e, r=r, x=x, y=y: e.reciprocal(col[0:r, x:y], col[0:r, x:y]), a)
        dg = [m["P"][0:q - p, 128 * i:128 * i + q - p] for i, (p, q) in enumerate(tiles)]
        for i, (p, q) in enumerate(tiles):
            g = DV.op(lambda e, i=i, r=q - p: e.tensor_scalar(dg[i], ident[0:r, 0:r], col[0:r, i:i + 1], None, ALU.mult), d, t)
        bks = [next_bank() for _ in groups]
        for i, (p, q) in enumerate(tiles):
            bk = bks[0 if i == 0 else -1]
            at = p - tiles[int(small) if i else 0][0]
            t = PE.op(lambda e, i=i, r=q - p, bk=bk, at=at: e.matmul(
                bank(bk)[:, at:at + r], ones[0:r, :], dg[i], start=True, stop=True), g, free[bk] if at == 0 else None)
        for (r, x, y), bk in zip(groups, bks):
            p, q = tiles[x][0] - base, tiles[y - 1][1] - base
            free[bk] = AC.op(lambda e, p=p, q=q, bk=bk: e.activation(rs[:, p:q], bank(bk)[:, 0:q - p], ACT.Copy), t)
        return AC.last()

    def normed_parts(xs, g, rs, outs, *after):
        ready = {}
        for c, x in enumerate(xs):
            a = DV.op(lambda e, c=c, x=x: e.scalar_tensor_tensor(
                out=x, in0=x, scalar=sm[:, g + c:g + c + 1], in1=rs, op0=ALU.mult, op1=ALU.mult), *after)
            ready[c] = parts(x, *outs[c], a)
        return ready

    units = {"n": 0}

    def attend(heads, finish, steps=(), rate=1.0):
        steps = iter(steps)
        due = {"n": 0.0}
        pend1, pend2, late = [], [], []
        now = [DV.last(), AC.last(), PE.last()]
        pfree, ptfree = [now] * 4, [now] * 2

        def fill():
            due["n"] += rate
            while due["n"] >= 1:
                due["n"] -= 1
                next(steps, None)

        def scores(u):
            n = units["n"]
            units["n"] += 1
            u["n"] = n
            qr, ext = u["qr"], u["ext"]
            single = len(u["qk"]) == 1
            u["p"], u["slots"], u["exps"] = [], [], []
            for x, (q, k) in enumerate(u["qk"]):
                slot = n % 3 if single else 2 * (n % 2) + x
                if ext <= 512:
                    bk = [n % 2 if single else x]
                    sc = bank(bk[0])[0:qr, 0:ext]
                    t = PE.op(lambda e, sc=sc, q=q, k=k: e.matmul(sc, q, k, start=True, stop=True), free[bk[0]], u["ready"])
                else:
                    bk, c0, cut = [0, 1], 1024 - ext, ext - 512
                    sc = PP[0][0:qr, c0:1024]
                    PE.op(lambda e, q=q, k=k: e.matmul(PP[0][0:qr, c0:512], q, k[:, 0:cut], start=True, stop=True), free[0], u["ready"])
                    t = PE.op(lambda e, q=q, k=k: e.matmul(PP[0][0:qr, 512:1024], q, k[:, cut:ext], start=True, stop=True), free[1])
                p = pbuf(slot)[0:qr, 0:ext]
                s = n % 32 if single else 2 * (n % 16) + x
                neg, tot = st[0:qr, s:s + 1], u["sums"][x]
                a = DV.op(lambda e, sc=sc, p=p, neg=neg: e.tensor_tensor_reduce(
                    p, sc, u["mask"], -u["scale"], u["init"], ALU.add, ALU.min, neg), t, pfree[slot])
                for b in bk:
                    free[b] = a
                u["exp"] = AC.op(lambda e, p=p, neg=neg, tot=tot: e.activation(
                    p, p, ACT.Exp, bias=neg, scale=-1.0, accum_out=tot), a)
                u["p"].append(p)
                u["slots"].append(slot)
            if "sink" in u:
                snk, e1 = u["sink"]
                u["e1"] = AC.op(lambda e, neg=neg: e.activation(e1, snk, ACT.Exp, bias=neg, scale=1.0))

        def turn(u):
            qr = u["qr"]
            if "mix" in u:
                u["exp"] = u["mix"](u)
            p = u["p"][0]
            whole = [c for c in u["chunks"] if c[1] == 128]
            small = [c for c in u["chunks"] if c[1] != 128]
            slot = u["n"] % 2
            pt = m["PT"][:, slot * 640:slot * 640 + 640]
            u["pt"], u["cp"] = [], []
            for o, rows, v in small:
                if qr == 128:
                    t = PE.op(lambda e, o=o: e.transpose(bank(5)[:, 0:128], p[:, o:o + 128], ident), free[5], u["exp"])
                else:
                    t = PE.op(lambda e, o=o, rows=rows: e.matmul(bank(5)[0:rows, 0:qr], p[:, o:o + rows], ident[0:qr, 0:qr], start=True, stop=True), free[5], u["exp"])
                free[5] = DV.op(lambda e, rows=rows: e.tensor_copy(pt[0:rows, 512:512 + qr], bank(5)[0:rows, 0:qr]), t, ptfree[slot])
                u["pt"].append((pt[0:rows, 512:512 + qr], v))
                u["cp"].append(free[5])
            if whole:
                for x, (o, rows, v) in enumerate(whole):
                    t = PE.op(lambda e, o=o, x=x: e.transpose(bank(4)[:, 128 * x:128 * x + 128], p[:, o:o + 128], ident), free[4] if x == 0 else None, u["exp"])
                    u["pt"].append((pt[:, 128 * x:128 * x + 128], v))
                w = 128 * len(whole)
                if u["n"] % 2:
                    free[4] = AC.op(lambda e: e.activation(pt[:, 0:w], bank(4)[:, 0:w], ACT.Copy), t, ptfree[slot])
                else:
                    free[4] = DV.op(lambda e: e.tensor_copy(pt[:, 0:w], bank(4)[:, 0:w]), t, ptfree[slot])
                u["cp"].append(free[4])
            for x in u["slots"]:
                pfree[x] = t

        def product(u):
            qr = u["qr"]
            o = bank(6)[0:qr, u["o"]:u["o"] + u["dv"]]
            n = len(u["pt"])
            for x, (p, v) in enumerate(u["pt"]):
                t = PE.op(lambda e, x=x, p=p, v=v: e.matmul(o, p, v, start=x == 0, stop=x == n - 1),
                          u["cp"], free[6] if u["o"] == 0 else None, count=x == n - 1)
            ptfree[u["n"] % 2] = t
            if "end" in u:
                late.append(finish(u, t))

        rot["banks"] = FILL
        for u in heads + [None, None]:
            if u:
                scores(u)
                pend1.append(u)
                fill()
            if len(pend1) > (1 if u else 0):
                turn(pend1[0])
                pend2.append(pend1.pop(0))
            if len(pend2) > (1 if u else 0):
                product(pend2.pop(0))
            if late and next(late[0], "end") == "end":
                late.pop(0)
        for g in late:
            run(g)
        run(steps)
        rot["banks"] = FREE

    def pbuf(slot):
        return m["P"][:, slot * T:(slot + 1) * T] if slot < 3 else m["Z"][:, 0:T]

    turned = {"o": None}

    def turn_out(qr, *after):
        for c in range(4):
            t = PE.op(lambda e, c=c: e.transpose(bank(5)[:, 128 * c:128 * c + qr], m["O"][0:qr, 128 * c:128 * c + 128], ident[0:qr, 0:qr]),
                      free[5] if c == 0 else None, *after, count=c == 3)
        turned["o"] = t
        return t

    def divided(u, t, sums):
        qr = u["qr"]
        o = m["O"][0:qr, :]
        DV.chain(lambda e: e.reciprocal(sums, sums), t)
        free[6] = DV.chain(lambda e: e.tensor_tensor(
            o.rearrange("p (h d) -> p h d", h=8), bank(6)[0:qr, :].rearrange("p (h d) -> p h d", h=8),
            sums.unsqueeze(2).to_broadcast([qr, 8, 64]), ALU.mult), turned["o"])
        return free[6]

    X = v3("X", T, 8)
    SP.dma(lambda e: e.dma_start(m["X"][:, :], A["x"]), sems["in0"])
    AC.dma(lambda e: e.dma_start(con[:, :], A["con"]), sems["in1"])
    AC.dma(lambda e: e.dma_start(sm[:, :], A["sm"]), sems["in2"])
    loaded = [(sems["in0"], 16), (sems["in1"], 16), (sems["in2"], 16)]
    DV.chain(lambda e: e.memset(k1[:, 0:1], EPS))
    DV.chain(lambda e: e.memset(k1[:, 1:2], 1.0))
    DV.chain(lambda e: e.memset(k1[:, 2:3], BIG))
    for q in (AC, DV, PE):
        q.wait(loaded, DV.last())

    maskF = con[:, MASKF:MASKF + T]
    maskS = con[:, MASKS:MASKS + 256]
    cos, sin, t2 = (con[:, o:o + T] for o in (COS, SIN, T2))
    big = k1[:, 2:3]

    rs = m["rs"]
    rs2 = m["P"][:, 2 * T:3 * T]
    col, col2 = st[:, 64:72], st[:, 72:80]

    def scaled(dst, ps, r, *after):
        if r is None:
            return AC.op(lambda e: e.activation(dst, ps, ACT.Copy), *after)
        return DV.op(lambda e: e.tensor_tensor(dst, ps, r, ALU.mult), *after)

    def rope64(ps, dst, a, b, t, *after):
        p, q = (tmp[:, i, 0:b - a] for i in range(2))
        last = [t, DV.last(), tu, *after]
        for r in range(4):
            s = r ^ 1
            DV.op(lambda e, r=r, s=s: e.tensor_tensor(
                p[32 * r:32 * r + 32], ps[32 * s:32 * s + 32, :], sin[32 * s:32 * s + 32, a:b], ALU.mult), last if r == 0 else None)
        f = DV.op(lambda e: e.tensor_tensor(q, ps, cos[:, a:b], ALU.mult))
        DV.chain(lambda e: e.tensor_tensor(p, p, q, ALU.add))
        DV.chain(lambda e: e.tensor_tensor(dst, p, rs[:, a:b], ALU.mult))
        return f

    def rope32(ps, row, dst, a, b, t, r, *after):
        p, q = (tmp[row:row + 32, i, 0:b - a] for i in range(2))
        DV.chain(lambda e: e.tensor_tensor(p, ps[96:128, :], t2[96:128, a:b], ALU.mult), t, tu, *after)
        f = DV.op(lambda e: e.tensor_tensor(q, ps[row:row + 32, :], t2[row:row + 32, a:b], ALU.mult))
        if r is None:
            DV.chain(lambda e: e.tensor_tensor(dst, p, q, ALU.add))
        else:
            DV.chain(lambda e: e.tensor_tensor(p, p, q, ALU.add))
            DV.chain(lambda e: e.tensor_tensor(dst, p, r[row:row + 32, a:b], ALU.mult))
        return f

    K8, K4, K3, K2 = range(8), range(4), range(3), range(2)

    def cols(a, n):
        return range(a, a + n)

    def swapped(a):
        return [*range(a + 16, a + 32), *range(a, a + 16)]

    def mla_q(name, l, heads, x, ranges, ready, Q, *after):
        for i, h in enumerate(heads):
            def evac(ps, a, b, t, i=i):
                x = AC.op(lambda e: e.activation(Q[0:64, i, a:b], ps[0:64, :], ACT.Copy), t, *after)
                return [x, rope32(ps, 64, Q[64:96, i, a:b], a, b, t, None, *after)]
            yield from gemm_steps(panel(name, l, K3, [*cols(96 * h, 64), *cols(96 * h + 64, 32), *swapped(96 * h + 64)]),
                                  0, 128, x, 3, ranges, ready, evac)

    def two_heads(dst, h, r, *after):
        def evac(ps, a, b, t):
            if r is None:
                x = AC.op(lambda e: e.activation(dst[0:64, h, a:b], ps[0:64, :], ACT.Copy), t, *after)
                return [x, DV.op(lambda e: e.tensor_copy(dst[0:64, h + 1, a:b], ps[64:128, :]), t, *after)]
            DV.op(lambda e: e.tensor_tensor(dst[0:64, h, a:b], ps[0:64, :], r[0:64, a:b], ALU.mult), t, *after)
            return DV.op(lambda e: e.tensor_tensor(dst[0:64, h + 1, a:b], ps[64:128, :], r[64:128, a:b], ALU.mult))
        return evac

    TOKR = [(0, HALF), (HALF, T)]
    TILES = [(0, NM)] + [(NM + 128 * i, NM + 128 * i + 128) for i in range(4)]

    def all_of():
        return [q.last() for q in (AC, DV, GP, PE)]

    Hx = both("Hh", "Hl", T, 8)

    def first_layer(l, hr):
        QR = TOKR if l == 0 else [(NM, T)]
        Q, K, M, Z = v3("Q", T, 8), v3("K", T, 8), v3("M", T, 8), v3("Z", T, 4)
        V = v3("V", 512, 5)
        Yv = [[x[:, 4 * T * i:4 * T * i + 4 * T].rearrange("p (c n) -> p c n", c=4) for x in (m["Yh"], m["Yl"])] for i in range(2)]
        Yx = [both("Yh", "Yl", T, 4, 4 * T * i) for i in range(2)]

        def win(cs, ranges, evac):
            return gemm_steps(panel("w_in", l, K8, cs), 0, 128, Hx, 8, ranges, hr, evac)

        def zgate(c0, c):
            def evac(ps, a, b, t):
                zz, g = tmp[:, 0, 0:b - a], tmp[:, 1, 0:b - a]
                f = DV.chain(lambda e: e.tensor_tensor(zz, ps, rs[:, a:b], ALU.mult), t, tu)
                x = AC.op(lambda e: e.activation(g, zz, ACT.Tanh, scale=0.5), f)
                DV.op(lambda e: e.scalar_tensor_tensor(out=Z[:, c, a:b], in0=g, scalar=1.0, in1=zz, op0=ALU.add, op1=ALU.mult), x)
                return f
            run(win(cols(c0 + 128 * c, 128), QR, evac))

        def merge(n, ready, slots, then=None):
            used = [all_of()] * len(slots)
            gated = {}
            Mready = all_of()

            def gate(c):
                s = c % len(slots)

                def evac(ps, a, b, t):
                    tg = slots[s][:, a:b]
                    f = DV.op(lambda e: e.tensor_tensor(tg, ps, rs[:, a:b], ALU.mult), t, used[s])
                    gated[c] = AC.op(lambda e: e.activation(tg, tg, ACT.Tanh, scale=0.5), f)
                    return f
                return win(cols(4520 + 1024 * n + 128 * c, 128), QR, evac)

            def proj(c):
                s = c % len(slots)

                def evac(ps, a, b, t):
                    tg = slots[s][:, a:b]
                    dst = M[:, c, a:b] if n == 0 else tg
                    f = DV.op(lambda e: e.scalar_tensor_tensor(
                        out=dst, in0=tg, scalar=1.0, in1=ps, op0=ALU.add, op1=ALU.mult), t, gated[c], Mready)
                    if n:
                        DV.chain(lambda e: e.tensor_tensor(M[:, c, a:b], M[:, c, a:b], tg, ALU.add))
                    used[s] = DV.last()
                    if then and b == T:
                        then(c)
                    return f
                return gemm_steps(panel("w_branch", (l, n), K4, cols(128 * c, 128)), 0, 128, Yx[n % 2], 4, QR, ready, evac)

            ahead = len(slots) - 1
            if ahead:
                yield from gate(0)
            for c in range(8):
                if c + ahead < 8:
                    yield from gate(c + ahead)
                yield from proj(c)

        def finish_to(n):
            def finish(u, t):
                qr, a = u["qr"], u["tok"]
                if "sink" in u:
                    DV.chain(lambda e: e.tensor_tensor(u["all"], u["all"], u["alle"], ALU.add), t, u["e1"])
                r = divided(u, t, u["all"])
                yield
                x = turn_out(qr, r)
                q = tmp[:, 0, 0:4 * qr].rearrange("p (c n) -> p c n", c=4)
                free[5] = DV.chain(lambda e: e.tensor_tensor(q, bank(5)[:, :].rearrange("p (c n) -> p c n", c=4)[:, :, 0:qr],
                                                             Z[:, :, a:a + qr], ALU.mult), x, tu)
                parts(q, *(y[:, :, a:a + qr] for y in Yv[n % 2]), free[5])
                tu[0] = AC.last()
            return finish

        def units_of(qk, vof, scale, sinks=None, window=False):
            us = []
            ready = all_of()
            for i in range(-1 if l == 0 else 0, 4):
                qr, a = (NM, 0) if i < 0 else (128, NM + 128 * i)
                if i < 0:
                    k0, ext = 0, NM
                    mk = maskF[0:NM, 400:400 + NM] if not window else maskS[0:NM, 128:128 + NM]
                elif window:
                    k0 = 0 if i == 0 else NM + 128 * (i - 1)
                    ext = a + 128 - k0
                    mk = maskS[:, 256 - ext:256]
                else:
                    k0, ext = 0, a + 128
                    mk = maskF[:, T - ext:T]
                chunks = [(x - k0, y - x, v) for v, (x, y) in enumerate(TILES) if x >= k0 and y <= k0 + ext]
                o = 32 + 16 * (i % 2)
                sums, e1 = st[0:qr, o:o + 8], st[0:qr, o + 8:o + 16]
                for h in range(8):
                    q, k = qk(h)
                    u = dict(qr=qr, ext=ext, tok=a, mask=mk, scale=scale, qk=[(q[:, a:a + qr], k[:, k0:k0 + ext])],
                             chunks=[(o, r, vof(v, h)[0:r]) for o, r, v in chunks], dv=64, o=64 * h,
                             sums=[sums[:, h:h + 1]], all=sums, alle=e1, init=big[0:qr], ready=ready)
                    if sinks is not None:
                        u["init"] = negs[0:qr, h:h + 1]
                        u["sink"] = (sm[0:qr, sinks + h:sinks + h + 1], e1[:, h:h + 1])
                    if h == 7:
                        u["end"] = True
                    us.append(u)
            return us

        cum, w1, w2 = (m["Z"][0:8, T * i:T * i + T] for i in range(3))
        before = all_of()

        def fgate(ps, a, b, t):
            if a == 0:
                norm_end(D, rs, col)
            f = DV.op(lambda e: e.tensor_tensor(cum[:, a:b], ps[0:8], rs[0:8, a:b], ALU.mult), t, AC.last(), before)
            DV.chain(lambda e: e.tensor_scalar(cum[:, a:b], cum[:, a:b], sm[0:8, B_F + l:B_F + l + 1], None, ALU.add))
            return f
        run(win([*cols(1536, 8)] * 16, TOKR, fgate))
        AC.op(lambda e: e.activation(w1, cum, ACT.Abs), DV.last())
        AC.chain(lambda e: e.activation(w1, w1, ACT.Exp, scale=-1.0))
        AC.chain(lambda e: e.activation(w1, w1, ACT.Ln, bias=k1[0:8, 1:2], scale=1.0))
        DV.chain(lambda e: e.scalar_tensor_tensor(out=w2, in0=cum, scalar=0.0, in1=w1, op0=ALU.min, op1=ALU.subtract), AC.last())
        DV.chain(lambda e: e.memset(w1, 1.0))
        DV.chain(lambda e: e.tensor_tensor_scan(cum, w1, w2, 0.0, ALU.mult, ALU.add))
        DV.chain(lambda e: e.tensor_scalar(w1, cum, 8.0, None, ALU.mult))
        f = DV.op(lambda e: e.tensor_scalar(w2, cum, -8.0, None, ALU.mult))
        DV.op(lambda e: e.memset(Q[64:66, :, :], 1.0), before)
        r = DV.op(lambda e: e.memset(K[64:66, :, :], 1.0))
        for h in range(8):
            AC.dma(lambda e, h=h: e.dma_start(Q[64:65, h, :], w1[h:h + 1, :]), sems[f"aug{2 * l}"], f, r)
            AC.dma(lambda e, h=h: e.dma_start(K[65:66, h, :], w2[h:h + 1, :]), sems[f"aug{2 * l + 1}"])
        for dst, c0, rng in ((Q, 0, QR), (K, 512, TOKR)):
            for c in range(4):
                run(win(cols(c0 + 128 * c, 128), rng, two_heads(dst, 2 * c, rs, before)))

        def vcopy(scale, w=512):
            def evac(ps, n, a, b, t):
                return AC.op(lambda e: e.activation(V[0:b - a, n, 0:w], ps, ACT.Copy, scale=scale[0:b - a, n:n + 1] if scale is not None else 1.0), t, before)
            return evac
        gemm_tok("w_in", l, 8, cols(1024, 512), Hx, TILES, hr, vcopy(col))
        for q in (AC, DV, PE):
            q.wait((sems[f"aug{2 * l}"], 8 * 16), (sems[f"aug{2 * l + 1}"], 8 * 16))
        for c in range(4):
            zgate(1544, c)

        B0 = 2056
        cq, ckv = ([M[:, c, :] for c in cs] for cs in (range(3), range(3, 5)))
        kr = M[64:96, 5, :]
        before = all_of()

        def latent():
            for c in range(5):
                yield from win(cols(B0 + 128 * c, 128), TOKR, lambda ps, a, b, t, c=c: scaled(M[:, c, a:b], ps, rs[:, a:b], t, before))
            c0 = B0 + 640
            yield from win([*cols(c0, 32), *swapped(c0)] * 2, TOKR, lambda ps, a, b, t: rope32(ps, 64, kr[:, a:b], a, b, t, rs, before))
        attend(units_of(lambda h: (Q[0:66, h, :], K[0:66, h, :]), lambda v, h: V[:, v, 64 * h:64 * h + 64], 0.125), finish_to(0), latent(), 0.5)
        y0 = DV.last()

        before = all_of()
        for h in range(8):
            GP.op(lambda e, h=h: e.tensor_copy(K[64:96, h, :], kr), before)
        half = Yx[1]
        cqx, ckx = [half[2], half[3], half[0]], half[:2]
        norm_begin(TILES, 2)
        for c in range(2):
            norm_chunk(ckv[c], before)
        zgate(B0 + 672, 0)
        e = norm_end(256, rs2, col2)
        kvr = normed_parts(ckv, G_CKV + 2 * l, rs2, ckx, e, before)
        norm_begin(TILES, 3)
        for c in range(3):
            norm_chunk(cq[c], before)
        zgate(B0 + 672, 1)
        e = norm_end(384, rs2, col2)
        qr_ = normed_parts(cq[:2], G_CQ + 3 * l, rs2, cqx[:2], e)
        for c in range(2, 4):
            zgate(B0 + 672, c)
        for c in range(4):
            run(gemm_steps(panel("w_ukv", l, K2, [128 * h + d for h in range(2 * c, 2 * c + 2) for d in range(64)]),
                           0, 128, ckx, 2, TOKR, kvr, two_heads(K, 2 * c, None, before)))
        gemm_tok("w_ukv", l, 2, [128 * h + 64 + d for h in range(8) for d in range(64)], ckx, TILES, kvr, vcopy(None))
        qr_[2] = normed_parts(cq[2:], G_CQ + 3 * l + 2, rs2, cqx[2:], e, PE.last())[0]
        run(mla_q("w_uq", l, range(8), cqx, QR, qr_, Q, before))
        attend(units_of(lambda h: (Q[0:96, h, :], K[0:96, h, :]), lambda v, h: V[:, v, 64 * h:64 * h + 64], 96 ** -0.5),
               finish_to(1), merge(0, y0, [tmp[:, 1, :]]), 24 / (40 if l == 0 else 32))
        y1 = DV.last()

        C0 = 3240
        before = all_of()
        for c in range(4):
            run(win([*cols(C0 + 64 * c, 64), *cols(C0 + 64 * (c + 4), 64)], QR,
                    lambda ps, a, b, t, c=c: rope64(ps, Q[:, c, a:b], a, b, t, before)))
        run(win(cols(C0 + 512, 128), TOKR, lambda ps, a, b, t: rope64(ps, K[:, 0, a:b], a, b, t, before)))
        gemm_tok("w_in", l, 8, cols(C0 + 640, 128), Hx, TILES, hr, vcopy(col, 128))
        for c in range(4):
            zgate(C0 + 768, c)
        negs = st[:, 100:108]
        DV.op(lambda e: e.tensor_scalar(negs, sm[:, SINKS + 8 * l:SINKS + 8 * l + 8], -1.0, None, ALU.mult))
        attend(units_of(lambda h: (Q[64 * (h // 4):64 * (h // 4) + 64, h % 4, :], K[64 * (h // 4):64 * (h // 4) + 64, 0, :]),
                        lambda v, h: V[:, v, 64 * (h // 4):64 * (h // 4) + 64], 0.125, SINKS + 8 * l, True),
               finish_to(2), merge(1, y1, [tmp[:, 1, :]]), 24 / (40 if l == 0 else 32))
        before = all_of()
        a0 = QR[0][0]
        mr = {}
        Mx = Yx[1] + Yx[0]

        def part(c):
            mr[c] = parts(M[:, c, a0:T], *(x[:, a0:T] for x in Mx[c]), DV.last(), PE.last() if c >= 4 else before)
        run(merge(2, DV.last(), [m["P"][:, 0:T], m["P"][:, T:2 * T]], lambda c: part(c) if c < 4 else None))
        for c in range(4, 8):
            part(c)

        norm_begin(TILES if l == 0 else TILES[1:], 8)
        before = PE.last()
        nr = {}
        for c in range(8):
            def evac(ps, a, b, t, c=c):
                f = DV.op(lambda e: e.scalar_tensor_tensor(
                    out=X[:, c, a:b], in0=ps, scalar=0.25, in1=X[:, c, a:b], op0=ALU.mult, op1=ALU.add), t)
                if b == T:
                    norm_chunk(X[:, c, a0:T], f)
                    if l == 0:
                        g = NORM_G + 8 + c
                        nr[c] = scaled_parts(X[:, c, :], sm[:, g:g + 1], *Hx[c], f, before)
                return f
            run(gemm_steps(panel("w_out", l, K8, cols(128 * c, 128)), 0, 128, Mx, 8, QR, mr, evac))
        return nr

    norm_begin(TILES, 8)
    hr = {}
    for c in range(8):
        norm_chunk(X[:, c, :])
        hr[c] = scaled_parts(X[:, c, :], sm[:, NORM_G + c:NORM_G + c + 1], *Hx[c])
    for l in range(2):
        hr = first_layer(l, hr)

    X2 = X[:, :, NM:T]
    ALLR = [(0, S)]
    ST = [(128 * i, 128 * i + 128) for i in range(4)]
    Hx, Yx = both("Hh", "Hl", S, 8), both("Yh", "Yl", S, 8)
    Yh, Yl = v3("Yh", S, 8), v3("Yl", S, 8)
    Q, K, M = v3("Q", S, 8), v3("K", S, 8), v3("M", S, 8)
    V = v3("V", 512, 4)
    spare = m["V"][:, 4 * 512:5 * 512]
    rsS, rs2S = rs[:, 0:S], rs2[:, 0:S]

    def mult_parts(x, g, out, *after):
        norm_chunk(x, *after)
        return scaled_parts(x, sm[:, g:g + 1], *out, *after)

    def first_half(name, n, dst, before, ready):
        for c in range(8):
            yield from gemm_steps(panel(name, 0, K4, cols(128 * c, 128)), 0, 128, Yx, 4, ALLR, ready,
                                  lambda ps, a, b, t, c=c: AC.op(lambda e: e.activation(dst[:, c, :], ps, ACT.Copy), t, before))

    def second_half(name, dst, ready):
        norm_begin(ST, 8)
        for c in range(8):
            def evac(ps, a, b, t, c=c):
                f = DV.op(lambda e: e.tensor_tensor(dst[:, c, :], ps, dst[:, c, :], ALU.add), t, AC.last() if c == 0 else None)
                norm_chunk(dst[:, c, :], f)
                return f
            run(gemm_steps(panel(name, 0, range(4, 8), cols(128 * c, 128)), 0, 128, Yx[4:], 4, ALLR, ready, evac))

    def add_normed(y, g, then):
        for c in range(8):
            DV.op(lambda e, c=c: e.scalar_tensor_tensor(
                out=y[:, c, :], in0=y[:, c, :], scalar=sm[:, g + c:g + c + 1], in1=rsS, op0=ALU.mult, op1=ALU.mult), AC.last() if c == 0 else None)
            f = DV.chain(lambda e, c=c: e.tensor_tensor(X2[:, c, :], X2[:, c, :], y[:, c, :], ALU.add))
            then(c, f)

    def mix_end(y, i):
        norm_end(D, rsS, col)
        norm_begin(ST, 8)
        before = PE.last()
        ready = {}

        def then(c, f):
            ready[c] = mult_parts(X2[:, c, :], MLP_PRE + 8 * i + c, Hx[c], f, before)
        add_normed(y, MIX_POST + 8 * i, then)
        return ready

    def mlp(i, hr):
        pz = v3("Z", S, 2)
        AC.dma(lambda e: e.dma_start(m["Z"][:, 0:2 * S], A["p"][i]), sems[f"pin{i}"], all_of())
        start = all_of()
        for f in range(4):
            before = PE.last()
            ready = {}
            for c in range(8):
                def evac(ps, a, b, t, c=c):
                    if f == 0 and c == 0:
                        norm_end(D, rsS, col)
                    q = tmp[:, c % 2, 0:S]
                    x = DV.op(lambda e: e.scalar_tensor_tensor(out=q, in0=ps, scalar=0.0, in1=rsS, op0=ALU.max, op1=ALU.mult), t, AC.last() if f == 0 and c < 2 else None, tu)
                    AC.op(lambda e: e.activation(Yx[c][0], q, ACT.Square), x, before)
                    a = AC.op(lambda e: e.activation(q, q, ACT.Square))
                    ready[c] = DV.op(lambda e: e.tensor_tensor(Yx[c][1], q, Yx[c][0].bitcast(F), ALU.subtract), a)
                    return x
                run(gemm_steps(panel("w_mlp_in_2", i, K8, cols(1024 * f + 128 * c, 128)), 0, 128, Hx, 8, ALLR, hr, evac))
            if f == 3:
                norm_begin(ST, 8)
                px = Hx[6:]
                pr = {c: parts(pz[:, c, :], *px[c], (sems[f"pin{i}"], 16), PE.last()) for c in range(2)}
            for c in range(8):
                def add(ps, a, b, t, c=c):
                    if f == 0:
                        return AC.op(lambda e: e.activation(M[:, c, :], ps, ACT.Copy), t, start)
                    x = DV.op(lambda e: e.tensor_tensor(M[:, c, :], ps, M[:, c, :], ALU.add), t, DV.last(), AC.last() if f == 1 and c == 0 else None)
                    if f == 3:
                        norm_chunk(M[:, c, :], x)
                    return x
                run(gemm_steps(panel("w_mlp_out_2", i, range(8 * f, 8 * f + 8), cols(128 * c, 128)), 0, 128, Yx, 8, ALLR, ready, add))

        def project(c):
            run(gemm_steps(panel("w_ple_proj_2", i, K2, cols(128 * c, 128)), 0, 128, px, 2, ALLR, pr,
                           lambda ps, a, b, t: AC.op(lambda e: e.activation(Q[:, c, :], ps, ACT.Copy), t, start)))
        project(0)
        project(1)
        norm_end(D, rsS, col)
        before = PE.last()
        ready = {}

        def then(c, f):
            if c < 6:
                project(c + 2)
            ready[c] = parts(X2[:, c, :], *Hx[c], f, PE.last() if c >= 6 else before)
        add_normed(M, MLP_POST + 8 * i, then)
        return ready

    def ple(i, hr):
        norm_begin(ST, 8)
        before = all_of()
        ready = {}
        for c in range(8):
            tg = tmp[:, c % 2, 0:S]

            def evac(ps, a, b, t, c=c, tg=tg):
                x = AC.op(lambda e: e.activation(tg, ps, ACT.Tanh, scale=0.5), t, DV.last() if c > 1 else before)
                DV.op(lambda e: e.scalar_tensor_tensor(out=tg, in0=tg, scalar=1.0, in1=Q[:, c, :], op0=ALU.add, op1=ALU.mult), x)
                f = DV.chain(lambda e: e.scalar_tensor_tensor(
                    out=X2[:, c, :], in0=tg, scalar=0.5, in1=X2[:, c, :], op0=ALU.mult, op1=ALU.add))
                if i == 0:
                    ready[c] = mult_parts(X2[:, c, :], MIX_PRE + 8 + c, Yx[c], f, before)
                else:
                    SP.dma(lambda e: e.dma_start(out[:, c, :], X2[:, c, :]), sems["out"], f)
                return x
            run(gemm_steps(panel("w_ple_gate_2", i, K8, cols(128 * c, 128)), 0, 128, Hx, 8, ALLR, hr, evac))
        return ready

    def finish2(y0):
        def finish(u, t):
            a = u["tok"]
            r = divided(u, t, u["all"])
            yield
            x = turn_out(128, r)
            src = bank(5)[:, :].rearrange("p (c n) -> p c n", c=4)
            free[5] = parts(src, Yh[:, y0:y0 + 4, a:a + 128], Yl[:, y0:y0 + 4, a:a + 128], x)
        return finish

    def plain_units(qk, vof, scale, mask):
        us = []
        ready = all_of()
        for i in range(4):
            ext = 128 * i + 128
            sums = st[:, 32 + 16 * (i % 2):32 + 16 * (i % 2) + 8]
            for h in range(8):
                q, k = qk(h)
                u = dict(qr=128, ext=ext, tok=128 * i, mask=mask(i, ext), scale=scale, qk=[(q[:, 128 * i:ext], k[:, 0:ext])],
                         chunks=[(128 * v, 128, vof(v, h)) for v in range(i + 1)], dv=64, o=64 * h,
                         sums=[sums[:, h:h + 1]], all=sums, init=big, ready=ready)
                if h == 7:
                    u["end"] = True
                us.append(u)
        return us

    def vcopy2(scale, *after):
        def evac(ps, n, a, b, t):
            return AC.op(lambda e: e.activation(V[:, n, :], ps, ACT.Copy, scale=scale[:, n:n + 1] if scale is not None else 1.0), t, *after)
        return evac

    def mixer_ab(hr):
        before = all_of()
        lam = m["Z"][:, 2 * T:2 * T + 256]
        AC.dma(lambda e: e.dma_start(lam, A["lam"]), sems["lam"], before)
        AC.dma(lambda e: e.dma_start(spare, A["maskd"]), sems["md"])

        def rotary(dst, o, c, c0):
            def evac(ps, a, b, t):
                if (c0, c) == (0, 0):
                    norm_end(D, rsS, col)
                return rope64(ps, dst[:, o + c, :], a, b, t, AC.last() if (c0, c) == (0, 0) else None, before)
            yield from gemm_steps(panel("w_in_ab_2", 0, K8, cols(c0 + 128 * c, 128)), 0, 128, Hx, 8, ALLR, hr, evac)

        for dst, c0 in ((Q, 0), (K, 512)):
            for c in range(4):
                run(rotary(dst, 0, c, c0))
        gemm_tok("w_in_ab_2", 0, 8, cols(1024, 512), Hx, ST, hr, vcopy2(col, before))
        la = [lam[:, 64 * i:64 * i + 64] for i in range(4)]
        e2 = k1[:, 3:4]
        dots = st[:, 108:110]
        DV.wait((sems["lam"], 16))
        for x in range(2):
            DV.chain(lambda e, x=x: e.tensor_tensor_reduce(la[2 * x], la[2 * x], la[2 * x + 1], 1.0, 0.0, ALU.mult, ALU.add, dots[:, x:x + 1]))
        AC.op(lambda e: e.activation(dots, dots, ACT.Exp), DV.last())
        DV.op(lambda e: e.scalar_tensor_tensor(out=e2, in0=dots[:, 1:2], scalar=-LAM_INIT, in1=dots[:, 0:1], op0=ALU.add, op1=ALU.subtract), AC.last())

        def mix(u):
            s = u["pairsum"]
            p1, p2 = u["p"]
            DV.op(lambda e: e.reciprocal(s, s), u["exp"])
            DV.chain(lambda e: e.tensor_scalar(p2, p2, s[:, 1:2], e2, ALU.mult, ALU.mult))
            return DV.chain(lambda e: e.scalar_tensor_tensor(out=p1, in0=p1, scalar=s[:, 0:1], in1=p2, op0=ALU.mult, op1=ALU.add))

        def finish(u, t):
            a = u["tok"]
            o = m["O"][:, :]
            free[6] = f = AC.op(lambda e: e.activation(o, bank(6), ACT.Copy), t, turned["o"])
            sq = tmp[:, 1, 0:512]
            ss = st[:, 96:100]
            DV.op(lambda e: e.tensor_tensor(sq, o, o, ALU.mult), f, tu[1], DV.last())
            r = DV.chain(lambda e: e.tensor_reduce(ss, sq.rearrange("p (h d) -> p h d", h=4), AX.X, ALU.add))
            r = AC.op(lambda e: e.activation(ss, ss, ACT.Sqrt, bias=k1[:, 0:1], scale=1.0 / 128), r)
            yield
            DV.op(lambda e: e.reciprocal(ss, ss), r)
            o3 = o.rearrange("p (h d) -> p h d", h=4)
            r = DV.chain(lambda e: e.tensor_tensor(o3, o3, ss.unsqueeze(2).to_broadcast([128, 4, 128]), ALU.mult))
            yield
            x = turn_out(128, r)
            q = tmp[:, 0, 0:512]
            free[5] = DV.chain(lambda e: e.tensor_scalar(q, bank(5), sm[:, DIFF_SUB:DIFF_SUB + 1], 1.0 - LAM_INIT, ALU.mult, ALU.mult), x, tu[0])
            parts(q.rearrange("p (c n) -> p c n", c=4), Yh[:, 0:4, a:a + 128], Yl[:, 0:4, a:a + 128], free[5])
            tu[0] = AC.last()

        us = []
        ready = all_of()
        for i in range(4):
            ext = 128 * i + 128
            for h in range(4):
                s = st[:, 80 + 2 * h:82 + 2 * h]
                u = dict(qr=128, ext=ext, tok=128 * i, mask=causal(ext), scale=0.125,
                         qk=[(Q[64 * x:64 * x + 64, h, 128 * i:ext], K[64 * x:64 * x + 64, h, 0:ext]) for x in range(2)],
                         chunks=[(128 * v, 128, V[:, v, 128 * h:128 * h + 128]) for v in range(i + 1)], dv=128, o=128 * h,
                         sums=[s[:, 0:1], s[:, 1:2]], pairsum=s, init=big, mix=mix, ready=ready)
                if h == 3:
                    u["end"] = True
                us.append(u)

        def others():
            for dst, c0 in ((Q, 1536), (K, 2048)):
                for c in range(4):
                    yield from rotary(dst, 4, c, c0)
        attend(us, finish, others(), 1.0)
        y0 = DV.last()
        gemm_tok("w_in_ab_2", 0, 8, cols(2560, 512), Hx, ST, hr, vcopy2(col, all_of()))
        DV.wait((sems["md"], 16))
        attend(plain_units(lambda h: (Q[64 * (h % 2):64 * (h % 2) + 64, 4 + h // 2, :], K[64 * (h % 2):64 * (h % 2) + 64, 4 + h // 2, :]),
                           lambda v, h: V[:, v, 64 * h:64 * h + 64], 0.125, lambda i, ext: spare[:, S - ext:S]), finish2(4),
               first_half("w_out_ab_2", 0, M, all_of(), y0), 0.25)
        second_half("w_out_ab_2", M, DV.last())
        return mix_end(M, 0)

    def mixer_c(yr):
        before = all_of()
        cq, ckv = [Q[:, c, :] for c in range(3)], [Q[:, c, :] for c in range(3, 5)]
        cqx, ckx = Hx[:3], Hx[3:5]
        ki, kr = spare[0:64], spare[64:96]
        ready = {}

        def win(cs, evac):
            run(gemm_steps(panel("w_in_c_2", 0, K8, cs), 0, 128, Yx, 8, ALLR, yr, evac))
        for c in range(5):
            def evac(ps, a, b, t, c=c):
                if c == 0:
                    norm_end(D, rsS, col)
                    norm_begin(ST, 3)
                if c == 3:
                    x = norm_end(384, rs2S, col2)
                    ready["q"] = normed_parts(cq, G_CQ2, rs2S, cqx, x, before)
                    norm_begin(ST, 2)
                f = DV.op(lambda e: e.tensor_tensor(Q[:, c, :], ps, rsS, ALU.mult), t, AC.last() if c == 0 else None, before)
                norm_chunk(Q[:, c, :], f)
                return f
            win(cols(128 * c, 128), evac)

        def krope(ps, a, b, t):
            x = norm_end(256, rs2S, col2)
            ready["k"] = normed_parts(ckv, G_CKV2, rs2S, ckx, x)
            return rope32(ps, 64, kr, a, b, t, rsS, before)
        win([*cols(640, 32), *swapped(640)] * 2, krope)

        def index_rope(dst, r):
            def evac(ps, a, b, t):
                x = scaled(dst[32:64], ps[32:64, :], r if r is None else r[32:64], t, before)
                return [x, rope32(ps, 0, dst[0:32], a, b, t, r, before)]
            return evac
        win([*cols(672, 64), *cols(704, 32), *swapped(672)], index_rope(ki, rsS))
        k2 = st[:, 112:144].rearrange("p (i h) -> p i h", i=4)
        gemm_tok("w_in_c_2", 0, 8, cols(736, 8), Yx, ST, yr, lambda ps, n, a, b, t: DV.op(
            lambda e: e.tensor_scalar(k2[:, n, :], ps, col[:, n:n + 1], 8.0 ** -0.5 / 8.0, ALU.mult, ALU.mult), t, before))
        for h in range(8):
            cs = [*cols(64 * h, 64), *cols(64 * h + 32, 32), *swapped(64 * h)]
            run(gemm_steps(panel("w_qi_2", 0, K3, cs), 0, 128, cqx, 3, ALLR, ready["q"], index_rope(M[0:64, h, :], None)))
        sel = v3("Z", S, 4)
        best = m["O"][:, 0:8]
        score = m["PT"][:, 0:S]
        indexed = all_of()

        def pick(i):
            ext = 128 * i + 128
            for h in range(8):
                bk = next_bank()
                ps = bank(bk)[:, 0:ext]
                t = PE.op(lambda e, ps=ps, h=h: e.matmul(ps, M[0:64, h, 128 * i:ext], ki[:, 0:ext], start=True, stop=True), free[bk], indexed)
                rl = m["P"][:, T * (h % 3):T * (h % 3) + ext]
                free[bk] = x = AC.op(lambda e, ps=ps, rl=rl: e.activation(rl, ps, ACT.Relu), t, rel.get(h % 3, indexed))
                if h == 0:
                    r = DV.chain(lambda e, rl=rl: e.tensor_scalar(score[:, 0:ext], rl, k2[:, i, 0:1], 0.0, ALU.mult, ALU.add), x, indexed)
                else:
                    r = DV.chain(lambda e, rl=rl, h=h: e.scalar_tensor_tensor(
                        out=score[:, 0:ext], in0=rl, scalar=k2[:, i, h:h + 1], in1=score[:, 0:ext], op0=ALU.mult, op1=ALU.add), x)
                rel[h % 3] = r
                if h % 2:
                    yield
            DV.chain(lambda e: e.tensor_tensor(score[:, 0:ext], score[:, 0:ext], causal(ext), ALU.add))
            for n in range(16):
                DV.chain(lambda e: e.max(best, score[:, 0:ext]))
                DV.chain(lambda e: e.match_replace(score[:, 0:ext], best, score[:, 0:ext], TAKEN))
                if n % 4 == 3:
                    yield
            DV.chain(lambda e: e.tensor_scalar(sel[:, i, 0:ext], score[:, 0:ext], -2e38, NEG, ALU.is_gt, ALU.mult))
        rel = {}

        def picks():
            for i in range(1, 4):
                yield from pick(i)
        picking = picks()

        def latent(g, Qg, before):
            yield from mla_q("w_uq_2", 0, range(8 * g, 8 * g + 8), cqx, ALLR, ready["q"], Qg, before)

        def keys(g, before):
            for c in range(4):
                hs = range(8 * g + 2 * c, 8 * g + 2 * c + 2)
                yield from gemm_steps(panel("w_uk_2", 0, K2, [64 * h + d for h in hs for d in range(64)]), 0, 128, ckx, 2, ALLR,
                                      ready["k"], two_heads(K, 2 * c, None, before))
            gemm_tok("w_uv_2", 0, 2, [64 * h + d for h in range(8 * g, 8 * g + 8) for d in range(64)], ckx, ST, ready["k"], vcopy2(None, before))
        before0 = all_of()
        for h in range(8):
            GP.op(lambda e, h=h: e.tensor_copy(K[64:96, h, :], kr), before0)
        for steps in (latent(0, Q, before0), keys(0, before0)):
            for _ in steps:
                next(picking, None)
                next(picking, None)
        run(picking)
        Qs = [Q, M]
        for g in range(2):
            if g:
                run(keys(1, all_of()))
            attend(plain_units(lambda h: (Qs[g][0:96, h, :], K[0:96, h, :]), lambda v, h: V[:, v, 64 * h:64 * h + 64], 96 ** -0.5,
                               lambda i, ext: causal(128) if i == 0 else sel[:, i, 0:ext]), finish2(4 * g),
                   latent(1, M, all_of()) if g == 0 else first_half("w_out_c_2", 0, Q, all_of(), DV.last()), 0.25)
        second_half("w_out_c_2", Q, DV.last())
        return mix_end(Q, 1)

    def causal(ext):
        return con[:, MASKF + T - ext:MASKF + T]

    x = norm_end(D, rsS, col)
    norm_begin(ST, 8)
    before = PE.last()
    hr = {}
    for c in range(8):
        f = DV.op(lambda e, c=c: e.scalar_tensor_tensor(
            out=X2[:, c, :], in0=X2[:, c, :], scalar=sm[:, FINAL_G + c:FINAL_G + c + 1], in1=rsS, op0=ALU.mult, op1=ALU.mult), x)
        hr[c] = mult_parts(X2[:, c, :], MIX_PRE + c, Hx[c], f, before)
    hr = mixer_ab(hr)
    hr = mlp(0, hr)
    hr = ple(0, hr)
    hr = mixer_c(hr)
    hr = mlp(1, hr)
    ple(1, hr)
    SP.wait((sems["out"], 8 * 16))
    return dict(sp=SP, act=AC, dve=DV, pool=GP, pe=PE), panels


def tables():
    c = np.zeros((128, NCON), np.float32)
    c[:, IDENT:IDENT + 128] = np.eye(128)
    c[:, ONES:ONES + 128] = 1.0
    q, k = np.arange(128)[:, None], np.arange(128)[None, :]
    c[:, MASKF + 400:MASKF + 528] = np.where(k <= q, 0.0, NEG)
    c[:, MASKS:MASKS + 128] = np.where(k > q, 0.0, NEG)
    c[:, MASKS + 128:MASKS + 256] = np.where(k <= q, 0.0, NEG)
    pos = np.arange(T, dtype=np.float32)

    def angles(half):
        inv = (np.float32(10000.0) ** (-np.arange(half, dtype=np.float32) / np.float32(half))).astype(np.float32)
        return inv[:, None] * pos[None, :]
    a = angles(32)
    for h in range(0, 128, 64):
        c[h:h + 32, COS:COS + T] = c[h + 32:h + 64, COS:COS + T] = np.cos(a)
        c[h:h + 32, SIN:SIN + T] = np.sin(a)
        c[h + 32:h + 64, SIN:SIN + T] = -np.sin(a)
    a = angles(16)
    for h in (0, 64):
        c[h:h + 16, T2:T2 + T] = c[h + 16:h + 32, T2:T2 + T] = np.cos(a)
    c[96:112, T2:T2 + T] = -np.sin(a)
    c[112:128, T2:T2 + T] = np.sin(a)
    d = (np.arange(128)[:, None] + 384) - np.arange(512)[None, :]
    n = ((d >= 0) & (d <= 128)).astype(int) + ((d >= 0) & (d % 4 == 0)) + ((d >= 0) & (d % 16 == 0))
    maskd = np.where(n > 0, 8.0 * np.log(np.maximum(n, 1)), NEG).astype(np.float32)
    return c, maskd


_NAMES = ("w_in", "w_branch", "w_out", "w_uq", "w_ukv", "w_mlp_in_2", "w_mlp_out_2", "w_ple_proj_2", "w_ple_gate_2",
          "w_in_ab_2", "w_out_ab_2", "w_in_c_2", "w_uq_2", "w_qi_2", "w_uk_2", "w_uv_2", "w_out_c_2")


def kernel(**inputs):
    import concourse.bacc as _bacc
    from concourse.bass_utils import run_bass_kernel_spmd as _run

    a = {k: np.asarray(v) for k, v in inputs.items()}
    con, maskd = tables()
    x = np.concatenate([a["meta_tokens"], a["x"][0]], axis=0)
    xT = np.ascontiguousarray(x.reshape(T, 8, 128).transpose(2, 1, 0)).reshape(128, 8 * T)
    pT = np.ascontiguousarray(a["p_2"][:, 0].reshape(2, S, 2, 128).transpose(0, 3, 2, 1)).reshape(2, 128, 2 * S)
    sm = np.zeros((128, NSM), np.float32)

    def put(o, v):
        v = v.reshape(-1, 128).T
        sm[:, o:o + v.shape[1]] = v
    for o, n in ((NORM_G, "norm_g"), (G_CQ, "g_cq"), (G_CKV, "g_ckv"), (FINAL_G, "final_g"), (MIX_PRE, "g_mix_pre_2"),
                 (MIX_POST, "g_mix_post_2"), (MLP_PRE, "g_mlp_pre_2"), (MLP_POST, "g_mlp_post_2"),
                 (DIFF_SUB, "g_diff_sub_2"), (G_CQ2, "g_cq_2"), (G_CKV2, "g_ckv_2")):
        put(o, a[n])
    sm[0:8, B_F:B_F + 2] = a["b_f"].T
    sm[:, SINKS:SINKS + 16] = a["sinks"].reshape(1, 16)
    lam = np.concatenate([np.broadcast_to(a[n].reshape(1, 64), (128, 64)) for n in (
        "diff_lq1_2", "diff_lk1_2", "diff_lq2_2", "diff_lk2_2")], axis=1)

    nc = _bacc.Bacc("TRN2", target_bir_lowering=False, num_devices=1)
    A = {
        "x": nc.dram_tensor("in_x", (128, 8 * T), F, kind="ExternalInput").ap(),
        "con": nc.dram_tensor("in_con", (128, NCON), F, kind="ExternalInput").ap(),
        "sm": nc.dram_tensor("in_sm", (128, NSM), F, kind="ExternalInput").ap(),
        "p": nc.dram_tensor("in_p", (2, 128, 2 * S), F, kind="ExternalInput").ap(),
        "lam": nc.dram_tensor("in_lam", (128, 256), F, kind="ExternalInput").ap(),
        "maskd": nc.dram_tensor("in_maskd", (128, S), F, kind="ExternalInput").ap(),
        "w": nc.dram_tensor("in_w", (WTOTAL,), F, kind="ExternalInput").ap(),
    }
    out = nc.dram_tensor("out_0", (128, 8, S), F, kind="ExternalOutput").ap()
    spec = program(nc, A, out)

    w = np.empty(WTOTAL, np.float32)
    mats = {n: a[n] for n in _NAMES}
    for n in ("w_uk_2", "w_uv_2"):
        mats[n] = mats[n].reshape(1, 256, 1024)
    o = 0
    for name, idx, kcs, cols in spec:
        mat = mats[name][idx]
        cs = np.asarray(cols)
        rows = mat[128 * kcs[0]:128 * kcs[-1] + 128]
        part = rows[:, cs[0]:cs[0] + len(cs)] if np.all(np.diff(cs) == 1) else rows[:, cs]
        n = 128 * len(kcs) * len(cs)
        w[o:o + n].reshape(128, len(kcs), len(cs))[:] = part.reshape(len(kcs), 128, len(cs)).transpose(1, 0, 2)
        o += n
    r = _run(nc, [{"in_x": xT, "in_con": con, "in_sm": sm, "in_p": pT, "in_maskd": maskd, "in_lam": np.ascontiguousarray(lam), "in_w": w}], core_ids=[0])
    y = r.results[0]["out_0"]
    return np.ascontiguousarray(y.reshape(128, 8, S).transpose(2, 1, 0)).reshape(1, S, D)
```

```python
import numpy as np
from contextlib import ExitStack

import concourse.bass as bass
from concourse import mybir

F = mybir.dt.float32
FR = mybir.dt.float32r
ALU = mybir.AluOpType
ACT = mybir.ActivationFunctionType
AX = mybir.AxisListType

D = 1024
NM = 16
S = 512
T = NM + S
EPS = 1e-6
NEG = -1e30
BIG = 3e38
TAKEN = -3e38
HALF = 264
PAN = 512
RAW = 5
WS = 4
WTOTAL = 128 * 389120
LAM_INIT = 0.8 - 0.6

NORM_G, G_CQ, G_CKV, FINAL_G = 0, 16, 22, 26
MIX_PRE, MIX_POST, MLP_PRE, MLP_POST = 34, 50, 66, 82
DIFF_SUB, G_CQ2, G_CKV2, B_F, SINKS = 98, 99, 102, 104, 106
NSM = 122

IDENT, ONES, MASKF, MASKS, COS, SIN, T2, NCON = 0, 128, 256, 784, 1040, 1568, 2096, 2624


class Queue:

    def __init__(self, sem):
        self.sem, self.n, self.list, self.waited = sem, 0, [], {}

    def wait(self, *tokens):
        for t in tokens:
            if t is None:
                continue
            if isinstance(t, list):
                self.wait(*t)
                continue
            sem, v = t
            if self.waited.get(id(sem), 0) < v:
                self.waited[id(sem)] = v
                self.list.append(("wait", sem, v))

    def op(self, make, *after, count=True):
        self.wait(*after)
        self.list.append(("op", make, count))
        self.n += count
        return self.last()

    def chain(self, make, *after):
        return self.op(make, self.last(), *after)

    def last(self):
        return (self.sem, self.n) if self.n else None

    def dma(self, make, sem, *after):
        self.wait(*after)
        self.list.append(("dma", make, sem))

    def play(self, eng):
        for kind, a, b in self.list:
            if kind == "wait":
                eng.wait_ge(a, b)
            elif kind == "dma":
                a(eng).then_inc(b, 16)
            else:
                ins = a(eng)
                if b:
                    ins.then_inc(self.sem, 1)


def program(nc, A, out):
    with ExitStack() as ctx:
        def sb(name, cols, dt=F):
            return ctx.enter_context(nc.sbuf_tensor(name, [128, cols], dt))

        def sem(name):
            return ctx.enter_context(nc.semaphore(name))

        m = {
            "X": sb("X", 8 * T), "Hh": sb("Hh", 8 * T, FR), "Hl": sb("Hl", 8 * T, FR),
            "M": sb("M", 8 * T), "Q": sb("Q", 8 * T), "K": sb("K", 8 * T), "V": sb("V", 5 * 512),
            "Yh": sb("Yh", 8 * T, FR), "Yl": sb("Yl", 8 * T, FR), "Z": sb("Z", 4 * T),
            "raw": sb("raw", RAW * PAN), "wh": sb("wh", WS * PAN, FR), "wl": sb("wl", WS * PAN, FR),
            "P": sb("P", 3 * T), "PT": sb("PT", 2 * 640), "O": sb("O", 512),
            "tmp": sb("tmp", 2 * T), "rs": sb("rs", T), "st": sb("st", 160),
            "con": sb("con", NCON), "sm": sb("sm", NSM), "k1": sb("k1", 4),
        }
        PP = [ctx.enter_context(nc.psum_tensor(f"pp{i}", [128, 1024], F)) for i in range(4)]
        sems = {n: sem(n) for n in ("pe", "act", "dve", "pool", "sp", "x0", "x1", "x2", "x3", "in1", "in2", "md", "aug0", "aug1", "aug2", "aug3", "pin0", "pin1", "lam", "out")}
        sems["w"] = [sem(f"w{i}") for i in range(RAW)]
        spec = emit(m, PP, sems, A, out, None)[1]
        queues, _ = emit(m, PP, sems, A, out, spec)
        block = ctx.enter_context(nc.Block())

        @block.sync
        def _(eng):
            queues["sp"].play(eng)

        @block.scalar
        def _(eng):
            queues["act"].play(eng)

        @block.vector
        def _(eng):
            queues["dve"].play(eng)

        @block.gpsimd
        def _(eng):
            queues["pool"].play(eng)

        @block.tensor
        def _(eng):
            queues["pe"].play(eng)
    return spec


def emit(m, PP, sems, A, out, spec):
    SP, AC, DV, GP, PE = (Queue(sems[n]) for n in ("sp", "act", "dve", "pool", "pe"))
    panels = []
    con, sm, k1, st = m["con"], m["sm"], m["k1"], m["st"]

    def bank(b):
        return PP[b // 2][:, 512 * (b % 2):512 * (b % 2) + 512]

    free = [None] * 8

    def v3(name, n, c, off=0):
        return m[name][:, off:off + n * c].rearrange("p (c n) -> p c n", c=c)

    done = []
    where = []
    off = 0
    for _, _, kcs, cols in spec or []:
        where.append((off, len(kcs) * len(cols)))
        off += 128 * len(kcs) * len(cols)
    assert not spec or off == WTOTAL, off // 128
    landed, split_at = {}, {}

    def fetch(j):
        if j >= len(where):
            return
        o, n = where[j]
        dst = m["raw"][:, (j % RAW) * PAN:(j % RAW) * PAN + n]
        src = A["w"][o:o + 128 * n].rearrange("(p n) -> p n", p=128)
        SP.dma(lambda e: e.dma_start(dst, src), sems["w"][j % RAW], split_at.get(j - RAW))
        landed[j] = (sems["w"][j % RAW], 16 * (j // RAW + 1))

    def split(j):
        if j >= len(where):
            return
        n = where[j][1]
        raw = m["raw"][:, (j % RAW) * PAN:(j % RAW) * PAN + n]
        hi = m["wh"][:, (j % WS) * PAN:(j % WS) * PAN + n]
        lo = m["wl"][:, (j % WS) * PAN:(j % WS) * PAN + n]
        used = done[j - WS] if j >= WS else None
        a = AC.op(lambda e: e.activation(hi, raw, ACT.Copy), landed[j], used)
        b = DV.op(lambda e: e.tensor_tensor(lo, raw, hi.bitcast(F), ALU.subtract), a, used)
        split_at[j] = [a, b]
        fetch(j + RAW)

    def panel(name, idx, kcs, cols):
        kcs, cols = list(kcs), list(cols)
        per = PAN // len(cols)
        assert per
        out = []
        for i in range(0, len(kcs), per):
            ks = kcs[i:i + per]
            panels.append((name, idx, ks, cols))
            out.append((range(i, i + len(ks)), len(panels) - 1))
        return out

    def use(part):
        ks, j = part
        while len(done) < j:
            done.append(PE.last())
        if where:
            if j == 0:
                for i in range(RAW):
                    fetch(i)
                for i in range(WS - 2):
                    split(i)
            split(j + WS - 2)
        n = len(panels[j][2]) * len(panels[j][3])
        o = (j % WS) * PAN
        hi, lo = (m[x][:, o:o + n].rearrange("p (k n) -> p k n", k=len(ks)) for x in ("wh", "wl"))
        return ks, hi, lo, split_at.get(j)

    NB = 5
    FREE, FILL = [0, 1, 2, 3, 4, 6, 7], [2, 3, 7]
    rot = {"banks": FREE, "n": 0}

    def next_bank():
        b = rot["banks"][rot["n"] % len(rot["banks"])]
        rot["n"] += 1
        return b

    def products(w, x, first, last, outs, *after):
        (wh, wl), (xh, xl) = w, x
        for n, (p, q) in enumerate(((wh, xh), (wh, xl), (wl, xh))):
            for ps, wc, xc in outs:
                t = PE.op(lambda e, ps=ps, p=p[:, wc], q=q[:, xc], n=n: e.matmul(
                    ps, p, q, start=first and n == 0, stop=last and n == 2), *after, count=n == 2)
        return t

    def gemm_steps(parts_, c0, c1, x, kc, ranges, ready, evac):
        outs = []
        for a, b in ranges:
            bk = next_bank()
            outs.append([bk, a, b, bank(bk)[0:c1 - c0, 0:b - a], None])
        for part in parts_:
            ks, hi, lo, there = use(part)
            for out in outs:
                bk, a, b, ps, _ = out
                for k in ks:
                    out[4] = products((hi[:, k - ks[0], :], lo[:, k - ks[0], :]), x[k], k == 0, k == kc - 1,
                                      [(ps, slice(c0, c1), slice(a, b))], there, free[bk] if k == 0 else None,
                                      ready[k] if isinstance(ready, dict) else ready)
                    yield
        for bk, a, b, ps, t in outs:
            free[bk] = evac(ps, a, b, t)

    def run(steps):
        for _ in steps:
            pass

    def gemm(*args):
        run(gemm_steps(*args))

    def gemm_tok(name, idx, kc, cols, x, tiles, ready, evac):
        bks = [next_bank() for _ in tiles]
        for part in panel(name, idx, range(kc), cols):
            ks, hi, lo, there = use(part)
            for (a, b), bk in zip(tiles, bks):
                for k in ks:
                    t = products(x[k], (hi[:, k - ks[0], :], lo[:, k - ks[0], :]), k == 0, k == kc - 1,
                                 [(bank(bk)[:, 0:len(cols)], slice(a, a + 128), slice(0, len(cols)))],
                                 there, ready[k] if isinstance(ready, dict) else ready, free[bk] if k == 0 else None)
        for n, ((a, b), bk) in enumerate(zip(tiles, bks)):
            free[bk] = evac(bank(bk)[0:b - a, 0:len(cols)], n, a, b, t)

    behind = []

    def lag(make):
        token = []
        behind.append((make, token))
        if len(behind) > 1:
            caught_up(1)
        return token

    def caught_up(keep=0):
        while len(behind) > keep:
            make, token = behind.pop(0)
            token.append(make())

    def parts(src, hi, lo, *after, lagging=False):
        a = AC.op(lambda e: e.activation(hi, src, ACT.Copy), *after)

        def low():
            return DV.op(lambda e: e.tensor_tensor(lo, src, hi.bitcast(F), ALU.subtract), a, *after)
        return lag(low) if lagging else low()

    def scaled_parts(src, g, hi, lo, *after, lagging=False):
        a = AC.op(lambda e: e.activation(hi, src, ACT.Copy, scale=g), *after)

        def low():
            return DV.op(lambda e: e.scalar_tensor_tensor(out=lo, in0=src, scalar=g, in1=hi.bitcast(F), op0=ALU.mult, op1=ALU.subtract), a, *after)
        return lag(low) if lagging else low()

    def both(h, l, n, c, off=0):
        return [(m[h][:, off + n * i:off + n * i + n], m[l][:, off + n * i:off + n * i + n]) for i in range(c)]

    tmp = v3("tmp", T, 2)
    ones = con[:, ONES:ONES + 128]
    ident = con[:, IDENT:IDENT + 128]
    tu = [None, None]

    def norm_begin(tiles, squares="K", first=0, at=0):
        return dict(tiles=tiles, at=at, squares=squares, first=first, c=first, todo=[], free=[free[NB], DV.last(), PE.last()])

    def norm_chunk(N, src, *after):
        c, tiles, first = N["c"], N["tiles"], N["first"]
        N["c"] += 1
        n = tiles[-1][1] - tiles[0][0]
        sqs = [m[N["squares"]][:, T * x:T * x + n] for x in range(first, c + 1)]
        if c > first + 1:
            N["added"] = GP.chain(lambda e: e.tensor_tensor(sqs[0], sqs[0], sqs[-2], ALU.add), N["squared"])
        N["squared"] = AC.op(lambda e: e.activation(sqs[-1], src, ACT.Square), N["free"] if c == first else None, *after)

    def norm_sum(N):
        tiles, at, first, last = N["tiles"], N["at"], N["first"], N["c"] - 1
        for q in (PE, DV):
            q.wait((sems["in1"], 16))
        base = tiles[0][0]
        sqs = [m[N["squares"]][:, T * x:T * x + tiles[-1][1] - base] for x in (first, last)]
        for i, (p, q) in enumerate(tiles):
            for x, sq in enumerate(sqs):
                N["sum"] = PE.op(lambda e, i=i, p=p, q=q, x=x, sq=sq: e.matmul(
                    bank(NB)[0:q - p, at + i:at + i + 1], sq[:, p - base:q - base], ones[:, 0:1], start=x == 0, stop=x == 1),
                    N["squared"], N.get("added"), N["free"], count=i == len(tiles) - 1 and x == 1)

    def norm_col(N, width, col):
        if "sum" not in N:
            norm_sum(N)
        tiles, at, k = N["tiles"], N["at"], len(N["tiles"])
        small = tiles[0][1] - tiles[0][0] < 128
        groups = N["groups"] = ([(NM, 0, 1)] if small else []) + [(128, int(small), k)]
        for r, x, y in groups:
            a = AC.op(lambda e, r=r, x=x, y=y: e.activation(
                col[0:r, x:y], bank(NB)[0:r, at + x:at + y], ACT.Sqrt, bias=k1[0:r, 0:1], scale=1.0 / width), N["sum"], N["free"])
        free[NB] = a
        for r, x, y in groups:
            d = DV.op(lambda e, r=r, x=x, y=y: e.reciprocal(col[0:r, x:y], col[0:r, x:y]), a)
        N["dg"] = [m["PT"][0:q - p, 80 * at + 128 * i:80 * at + 128 * i + q - p] for i, (p, q) in enumerate(tiles)]
        for i, (p, q) in enumerate(tiles):
            N["d"] = DV.op(lambda e, i=i, r=q - p: e.tensor_scalar(N["dg"][i], ident[0:r, 0:r], col[0:r, i:i + 1], None, ALU.mult), d, N["sum"])

    def norm_rows(N, rs):
        tiles, groups = N["tiles"], N["groups"]
        base = tiles[0][0]
        bks = [next_bank() for _ in groups]
        for i, (p, q) in enumerate(tiles):
            bk = bks[0 if i == 0 else -1]
            at = p - tiles[len(groups) - 1 if i else 0][0]
            t = PE.op(lambda e, i=i, r=q - p, bk=bk, at=at: e.matmul(
                bank(bk)[:, at:at + r], ones[0:r, :], N["dg"][i], start=True, stop=True), N["d"], free[bk] if at == 0 else None)
        for (r, x, y), bk in zip(groups, bks):
            p, q = tiles[x][0] - base, tiles[y - 1][1] - base
            free[bk] = AC.op(lambda e, p=p, q=q, bk=bk: e.activation(rs[:, p:q], bank(bk)[:, 0:q - p], ACT.Copy), t)
        DV.wait(AC.last())
        return AC.last()

    def lead(N, rs, first, second, first_n=1, second_n=1):
        for k in range(8 * first_n):
            next(first)
        norm_col(N, D, col)
        for k in range(8 * second_n):
            next(second)
        norm_rows(N, rs)
        run(first)
        run(second)

    def normed_parts(xs, g, rs, outs, *after):
        ready = {}
        for c, x in enumerate(xs):
            a = DV.op(lambda e, c=c, x=x: e.scalar_tensor_tensor(
                out=x, in0=x, scalar=sm[:, g + c:g + c + 1], in1=rs, op0=ALU.mult, op1=ALU.mult), *after)
            ready[c] = parts(x, *outs[c], a, lagging=True)
        caught_up()
        return ready

    units = {"n": 0}

    def attend(heads, finish, steps, total):
        steps = iter(steps)
        due = {"n": 0.0}
        pend1, pend2, late = [], [], []
        now = [DV.last(), AC.last(), PE.last()]
        pfree, ptfree = [now] * 6, [now] * 2
        deep = 2

        def fill():
            due["n"] += total / (2 * (len(heads) + deep + 1) + 3)
            while due["n"] >= 1:
                due["n"] -= 1
                next(steps, None)

        def scores(u):
            n = units["n"]
            units["n"] += 1
            u["n"] = n
            qr, ext = u["qr"], u["ext"]
            assert u.get("after") != []
            single = len(u["qk"]) == 1
            u["p"], u["slots"], u["exps"] = [], [], []
            for x, (q, k) in enumerate(u["qk"]):
                slot = n % 3 if single else 2 * (n % 3) + x
                bk = n % 2 if single else x
                cut = max(0, ext - 512)
                sc = bank(bk)[0:qr, 0:ext - cut]
                p = m["P" if single else "M"][0:qr, slot * T:slot * T + ext]
                s = n % 32 if single else 2 * (n % 16) + x
                neg, init, tot, mask = st[0:qr, s:s + 1], u["init"], u["sums"][x], u["mask"]
                a = None
                if cut:
                    over = bank(5)[0:qr, 0:cut]
                    t = PE.op(lambda e, q=q, k=k: e.matmul(over, q, k[:, 0:cut], start=True, stop=True), free[5], u["ready"])
                    first = st[0:qr, 144 + n % 16:145 + n % 16]
                    a = free[5] = DV.op(lambda e, p=p, init=init: e.tensor_tensor_reduce(
                        p[:, 0:cut], over, mask[:, 0:cut], -u["scale"], init, ALU.add, ALU.min, first), t, pfree[slot])
                    init = first
                t = PE.op(lambda e, sc=sc, q=q, k=k: e.matmul(sc, q, k[:, cut:ext], start=True, stop=True), free[bk], u["ready"])
                free[bk] = a = DV.op(lambda e, sc=sc, p=p, neg=neg, init=init: e.tensor_tensor_reduce(
                    p[:, cut:ext], sc, mask[:, cut:ext], -u["scale"], init, ALU.add, ALU.min, neg), a, t, pfree[slot], u.get("after"))
                u["exp"] = AC.op(lambda e, p=p, neg=neg, tot=tot: e.activation(
                    p, p, ACT.Exp, bias=neg, scale=-1.0, accum_out=tot), a)
                u["p"].append(p)
                u["slots"].append(slot)
            if "sink" in u:
                snk, e1 = u["sink"]
                u["e1"] = AC.op(lambda e, neg=neg: e.activation(e1, snk, ACT.Exp, bias=neg, scale=1.0))

        def turn(u):
            qr = u["qr"]
            if u is heads[-1] and "mix" in u:
                u["exp"] = u["mix"](u)
            p = u["p"][0]
            whole = [c for c in u["chunks"] if c[1] == 128]
            small = [c for c in u["chunks"] if c[1] != 128]
            slot = u["n"] % 2
            pt = m["PT"][:, slot * 640:slot * 640 + 640]
            u["pt"], u["cp"] = [], []
            for o, rows, v in small:
                if qr == 128:
                    t = PE.op(lambda e, o=o: e.transpose(bank(5)[:, 0:128], p[:, o:o + 128], ident), free[5], u["exp"])
                else:
                    t = PE.op(lambda e, o=o, rows=rows: e.matmul(bank(5)[0:rows, 0:qr], p[:, o:o + rows], ident[0:qr, 0:qr], start=True, stop=True), free[5], u["exp"])
                free[5] = DV.op(lambda e, rows=rows: e.tensor_copy(pt[0:rows, 512:512 + qr], bank(5)[0:rows, 0:qr]), t, ptfree[slot])
                u["pt"].append((pt[0:rows, 512:512 + qr], v))
                u["cp"].append(free[5])
            if whole:
                for x, (o, rows, v) in enumerate(whole):
                    t = PE.op(lambda e, o=o, x=x: e.transpose(bank(4)[:, 128 * x:128 * x + 128], p[:, o:o + 128], ident), free[4] if x == 0 else None, u["exp"])
                    u["pt"].append((pt[:, 128 * x:128 * x + 128], v))
                w = 128 * len(whole)
                if u["n"] % 2:
                    free[4] = AC.op(lambda e: e.activation(pt[:, 0:w], bank(4)[:, 0:w], ACT.Copy), t, ptfree[slot])
                else:
                    free[4] = DV.op(lambda e: e.tensor_copy(pt[:, 0:w], bank(4)[:, 0:w]), t, ptfree[slot])
                u["cp"].append(free[4])
            for x in u["slots"]:
                pfree[x] = t

        def product(u):
            qr = u["qr"]
            o = bank(6)[0:qr, u["o"]:u["o"] + u["dv"]]
            n = len(u["pt"])
            for x, (p, v) in enumerate(u["pt"]):
                t = PE.op(lambda e, x=x, p=p, v=v: e.matmul(o, p, v, start=x == 0, stop=x == n - 1),
                          u["cp"], u["vready"], free[6] if u["o"] == 0 else None, count=x == n - 1)
            ptfree[u["n"] % 2] = t
            if "end" in u:
                late.append(finish(u, t))

        rot["banks"] = FILL
        for u in heads + [None] * (deep + 1):
            if u:
                scores(u)
                if pend1 and "mix" in u:
                    pend1[-1]["exp"] = u["mix"](pend1[-1])
                pend1.append(u)
            fill()
            if len(pend1) > (deep if u else 0):
                turn(pend1[0])
                pend2.append(pend1.pop(0))
            fill()
            if len(pend2) > (1 if u else 0):
                product(pend2.pop(0))
            if late and next(late[0], "end") == "end":
                late.pop(0)
        for g in late:
            for _ in g:
                fill()
        run(steps)
        rot["banks"] = FREE

    turned = {"o": None}

    def turn_out(qr, *after):
        for c in range(4):
            t = PE.op(lambda e, c=c: e.transpose(bank(5)[:, 128 * c:128 * c + qr], m["O"][0:qr, 128 * c:128 * c + 128], ident[0:qr, 0:qr]),
                      free[5] if c == 0 else None, *after, count=c == 3)
        turned["o"] = t
        return t

    def divided(u, t, sums):
        qr = u["qr"]
        o = m["O"][0:qr, :]
        DV.chain(lambda e: e.reciprocal(sums, sums), t)
        free[6] = DV.chain(lambda e: e.tensor_tensor(
            o.rearrange("p (h d) -> p h d", h=8), bank(6)[0:qr, :].rearrange("p (h d) -> p h d", h=8),
            sums.unsqueeze(2).to_broadcast([qr, 8, 64]), ALU.mult), turned["o"])
        return free[6]

    X = v3("X", T, 8)
    AC.dma(lambda e: e.dma_start(sm[:, :], A["sm"]), sems["in2"])
    for i in range(4):
        (SP if i < 2 else AC).dma(lambda e, i=i: e.dma_start(m["X"][:, 2 * T * i:2 * T * i + 2 * T], A["x"][:, 2 * T * i:2 * T * i + 2 * T]), sems[f"x{i}"])
    AC.dma(lambda e: e.dma_start(con[:, :], A["con"]), sems["in1"])
    loaded = [(sems["in2"], 16)]

    def x_at(c):
        return (sems[f"x{c // 2}"], 16)
    DV.chain(lambda e: e.memset(k1[:, 0:1], EPS))
    DV.chain(lambda e: e.memset(k1[:, 1:2], 1.0))
    DV.chain(lambda e: e.memset(k1[:, 2:3], BIG))
    for q in (AC, DV, PE):
        q.wait(loaded, DV.last())

    maskF = con[:, MASKF:MASKF + T]
    maskS = con[:, MASKS:MASKS + 256]
    cos, sin, t2 = (con[:, o:o + T] for o in (COS, SIN, T2))
    big = k1[:, 2:3]

    rs = m["rs"]
    rs2, rs3 = m["P"][:, 2 * T:3 * T], m["P"][:, T:2 * T]
    col, col2, col3 = st[:, 64:72], st[:, 72:80], st[:, 88:96]

    def scaled(dst, ps, r, *after):
        if r is None:
            return AC.op(lambda e: e.activation(dst, ps, ACT.Copy), *after)
        return DV.op(lambda e: e.tensor_tensor(dst, ps, r, ALU.mult), *after)

    def rope64(ps, dst, a, b, t, *after, later=None):
        p, q = (tmp[:, i, 0:b - a] for i in range(2))
        AC.op(lambda e: e.activation(q, ps, ACT.Copy), t, DV.last(), tu)
        for r in range(4):
            x = AC.op(lambda e, r=r: e.activation(p[32 * r:32 * r + 32], ps[32 * (r ^ 1):32 * (r ^ 1) + 32, :], ACT.Copy))

        def rest():
            DV.op(lambda e: e.tensor_tensor(q, q, cos[:, a:b], ALU.mult), x, *after)
            DV.op(lambda e: e.tensor_tensor(p, p, sin[:, a:b], ALU.mult))
            DV.chain(lambda e: e.tensor_tensor(p, p, q, ALU.add))
            DV.chain(lambda e: e.tensor_tensor(dst, p, rs[:, a:b], ALU.mult))
        if later is None:
            rest()
        else:
            later.append(rest)
        return x

    def rope32(ps, row, dst, a, b, t, r, *after):
        p, q = (tmp[row:row + 32, i, 0:b - a] for i in range(2))
        DV.chain(lambda e: e.tensor_tensor(p, ps[96:128, :], t2[96:128, a:b], ALU.mult), t, tu, *after)
        f = DV.op(lambda e: e.tensor_tensor(q, ps[row:row + 32, :], t2[row:row + 32, a:b], ALU.mult))
        if r is None:
            DV.chain(lambda e: e.tensor_tensor(dst, p, q, ALU.add))
        else:
            DV.chain(lambda e: e.tensor_tensor(p, p, q, ALU.add))
            DV.chain(lambda e: e.tensor_tensor(dst, p, r[row:row + 32, a:b], ALU.mult))
        return f

    K8, K4, K3, K2 = range(8), range(4), range(3), range(2)

    def cols(a, n):
        return range(a, a + n)

    def swapped(a):
        return [*range(a + 16, a + 32), *range(a, a + 16)]

    def mla_q(name, l, heads, x, ranges, ready, Q, *after, headed=None):
        for i, h in enumerate(heads):
            def evac(ps, a, b, t, i=i):
                x = AC.op(lambda e: e.activation(Q[0:64, i, a:b], ps[0:64, :], ACT.Copy), t, *after)
                f = rope32(ps, 64, Q[64:96, i, a:b], a, b, t, None, *after)
                if headed is not None:
                    headed[i] = [x, DV.last()]
                return [x, f]
            yield from gemm_steps(panel(name, l, K3, [*cols(96 * h, 64), *cols(96 * h + 64, 32), *swapped(96 * h + 64)]),
                                  0, 128, x, 3, ranges, ready, evac)

    def two_heads(dst, h, r, *after):
        def evac(ps, a, b, t):
            if r is None:
                x = AC.op(lambda e: e.activation(dst[0:64, h, a:b], ps[0:64, :], ACT.Copy), t, *after)
                return [x, DV.op(lambda e: e.tensor_copy(dst[0:64, h + 1, a:b], ps[64:128, :]), t, *after)]
            DV.op(lambda e: e.tensor_tensor(dst[0:64, h, a:b], ps[0:64, :], r[0:64, a:b], ALU.mult), t, *after)
            return DV.op(lambda e: e.tensor_tensor(dst[0:64, h + 1, a:b], ps[64:128, :], r[64:128, a:b], ALU.mult))
        return evac

    TOKR = [(0, HALF), (HALF, T)]
    TILES = [(0, NM)] + [(NM + 128 * i, NM + 128 * i + 128) for i in range(4)]

    def all_of():
        return [q.last() for q in (AC, DV, GP, PE)]

    Hx = both("Hh", "Hl", T, 8)

    def first_layer(l, hr, N):
        QR = TOKR if l == 0 else [(NM, T)]
        Q, K, M, Z = v3("Q", T, 8), v3("K", T, 8), v3("M", T, 8), v3("Z", T, 4)
        V = v3("V", 512, 5)
        Yv = [[x[:, 4 * T * i:4 * T * i + 4 * T].rearrange("p (c n) -> p c n", c=4) for x in (m["Yh"], m["Yl"])] for i in range(2)]
        Yx = [both("Yh", "Yl", T, 4, 4 * T * i) for i in range(2)]

        def win(cs, ranges, evac):
            return gemm_steps(panel("w_in", l, K8, cs), 0, 128, Hx, 8, ranges, hr, evac)

        def zgate(c0, c):
            def evac(ps, a, b, t):
                zz, g = tmp[:, 0, 0:b - a], tmp[:, 1, 0:b - a]
                f = DV.chain(lambda e: e.tensor_tensor(zz, ps, rs[:, a:b], ALU.mult), t, tu)
                x = AC.op(lambda e: e.activation(g, zz, ACT.Tanh, scale=0.5), f)
                DV.op(lambda e: e.scalar_tensor_tensor(out=Z[:, c, a:b], in0=g, scalar=1.0, in1=zz, op0=ALU.add, op1=ALU.mult), x)
                return f
            run(win(cols(c0 + 128 * c, 128), QR, evac))

        def merge(n, ready, slots, then=None):
            used = [all_of()] * len(slots)
            gated = {}
            Mready = all_of()

            def gate(c):
                s = c % len(slots)

                def evac(ps, a, b, t):
                    tg = slots[s][:, a:b]
                    f = DV.op(lambda e: e.tensor_tensor(tg, ps, rs[:, a:b], ALU.mult), t, used[s])
                    gated[c] = AC.op(lambda e: e.activation(tg, tg, ACT.Tanh, scale=0.5), f)
                    return f
                return win(cols(4520 + 1024 * n + 128 * c, 128), QR, evac)

            def proj(c):
                s = c % len(slots)

                def evac(ps, a, b, t):
                    tg = slots[s][:, a:b]
                    dst = M[:, c, a:b] if n == 0 else tg
                    f = DV.op(lambda e: e.scalar_tensor_tensor(
                        out=dst, in0=tg, scalar=1.0, in1=ps, op0=ALU.add, op1=ALU.mult), t, gated[c], Mready)
                    if n:
                        DV.chain(lambda e: e.tensor_tensor(M[:, c, a:b], M[:, c, a:b], tg, ALU.add))
                    used[s] = DV.last()
                    if then and b == T:
                        then(c)
                    return f
                return gemm_steps(panel("w_branch", (l, n), K4, cols(128 * c, 128)), 0, 128, Yx[n % 2], 4, QR, ready, evac)

            ahead = len(slots) - 1
            if ahead:
                yield from gate(0)
            for c in range(8):
                if c + ahead < 8:
                    yield from gate(c + ahead)
                yield from proj(c)

        def finish_to(n):
            def finish(u, t):
                qr, a = u["qr"], u["tok"]
                if "sink" in u:
                    DV.chain(lambda e: e.tensor_tensor(u["all"], u["all"], u["alle"], ALU.add), t, u["e1"])
                r = divided(u, t, u["all"])
                yield
                x = turn_out(qr, r)
                q = tmp[:, 0, 0:4 * qr].rearrange("p (c n) -> p c n", c=4)
                free[5] = DV.chain(lambda e: e.tensor_tensor(q, bank(5)[:, :].rearrange("p (c n) -> p c n", c=4)[:, :, 0:qr],
                                                             Z[:, :, a:a + qr], ALU.mult), x, tu)
                parts(q, *(y[:, :, a:a + qr] for y in Yv[n % 2]), free[5])
                tu[0] = AC.last()
            return finish

        def units_of(qk, vof, scale, ready, vready, sinks=None, window=False):
            us = []
            for i in range(-1 if l == 0 else 0, 4):
                qr, a = (NM, 0) if i < 0 else (128, NM + 128 * i)
                if i < 0:
                    k0, ext = 0, NM
                    mk = maskF[0:NM, 400:400 + NM] if not window else maskS[0:NM, 128:128 + NM]
                elif window:
                    k0 = 0 if i == 0 else NM + 128 * (i - 1)
                    ext = a + 128 - k0
                    mk = maskS[:, 256 - ext:256]
                else:
                    k0, ext = 0, a + 128
                    mk = maskF[:, T - ext:T]
                chunks = [(x - k0, y - x, v) for v, (x, y) in enumerate(TILES) if x >= k0 and y <= k0 + ext]
                o = 32 + 16 * (i % 2)
                sums, e1 = st[0:qr, o:o + 8], st[0:qr, o + 8:o + 16]
                for h in range(8):
                    q, k = qk(h)
                    u = dict(qr=qr, ext=ext, tok=a, mask=mk, scale=scale, qk=[(q[:, a:a + qr], k[:, k0:k0 + ext])],
                             chunks=[(o, r, vof(v, h)[0:r]) for o, r, v in chunks], dv=64, o=64 * h,
                             sums=[sums[:, h:h + 1]], all=sums, alle=e1, init=big[0:qr], ready=[ready, headed.get(h)], vready=vready)
                    if sinks is not None:
                        u["init"], u["after"] = negs[0:qr, h:h + 1], negd
                        u["sink"] = (sm[0:qr, sinks + h:sinks + h + 1], e1[:, h:h + 1])
                    if h == 7:
                        u["end"] = True
                    us.append(u)
            return us

        cum, w1, w2 = (m["Z"][0:8, T * i:T * i + T] for i in range(3))
        before = [*all_of()]

        def fgate(ps, a, b, t):
            f = DV.op(lambda e: e.tensor_tensor(cum[:, a:b], ps[0:8], rs[0:8, a:b], ALU.mult), t, before)
            DV.chain(lambda e: e.tensor_scalar(cum[:, a:b], cum[:, a:b], sm[0:8, B_F + l:B_F + l + 1], None, ALU.add))
            return f

        def qk(dst, c0, c, rng):
            return win(cols(c0 + 128 * c, 128), rng, two_heads(dst, 2 * c, rs, before))
        gates = win([*cols(1536, 8)] * 16, TOKR, fgate)
        lead(N, rs, gates, qk(Q, 0, 0, QR), 2, len(QR))
        gated = PE.last()
        AC.op(lambda e: e.activation(w1, cum, ACT.Abs), DV.last())
        AC.chain(lambda e: e.activation(w1, w1, ACT.Exp, scale=-1.0))
        AC.chain(lambda e: e.activation(w1, w1, ACT.Ln, bias=k1[0:8, 1:2], scale=1.0))
        DV.chain(lambda e: e.scalar_tensor_tensor(out=w2, in0=cum, scalar=0.0, in1=w1, op0=ALU.min, op1=ALU.subtract), AC.last())
        DV.chain(lambda e: e.memset(w1, 1.0))
        DV.chain(lambda e: e.tensor_tensor_scan(cum, w1, w2, 0.0, ALU.mult, ALU.add))
        DV.chain(lambda e: e.tensor_scalar(w1, cum, 8.0, None, ALU.mult))
        f = DV.op(lambda e: e.tensor_scalar(w2, cum, -8.0, None, ALU.mult))
        GP.chain(lambda e: e.memset(Q[64:66, :, :], 1.0), before)
        r = GP.chain(lambda e: e.memset(K[64:66, :, :], 1.0), before, gated)
        for c in range(1, 4):
            run(qk(Q, 0, c, QR))
        for c in range(4):
            run(qk(K, 512, c, TOKR))
        for h in range(8):
            SP.dma(lambda e, h=h: e.dma_start(Q[64:65, h, :], w1[h:h + 1, :]), sems[f"aug{2 * l}"], f, r)
            SP.dma(lambda e, h=h: e.dma_start(K[65:66, h, :], w2[h:h + 1, :]), sems[f"aug{2 * l + 1}"])

        def vcopy(scale):
            def evac(ps, n, a, b, t):
                return AC.op(lambda e: e.activation(V[0:b - a, n, :], ps, ACT.Copy, scale=scale[0:b - a, n:n + 1] if scale is not None else 1.0), t, before)
            return evac
        headed = {}
        qk_ready = all_of()
        gemm_tok("w_in", l, 8, cols(1024, 512), Hx, TILES, hr, vcopy(col))
        v_ready = AC.last()
        for q in (AC, DV, PE):
            q.wait((sems[f"aug{2 * l}"], 8 * 16), (sems[f"aug{2 * l + 1}"], 8 * 16))
        for c in range(4):
            zgate(1544, c)

        B0 = 2056
        cq, ckv = ([M[:, c, :] for c in cs] for cs in (range(3), range(3, 5)))
        kr = M[64:96, 5, :]
        before = all_of()

        def latent():
            for c in range(5):
                yield from win(cols(B0 + 128 * c, 128), TOKR, lambda ps, a, b, t, c=c: scaled(M[:, c, a:b], ps, rs[:, a:b], t, before))
            c0 = B0 + 640
            yield from win([*cols(c0, 32), *swapped(c0)] * 2, TOKR, lambda ps, a, b, t: rope32(ps, 64, kr[:, a:b], a, b, t, rs, before))
        attend(units_of(lambda h: (Q[0:66, h, :], K[0:66, h, :]), lambda v, h: V[:, v, 64 * h:64 * h + 64], 0.125, qk_ready, v_ready), finish_to(0), latent(), 96)
        y0 = DV.last()

        before = all_of()
        half = Yx[1]
        cqx, ckx = [half[2], half[3], half[0]], half[:2]
        Nk = norm_begin(TILES, "Q")
        for c in range(2):
            norm_chunk(Nk, ckv[c], before)
        Nq = norm_begin(TILES, "Q", 2, 8)
        for c in range(3):
            norm_chunk(Nq, cq[c], before)
        for h in range(8):
            GP.chain(lambda e, h=h: e.tensor_copy(K[64:96, h, :], kr), before)
        zgate(B0 + 672, 0)
        norm_sum(Nk)
        norm_sum(Nq)
        Nk["sum"] = Nq["sum"]
        norm_col(Nk, 256, col2)
        norm_col(Nq, 384, col3)
        zgate(B0 + 672, 1)
        e = norm_rows(Nk, rs2)
        kvr = normed_parts(ckv, G_CKV + 2 * l, rs2, ckx, e, before)
        e = norm_rows(Nq, rs3)
        qr_ = normed_parts(cq[:2], G_CQ + 3 * l, rs3, cqx[:2], e)
        zgate(B0 + 672, 2)
        for c in range(4):
            run(gemm_steps(panel("w_ukv", l, K2, [128 * h + d for h in range(2 * c, 2 * c + 2) for d in range(64)]),
                           0, 128, ckx, 2, TOKR, kvr, two_heads(K, 2 * c, None, before)))
        gemm_tok("w_ukv", l, 2, [128 * h + 64 + d for h in range(8) for d in range(64)], ckx, TILES, kvr, vcopy(None))
        qr_[2] = normed_parts(cq[2:], G_CQ + 3 * l + 2, rs3, cqx[2:], e, PE.last())[0]
        qk_ready, v_ready = all_of(), AC.last()
        run(mla_q("w_uq", l, range(8), cqx, QR, qr_, Q, before, headed=headed))
        zgate(B0 + 672, 3)
        attend(units_of(lambda h: (Q[0:96, h, :], K[0:96, h, :]), lambda v, h: V[:, v, 64 * h:64 * h + 64], 96 ** -0.5, qk_ready, v_ready),
               finish_to(1), merge(0, y0, [tmp[:, 1, :]]), 192 if l == 0 else 96)
        y1 = DV.last()

        C0 = 3240
        before = all_of()
        for c in range(4):
            run(win([*cols(C0 + 64 * c, 64), *cols(C0 + 64 * (c + 4), 64)], QR,
                    lambda ps, a, b, t, c=c: rope64(ps, Q[:, c, a:b], a, b, t, before)))
        run(win(cols(C0 + 512, 128), TOKR, lambda ps, a, b, t: rope64(ps, K[:, 0, a:b], a, b, t, before)))
        headed.clear()
        qk_ready = all_of()
        vt = m["P"][:, 0:T]
        run(win(cols(C0 + 640, 128), TOKR, lambda ps, a, b, t: scaled(vt[:, a:b], ps, rs[:, a:b], t, before)))
        v_ready = DV.last()
        zgate(C0 + 768, 0)
        bks = [next_bank() for _ in range(2)]
        for n, (a, b) in enumerate(TILES):
            bk, at = bks[min(n, 1)], 128 * max(0, n - 1)
            t = PE.op(lambda e, a=a, bk=bk, at=at: e.transpose(bank(bk)[:, at:at + 128], vt[:, a:a + 128], ident), v_ready, free[bk] if n < 2 else None)
        free[bks[0]] = AC.op(lambda e: e.activation(V[0:NM, 0, 0:128], bank(bks[0])[0:NM, 0:128], ACT.Copy), t, before)
        free[bks[1]] = v_ready = AC.op(lambda e: e.activation(
            V[:, 1:5, 0:128], bank(bks[1]).rearrange("p (i d) -> p i d", i=4), ACT.Copy), t)
        for c in range(1, 4):
            zgate(C0 + 768, c)
        negs = st[:, 100:108]
        negd = DV.op(lambda e: e.tensor_scalar(negs, sm[:, SINKS + 8 * l:SINKS + 8 * l + 8], -1.0, None, ALU.mult))
        attend(units_of(lambda h: (Q[64 * (h // 4):64 * (h // 4) + 64, h % 4, :], K[64 * (h // 4):64 * (h // 4) + 64, 0, :]),
                        lambda v, h: V[:, v, 64 * (h // 4):64 * (h // 4) + 64], 0.125, qk_ready, v_ready, SINKS + 8 * l, True),
               finish_to(2), merge(1, y1, [tmp[:, 1, :]]), 192 if l == 0 else 96)
        before = all_of()
        a0 = QR[0][0]
        mr = {}
        Mx = Yx[1] + Yx[0]

        def part(c):
            mr[c] = parts(M[:, c, a0:T], *(x[:, a0:T] for x in Mx[c]), DV.last(), PE.last() if c >= 4 else before)
        run(merge(2, DV.last(), [m["P"][:, 0:T], m["P"][:, T:2 * T]], lambda c: part(c) if c < 4 else None))
        for c in range(4, 8):
            part(c)

        N = norm_begin(TILES if l == 0 else TILES[1:])
        before = PE.last()
        nr = {}
        for c in range(8):
            def evac(ps, a, b, t, c=c):
                f = DV.op(lambda e: e.scalar_tensor_tensor(
                    out=X[:, c, a:b], in0=ps, scalar=0.25, in1=X[:, c, a:b], op0=ALU.mult, op1=ALU.add), t)
                if b == T:
                    norm_chunk(N, X[:, c, a0:T], f)
                    if l == 0:
                        g = NORM_G + 8 + c
                        nr[c] = scaled_parts(X[:, c, :], sm[:, g:g + 1], *Hx[c], f, before)
                return f
            run(gemm_steps(panel("w_out", l, K8, cols(128 * c, 128)), 0, 128, Mx, 8, QR, mr, evac))
        return nr, N

    N = norm_begin(TILES)
    hr = {}
    for c in range(8):
        norm_chunk(N, X[:, c, :], x_at(c))
        hr[c] = scaled_parts(X[:, c, :], sm[:, NORM_G + c:NORM_G + c + 1], *Hx[c], x_at(c))
    for l in range(2):
        hr, N = first_layer(l, hr, N)

    X2 = X[:, :, NM:T]
    ALLR = [(0, S)]
    ST = [(128 * i, 128 * i + 128) for i in range(4)]
    Hx, Yx = both("Hh", "Hl", S, 8), both("Yh", "Yl", S, 8)
    Yh, Yl = v3("Yh", S, 8), v3("Yl", S, 8)
    Q, K, M = v3("Q", S, 8), v3("K", S, 8), v3("M", S, 8)
    V = v3("V", 512, 4)
    spare = m["V"][:, 4 * 512:5 * 512]
    rsS, rs2S, rs3S = rs[:, 0:S], rs2[:, 0:S], rs3[:, 0:S]

    def mult_parts(N, x, g, out, *after):
        t = scaled_parts(x, sm[:, g:g + 1], *out, *after, lagging=True)
        norm_chunk(N, x, *after)
        return t

    def first_half(name, n, dst, before, ready):
        for c in range(8):
            yield from gemm_steps(panel(name, 0, K4, cols(128 * c, 128)), 0, 128, Yx, 4, ALLR, ready,
                                  lambda ps, a, b, t, c=c: AC.op(lambda e: e.activation(dst[:, c, :], ps, ACT.Copy), t, before))

    def second_half(name, dst, ready):
        N = norm_begin(ST)
        for c in range(8):
            def evac(ps, a, b, t, c=c):
                f = DV.op(lambda e: e.tensor_tensor(dst[:, c, :], ps, dst[:, c, :], ALU.add), t, AC.last() if c == 0 else None)
                norm_chunk(N, dst[:, c, :], f)
                return f
            run(gemm_steps(panel(name, 0, range(4, 8), cols(128 * c, 128)), 0, 128, Yx[4:], 4, ALLR, ready, evac))
        return N

    def add_normed(y, g, then):
        for c in range(8):
            DV.op(lambda e, c=c: e.scalar_tensor_tensor(
                out=y[:, c, :], in0=y[:, c, :], scalar=sm[:, g + c:g + c + 1], in1=rsS, op0=ALU.mult, op1=ALU.mult), AC.last() if c == 0 else None)
            q = GP if c % 2 else DV
            f = q.op(lambda e, c=c: e.tensor_tensor(X2[:, c, :], X2[:, c, :], y[:, c, :], ALU.add), q.last(), DV.last())
            then(c, f)
        caught_up()

    def mix_end(y, i, N):
        norm_col(N, D, col)
        norm_rows(N, rsS)
        N = norm_begin(ST)
        before = PE.last()
        ready = {}

        def then(c, f):
            ready[c] = mult_parts(N, X2[:, c, :], MLP_PRE + 8 * i + c, Hx[c], f, before)
        add_normed(y, MIX_POST + 8 * i, then)
        return ready, N

    def mlp(i, hr, N):
        pz = v3("Z", S, 2)
        AC.dma(lambda e: e.dma_start(m["Z"][:, 0:2 * S], A["p"][i]), sems[f"pin{i}"], all_of())
        start = all_of()
        for f in range(4):
            before = PE.last()
            ready = {}

            def up(c):
                def evac(ps, a, b, t):
                    q = tmp[:, c % 2, 0:S]
                    x = DV.op(lambda e: e.scalar_tensor_tensor(out=q, in0=ps, scalar=0.0, in1=rsS, op0=ALU.max, op1=ALU.mult), t, start, tu)
                    AC.op(lambda e: e.activation(Yx[c][0], q, ACT.Square), x, before)
                    a = AC.op(lambda e: e.activation(q, q, ACT.Square))
                    ready[c] = DV.op(lambda e: e.tensor_tensor(Yx[c][1], q, Yx[c][0].bitcast(F), ALU.subtract), a)
                    return x
                return gemm_steps(panel("w_mlp_in_2", i, K8, cols(1024 * f + 128 * c, 128)), 0, 128, Hx, 8, ALLR, hr, evac)
            if f == 0:
                lead(N, rsS, up(0), up(1))
            for c in range(0 if f else 2, 8):
                run(up(c))
            if f == 3:
                N = norm_begin(ST)
                px = Hx[6:]
                pr = {c: parts(pz[:, c, :], *px[c], (sems[f"pin{i}"], 16), PE.last()) for c in range(2)}
            for c in range(8):
                def add(ps, a, b, t, c=c):
                    if f == 0:
                        return AC.op(lambda e: e.activation(M[:, c, :], ps, ACT.Copy), t, start)
                    x = DV.op(lambda e: e.tensor_tensor(M[:, c, :], ps, M[:, c, :], ALU.add), t, DV.last(), AC.last() if f == 1 and c == 0 else None)
                    if f == 3:
                        norm_chunk(N, M[:, c, :], x)
                    return x
                run(gemm_steps(panel("w_mlp_out_2", i, range(8 * f, 8 * f + 8), cols(128 * c, 128)), 0, 128, Yx, 8, ALLR, ready, add))

        def project(c):
            run(gemm_steps(panel("w_ple_proj_2", i, K2, cols(128 * c, 128)), 0, 128, px, 2, ALLR, pr,
                           lambda ps, a, b, t: AC.op(lambda e: e.activation(Q[:, c, :], ps, ACT.Copy), t, start)))
        project(0)
        norm_col(N, D, col)
        project(1)
        norm_rows(N, rsS)
        before = PE.last()
        ready = {}

        def then(c, f):
            if c < 6:
                project(c + 2)
            ready[c] = parts(X2[:, c, :], *Hx[c], f, PE.last() if c >= 6 else before, lagging=True)
        add_normed(M, MLP_POST + 8 * i, then)
        return ready

    def ple(i, hr):
        N = norm_begin(ST)
        before = all_of()
        ready = {}
        for c in range(8):
            tg = tmp[:, c % 2, 0:S]

            def evac(ps, a, b, t, c=c, tg=tg):
                x = AC.op(lambda e: e.activation(tg, ps, ACT.Tanh, scale=0.5), t, DV.last() if c > 1 else before)
                DV.op(lambda e: e.scalar_tensor_tensor(out=tg, in0=tg, scalar=1.0, in1=Q[:, c, :], op0=ALU.add, op1=ALU.mult), x)
                f = DV.chain(lambda e: e.scalar_tensor_tensor(
                    out=X2[:, c, :], in0=tg, scalar=0.5, in1=X2[:, c, :], op0=ALU.mult, op1=ALU.add))
                if i == 0:
                    ready[c] = mult_parts(N, X2[:, c, :], MIX_PRE + 8 + c, Yx[c], f, before)
                    caught_up()
                else:
                    SP.dma(lambda e: e.dma_start(out[:, c, :], X2[:, c, :]), sems["out"], f)
                return x
            run(gemm_steps(panel("w_ple_gate_2", i, K8, cols(128 * c, 128)), 0, 128, Hx, 8, ALLR, hr, evac))
        return ready, N

    def finish2(y0):
        def finish(u, t):
            a = u["tok"]
            r = divided(u, t, u["all"])
            yield
            x = turn_out(128, r)
            src = bank(5)[:, :].rearrange("p (c n) -> p c n", c=4)
            free[5] = parts(src, Yh[:, y0:y0 + 4, a:a + 128], Yl[:, y0:y0 + 4, a:a + 128], x)
        return finish

    def plain_units(qk, vof, scale, mask, after={}):
        us = []
        ready = all_of()
        for i in range(4):
            ext = 128 * i + 128
            sums = st[:, 32 + 16 * (i % 2):32 + 16 * (i % 2) + 8]
            for h in range(8):
                q, k = qk(h)
                u = dict(qr=128, ext=ext, tok=128 * i, mask=mask(i, ext), scale=scale, qk=[(q[:, 128 * i:ext], k[:, 0:ext])],
                         chunks=[(128 * v, 128, vof(v, h)) for v in range(i + 1)], dv=64, o=64 * h,
                         sums=[sums[:, h:h + 1]], all=sums, init=big, ready=ready, vready=ready, after=after.get(i))
                if h == 7:
                    u["end"] = True
                us.append(u)
        return us

    def vcopy2(scale, *after):
        def evac(ps, n, a, b, t):
            return AC.op(lambda e: e.activation(V[:, n, :], ps, ACT.Copy, scale=scale[:, n:n + 1] if scale is not None else 1.0), t, *after)
        return evac

    def mixer_ab(hr, N):
        before = all_of()
        lam = m["Z"][:, 2 * T:2 * T + 256]
        AC.dma(lambda e: e.dma_start(lam, A["lam"]), sems["lam"], before)
        AC.dma(lambda e: e.dma_start(spare, A["maskd"]), sems["md"])

        def rotary(dst, o, c, c0, later=None):
            def evac(ps, a, b, t):
                return rope64(ps, dst[:, o + c, :], a, b, t, before, later=later)
            yield from gemm_steps(panel("w_in_ab_2", 0, K8, cols(c0 + 128 * c, 128)), 0, 128, Hx, 8, ALLR, hr, evac)

        lead(N, rsS, rotary(Q, 0, 0, 0), rotary(Q, 0, 1, 0))
        for dst, c0, c in ((Q, 0, 2), (Q, 0, 3), (K, 512, 0), (K, 512, 1), (K, 512, 2), (K, 512, 3)):
            run(rotary(dst, 0, c, c0))
        ready = all_of()
        gemm_tok("w_in_ab_2", 0, 8, cols(1024, 512), Hx, ST, hr, vcopy2(col, before))
        vready = AC.last()
        la = [lam[:, 64 * i:64 * i + 64] for i in range(4)]
        e2 = k1[:, 3:4]
        dots = st[:, 108:110]
        DV.wait((sems["lam"], 16))
        for x in range(2):
            DV.chain(lambda e, x=x: e.tensor_tensor_reduce(la[2 * x], la[2 * x], la[2 * x + 1], 1.0, 0.0, ALU.mult, ALU.add, dots[:, x:x + 1]))
        AC.op(lambda e: e.activation(dots, dots, ACT.Exp), DV.last())
        DV.op(lambda e: e.scalar_tensor_tensor(out=e2, in0=dots[:, 1:2], scalar=-LAM_INIT, in1=dots[:, 0:1], op0=ALU.add, op1=ALU.subtract), AC.last())

        def mix(u):
            s = u["pairsum"]
            p1, p2 = u["p"]
            DV.op(lambda e: e.reciprocal(s, s), u["exp"])
            DV.chain(lambda e: e.tensor_scalar(p2, p2, s[:, 1:2], e2, ALU.mult, ALU.mult))
            return DV.chain(lambda e: e.scalar_tensor_tensor(out=p1, in0=p1, scalar=s[:, 0:1], in1=p2, op0=ALU.mult, op1=ALU.add))

        def finish(u, t):
            a = u["tok"]
            o = m["O"][:, :]
            free[6] = f = AC.op(lambda e: e.activation(o, bank(6), ACT.Copy), t, turned["o"])
            sq = m["Z"][:, 0:512]
            ss = st[:, 96:100]
            DV.op(lambda e: e.tensor_tensor(sq, o, o, ALU.mult), f, start, DV.last())
            r = DV.chain(lambda e: e.tensor_reduce(ss, sq.rearrange("p (h d) -> p h d", h=4), AX.X, ALU.add))
            r = AC.op(lambda e: e.activation(ss, ss, ACT.Sqrt, bias=k1[:, 0:1], scale=1.0 / 128), r)
            yield
            DV.op(lambda e: e.reciprocal(ss, ss), r)
            o3 = o.rearrange("p (h d) -> p h d", h=4)
            r = DV.chain(lambda e: e.tensor_tensor(o3, o3, ss.unsqueeze(2).to_broadcast([128, 4, 128]), ALU.mult))
            yield
            x = turn_out(128, r)
            q = m["Z"][:, T:T + 512]
            free[5] = DV.chain(lambda e: e.tensor_scalar(q, bank(5), sm[:, DIFF_SUB:DIFF_SUB + 1], 1.0 - LAM_INIT, ALU.mult, ALU.mult), x, start)
            parts(q.rearrange("p (c n) -> p c n", c=4), Yh[:, 0:4, a:a + 128], Yl[:, 0:4, a:a + 128], free[5])
            start.append(AC.last())

        start = [all_of()]
        us = []
        for i in range(4):
            ext = 128 * i + 128
            for h in range(4):
                s = st[:, 80 + 2 * h:82 + 2 * h]
                u = dict(qr=128, ext=ext, tok=128 * i, mask=causal(ext), scale=0.125,
                         qk=[(Q[64 * x:64 * x + 64, h, 128 * i:ext], K[64 * x:64 * x + 64, h, 0:ext]) for x in range(2)],
                         chunks=[(128 * v, 128, V[:, v, 128 * h:128 * h + 128]) for v in range(i + 1)], dv=128, o=128 * h,
                         sums=[s[:, 0:1], s[:, 1:2]], pairsum=s, init=big, mix=mix, ready=ready, vready=vready)
                if h == 3:
                    u["end"] = True
                us.append(u)

        later = []

        def others():
            for dst, c0 in ((Q, 1536), (K, 2048)):
                for c in range(4):
                    for n, _ in enumerate(rotary(dst, 4, c, c0, later)):
                        if n == 3 and later:
                            later.pop()()
                        yield
            later.pop()()
        attend(us, finish, others(), 64)
        y0 = DV.last()
        gemm_tok("w_in_ab_2", 0, 8, cols(2560, 512), Hx, ST, hr, vcopy2(col, all_of()))
        DV.wait((sems["md"], 16))
        attend(plain_units(lambda h: (Q[64 * (h % 2):64 * (h % 2) + 64, 4 + h // 2, :], K[64 * (h % 2):64 * (h % 2) + 64, 4 + h // 2, :]),
                           lambda v, h: V[:, v, 64 * h:64 * h + 64], 0.125, lambda i, ext: spare[:, S - ext:S]), finish2(4),
               first_half("w_out_ab_2", 0, M, all_of(), y0), 32)
        return mix_end(M, 0, second_half("w_out_ab_2", M, DV.last()))

    def mixer_c(yr, N):
        before = all_of()
        cq, ckv = [Q[:, c, :] for c in range(3)], [Q[:, c, :] for c in range(3, 5)]
        cqx, ckx = Hx[:3], Hx[3:5]
        ki, kr = spare[0:64], spare[64:96]
        ready = {}

        def win(cs, evac):
            return gemm_steps(panel("w_in_c_2", 0, K8, cs), 0, 128, Yx, 8, ALLR, yr, evac)

        def low(c):
            def evac(ps, a, b, t):
                if c == 0:
                    norms["q"] = norm_begin(ST)
                if c == 3:
                    norms["k"] = norm_begin(ST, "K", 3, 8)
                N = norms["q" if c < 3 else "k"]
                f = DV.op(lambda e: e.tensor_tensor(Q[:, c, :], ps, rsS, ALU.mult), t, before)
                norm_chunk(N, Q[:, c, :], f)
                return f
            return win(cols(128 * c, 128), evac)
        norms = {}
        lead(N, rsS, low(0), low(1))
        run(low(2))
        norm_col(norms["q"], 384, col2)
        run(low(3))
        x = norm_rows(norms["q"], rs2S)
        ready["q"] = normed_parts(cq, G_CQ2, rs2S, cqx, x, before)
        run(low(4))
        norm_col(norms["k"], 256, col3)

        def krope(ps, a, b, t):
            return rope32(ps, 64, kr, a, b, t, rsS, before)
        run(win([*cols(640, 32), *swapped(640)] * 2, krope))
        x = norm_rows(norms["k"], rs3S)
        ready["k"] = normed_parts(ckv, G_CKV2, rs3S, ckx, x)

        def index_rope(dst, r):
            def evac(ps, a, b, t):
                x = scaled(dst[32:64], ps[32:64, :], r if r is None else r[32:64], t, before)
                return [x, rope32(ps, 0, dst[0:32], a, b, t, r, before)]
            return evac
        k2 = st[:, 112:144].rearrange("p (i h) -> p i h", i=4)
        wi = tmp[64:72, 0, 0:S]

        def index_key(ps, a, b, t):
            f = index_rope(ki, rsS)(ps, a, b, t)
            w = DV.chain(lambda e: e.tensor_tensor(wi, ps[64:72, :], rsS[64:72, :], ALU.mult), tu)
            return [f, w]
        run(win([*cols(672, 64), *(list(cols(736, 8)) * 4), *swapped(672)], index_key))
        bk = next_bank()
        w = DV.last()
        for i in range(4):
            t = PE.op(lambda e, i=i, bk=bk: e.matmul(bank(bk)[:, 8 * i:8 * i + 8], wi[:, 128 * i:128 * i + 128], ident[64:72, 64:72], start=True, stop=True), w, free[bk])
        free[bk] = DV.op(lambda e, bk=bk: e.tensor_scalar(st[:, 112:144], bank(bk)[:, 0:32], 8.0 ** -0.5 / 8.0, None, ALU.mult), t)
        for h in range(8):
            cs = [*cols(64 * h, 64), *cols(64 * h + 32, 32), *swapped(64 * h)]
            run(gemm_steps(panel("w_qi_2", 0, K3, cs), 0, 128, cqx, 3, ALLR, ready["q"], index_rope(M[0:64, h, :], None)))
        sel = v3("Z", S, 4)
        best = st[:, 144:152]
        indexed = all_of()

        def pick(i, score, *rls):
            ext = 128 * i + 128
            rel = [indexed if i == 1 else all_of()] * 2
            for h in range(8):
                bk = next_bank()
                ps = bank(bk)[:, 0:ext]
                t = PE.op(lambda e, ps=ps, h=h: e.matmul(ps, M[0:64, h, 128 * i:ext], ki[:, 0:ext], start=True, stop=True), free[bk], indexed)
                rl = rls[h % 2][:, 0:ext]
                free[bk] = x = AC.op(lambda e, ps=ps, rl=rl: e.activation(rl, ps, ACT.Relu), t, rel[h % 2])
                if h == 0:
                    r = DV.chain(lambda e, rl=rl: e.tensor_scalar(score[:, 0:ext], rl, k2[:, i, 0:1], 0.0, ALU.mult, ALU.add), x, rel[1])
                else:
                    r = DV.chain(lambda e, rl=rl, h=h: e.scalar_tensor_tensor(
                        out=score[:, 0:ext], in0=rl, scalar=k2[:, i, h:h + 1], in1=score[:, 0:ext], op0=ALU.mult, op1=ALU.add), x)
                rel[h % 2] = r
                yield
            DV.chain(lambda e: e.tensor_tensor(score[:, 0:ext], score[:, 0:ext], causal(ext), ALU.add))
            for n in range(16):
                DV.chain(lambda e: e.max(best, score[:, 0:ext]))
                DV.chain(lambda e: e.match_replace(score[:, 0:ext], best, score[:, 0:ext], TAKEN))
                if n % 2:
                    yield
            chosen[i].append(DV.chain(lambda e: e.tensor_scalar(sel[:, i, 0:ext], score[:, 0:ext], -2e38, NEG, ALU.is_gt, ALU.mult)))
        chosen = {i: [] for i in range(1, 4)}

        def latent(g, Qg, before):
            yield from mla_q("w_uq_2", 0, range(8 * g, 8 * g + 8), cqx, ALLR, ready["q"], Qg, before)

        def keys(g, before):
            for c in range(4):
                hs = range(8 * g + 2 * c, 8 * g + 2 * c + 2)
                yield from gemm_steps(panel("w_uk_2", 0, K2, [64 * h + d for h in hs for d in range(64)]), 0, 128, ckx, 2, ALLR,
                                      ready["k"], two_heads(K, 2 * c, None, before))
            gemm_tok("w_uv_2", 0, 2, [64 * h + d for h in range(8 * g, 8 * g + 8) for d in range(64)], ckx, ST, ready["k"], vcopy2(None, before))
        before0 = all_of()
        for h in range(8):
            GP.chain(lambda e, h=h: e.tensor_copy(K[64:96, h, :], kr), before0)
        picking = pick(1, *(m["P"][:, T * x:T * x + S] for x in range(3)))
        for steps in (latent(0, Q, before0), keys(0, before0)):
            for _ in steps:
                next(picking, None)
        run(picking)

        def beside():
            for i in (2, 3):
                yield from pick(i, tmp[:, 0, :], tmp[:, 1, :], m["rs"])
            yield from latent(1, M, all_of())
        Qs = [Q, M]
        for g in range(2):
            if g:
                run(keys(1, all_of()))
            us = plain_units(lambda h: (Qs[g][0:96, h, :], K[0:96, h, :]), lambda v, h: V[:, v, 64 * h:64 * h + 64], 96 ** -0.5,
                             lambda i, ext: causal(128) if i == 0 else sel[:, i, 0:ext], chosen)
            attend(us, finish2(4 * g), beside() if g == 0 else first_half("w_out_c_2", 0, Q, all_of(), DV.last()),
                   56 if g == 0 else 32)
        return mix_end(Q, 1, second_half("w_out_c_2", Q, DV.last()))

    def causal(ext):
        return con[:, MASKF + T - ext:MASKF + T]

    norm_col(N, D, col)
    x = norm_rows(N, rsS)
    N = norm_begin(ST)
    before = PE.last()
    hr = {}
    for c in range(8):
        f = DV.op(lambda e, c=c: e.scalar_tensor_tensor(
            out=X2[:, c, :], in0=X2[:, c, :], scalar=sm[:, FINAL_G + c:FINAL_G + c + 1], in1=rsS, op0=ALU.mult, op1=ALU.mult), x)
        hr[c] = mult_parts(N, X2[:, c, :], MIX_PRE + c, Hx[c], f, before)
    caught_up()
    hr, N = mixer_ab(hr, N)
    hr = mlp(0, hr, N)
    hr, N = ple(0, hr)
    hr, N = mixer_c(hr, N)
    hr = mlp(1, hr, N)
    ple(1, hr)
    SP.wait((sems["out"], 8 * 16))
    return dict(sp=SP, act=AC, dve=DV, pool=GP, pe=PE), panels


def tables():
    c = np.zeros((128, NCON), np.float32)
    c[:, IDENT:IDENT + 128] = np.eye(128)
    c[:, ONES:ONES + 128] = 1.0
    q, k = np.arange(128)[:, None], np.arange(128)[None, :]
    c[:, MASKF + 400:MASKF + 528] = np.where(k <= q, 0.0, NEG)
    c[:, MASKS:MASKS + 128] = np.where(k > q, 0.0, NEG)
    c[:, MASKS + 128:MASKS + 256] = np.where(k <= q, 0.0, NEG)
    pos = np.arange(T, dtype=np.float32)

    def angles(half):
        inv = (np.float32(10000.0) ** (-np.arange(half, dtype=np.float32) / np.float32(half))).astype(np.float32)
        return inv[:, None] * pos[None, :]
    a = angles(32)
    for h in range(0, 128, 64):
        c[h:h + 32, COS:COS + T] = c[h + 32:h + 64, COS:COS + T] = np.cos(a)
        c[h:h + 32, SIN:SIN + T] = -np.sin(a)
        c[h + 32:h + 64, SIN:SIN + T] = np.sin(a)
    a = angles(16)
    for h in (0, 64):
        c[h:h + 16, T2:T2 + T] = c[h + 16:h + 32, T2:T2 + T] = np.cos(a)
    c[96:112, T2:T2 + T] = -np.sin(a)
    c[112:128, T2:T2 + T] = np.sin(a)
    d = (np.arange(128)[:, None] + 384) - np.arange(512)[None, :]
    n = ((d >= 0) & (d <= 128)).astype(int) + ((d >= 0) & (d % 4 == 0)) + ((d >= 0) & (d % 16 == 0))
    maskd = np.where(n > 0, 8.0 * np.log(np.maximum(n, 1)), NEG).astype(np.float32)
    return c, maskd


_NAMES = ("w_in", "w_branch", "w_out", "w_uq", "w_ukv", "w_mlp_in_2", "w_mlp_out_2", "w_ple_proj_2", "w_ple_gate_2",
          "w_in_ab_2", "w_out_ab_2", "w_in_c_2", "w_uq_2", "w_qi_2", "w_uk_2", "w_uv_2", "w_out_c_2")


def kernel(**inputs):
    import concourse.bacc as _bacc
    from concourse.bass_utils import run_bass_kernel_spmd as _run

    a = {k: np.asarray(v) for k, v in inputs.items()}
    con, maskd = tables()
    x = np.concatenate([a["meta_tokens"], a["x"][0]], axis=0)
    xT = np.ascontiguousarray(x.reshape(T, 8, 128).transpose(2, 1, 0)).reshape(128, 8 * T)
    pT = np.ascontiguousarray(a["p_2"][:, 0].reshape(2, S, 2, 128).transpose(0, 3, 2, 1)).reshape(2, 128, 2 * S)
    sm = np.zeros((128, NSM), np.float32)

    def put(o, v):
        v = v.reshape(-1, 128).T
        sm[:, o:o + v.shape[1]] = v
    for o, n in ((NORM_G, "norm_g"), (G_CQ, "g_cq"), (G_CKV, "g_ckv"), (FINAL_G, "final_g"), (MIX_PRE, "g_mix_pre_2"),
                 (MIX_POST, "g_mix_post_2"), (MLP_PRE, "g_mlp_pre_2"), (MLP_POST, "g_mlp_post_2"),
                 (DIFF_SUB, "g_diff_sub_2"), (G_CQ2, "g_cq_2"), (G_CKV2, "g_ckv_2")):
        put(o, a[n])
    sm[0:8, B_F:B_F + 2] = a["b_f"].T
    sm[:, SINKS:SINKS + 16] = a["sinks"].reshape(1, 16)
    lam = np.concatenate([np.broadcast_to(a[n].reshape(1, 64), (128, 64)) for n in (
        "diff_lq1_2", "diff_lk1_2", "diff_lq2_2", "diff_lk2_2")], axis=1)

    nc = _bacc.Bacc("TRN2", target_bir_lowering=False, num_devices=1)
    A = {
        "x": nc.dram_tensor("in_x", (128, 8 * T), F, kind="ExternalInput").ap(),
        "con": nc.dram_tensor("in_con", (128, NCON), F, kind="ExternalInput").ap(),
        "sm": nc.dram_tensor("in_sm", (128, NSM), F, kind="ExternalInput").ap(),
        "p": nc.dram_tensor("in_p", (2, 128, 2 * S), F, kind="ExternalInput").ap(),
        "lam": nc.dram_tensor("in_lam", (128, 256), F, kind="ExternalInput").ap(),
        "maskd": nc.dram_tensor("in_maskd", (128, S), F, kind="ExternalInput").ap(),
        "w": nc.dram_tensor("in_w", (WTOTAL,), F, kind="ExternalInput").ap(),
    }
    out = nc.dram_tensor("out_0", (128, 8, S), F, kind="ExternalOutput").ap()
    spec = program(nc, A, out)

    w = np.empty(WTOTAL, np.float32)
    mats = {n: a[n] for n in _NAMES}
    for n in ("w_uk_2", "w_uv_2"):
        mats[n] = mats[n].reshape(1, 256, 1024)
    o = 0
    for name, idx, kcs, cols in spec:
        mat = mats[name][idx]
        cs = np.asarray(cols)
        rows = mat[128 * kcs[0]:128 * kcs[-1] + 128]
        part = rows[:, cs[0]:cs[0] + len(cs)] if np.all(np.diff(cs) == 1) else rows[:, cs]
        n = 128 * len(kcs) * len(cs)
        w[o:o + n].reshape(128, len(kcs), len(cs))[:] = part.reshape(len(kcs), 128, len(cs)).transpose(1, 0, 2)
        o += n
    r = _run(nc, [{"in_x": xT, "in_con": con, "in_sm": sm, "in_p": pT, "in_maskd": maskd, "in_lam": np.ascontiguousarray(lam), "in_w": w}], core_ids=[0])
    y = r.results[0]["out_0"]
    return np.ascontiguousarray(y.reshape(128, 8, S).transpose(2, 1, 0)).reshape(1, S, D)
```
